# Optimizing a Trainium2 kernel written in Bass

```python
import jax, jax.numpy as jnp
from jax import lax
import numpy as np

D_MODEL = 1024
BATCH = 1
SEQ = 1024
DEPTH = 1

N_HEADS = 8
HEAD_DIM = 64
ATTN_WIDTH = N_HEADS * HEAD_DIM
IDX_HEADS = 8
IDX_DIM = 64
IDX_SCALE = (IDX_HEADS ** -0.5) * (IDX_DIM ** -0.5)
TOPK_MAX = 256
Q_BLOCK = 128
POOL_WINDOWS = (2, 4, 8, 16)
POOL_GROUPS = len(POOL_WINDOWS)
POOL_WIDTH = 512
POOL_GROUP_WIDTH = POOL_WIDTH // POOL_GROUPS
N_BRANCHES = 2
D_FF = -(-8 * D_MODEL // (3 * 256)) * 256
RMS_EPS = 1e-6
NEG_BIG = -1e30

IN_COLS = (ATTN_WIDTH, HEAD_DIM, HEAD_DIM, IDX_HEADS * IDX_DIM, IDX_DIM, IDX_HEADS,
           POOL_WIDTH, N_BRANCHES * D_MODEL)
D_IN = int(sum(IN_COLS))
IN_SPLITS = [int(c) for c in np.cumsum(IN_COLS)[:-1]]

kernel_name = "hybrid_dsa_pool_gated_block"

def rms_norm(x, gain):
    xf = x.astype(jnp.float32)
    y = xf * lax.rsqrt(jnp.mean(xf * xf, axis=-1, keepdims=True) + RMS_EPS)
    return (y * gain.astype(jnp.float32)).astype(x.dtype)

def alibi_slopes(n_heads):
    return 2.0 ** (-8.0 * jnp.arange(1, n_heads + 1, dtype=jnp.float32) / n_heads)

def dsa_attention(q, k, v, q_idx, k_idx, w_idx):
    B, S = q.shape[0], q.shape[1]
    n_keep = min(TOPK_MAX, S // 4)
    nb = S // Q_BLOCK
    slopes = alibi_slopes(N_HEADS)
    key_pos = jnp.arange(S, dtype=jnp.int32)
    scale = HEAD_DIM ** -0.5

    def to_blocks(a):
        return a.reshape((B, nb, Q_BLOCK) + a.shape[2:]).swapaxes(0, 1)

    def one_block(args):
        qb, qib, wb, tb = args
        s = jnp.einsum('bqhd,bsd->bqhs', qib, k_idx)
        s = jnp.einsum('bqhs,bqh->bqs', jax.nn.relu(s), wb).astype(jnp.float32)
        causal = key_pos[None, :] <= tb[:, None]
        s = jnp.where(causal[None], s, -jnp.inf)
        _, idx = lax.top_k(s, n_keep)
        k_sel = jax.vmap(lambda kb, ib: kb[ib])(k, idx)
        v_sel = jax.vmap(lambda vb, ib: vb[ib])(v, idx)
        logits = jnp.einsum('bqhd,bqkd->bhqk', qb, k_sel).astype(jnp.float32) * scale
        dist = tb[None, :, None] - idx
        logits = logits - slopes[None, :, None, None] * dist[:, None].astype(jnp.float32)
        logits = jnp.where((dist >= 0)[:, None], logits, NEG_BIG)
        p = jax.nn.softmax(logits, axis=-1).astype(v.dtype)
        return jnp.einsum('bhqk,bqkd->bqhd', p, v_sel)

    tpos = jnp.arange(S, dtype=jnp.int32).reshape(nb, Q_BLOCK)
    out = lax.map(one_block, (to_blocks(q), to_blocks(q_idx), to_blocks(w_idx), tpos))
    return out.swapaxes(0, 1).reshape(B, S, ATTN_WIDTH)

def multiscale_pool(u, w_group, scale):
    B, S, P = u.shape
    uf = u.astype(jnp.float32)
    c0 = jnp.concatenate([jnp.zeros((B, 1, P), jnp.float32), jnp.cumsum(uf, axis=1)], axis=1)
    t = jnp.arange(S)
    outs = []
    for g, w in enumerate(POOL_WINDOWS):
        sl = slice(g * POOL_GROUP_WIDTH, (g + 1) * POOL_GROUP_WIDTH)
        cg = c0[..., sl]
        start = jnp.concatenate([jnp.zeros((B, w - 1, POOL_GROUP_WIDTH), jnp.float32),
                                 cg[:, :S - w + 1]], axis=1)
        count = jnp.minimum(t + 1, w).astype(jnp.float32)[None, :, None]
        mean = (cg[:, 1:] - start) / count
        outs.append((mean - uf[..., sl]).astype(u.dtype) @ w_group[g])
    return jnp.concatenate(outs, axis=-1) * scale

def setup_inputs(seed: int = 0) -> dict:
    key = jax.random.key(seed)
    ks = jax.random.split(key, 16)
    f32 = jnp.float32

    def w(k, shape, fan_in):
        return jax.random.normal(k, shape, f32) * (fan_in ** -0.5)

    def gain(k, shape):
        return 1.0 + 0.02 * jax.random.normal(k, shape, f32)

    L = DEPTH
    return {
        "x": jax.random.normal(ks[0], (BATCH, SEQ, D_MODEL), f32),
        "norm_mix": gain(ks[1], (L, D_MODEL)),
        "w_in": w(ks[2], (L, D_MODEL, D_IN), D_MODEL),
        "q_norm": gain(ks[3], (L, HEAD_DIM)),
        "k_norm": gain(ks[4], (L, HEAD_DIM)),
        "w_pool_group": w(ks[5], (L, POOL_GROUPS, POOL_GROUP_WIDTH, POOL_GROUP_WIDTH), POOL_GROUP_WIDTH),
        "pool_scale": gain(ks[6], (L, POOL_WIDTH)),
        "w_branch_attn": w(ks[7], (L, ATTN_WIDTH, D_MODEL), ATTN_WIDTH),
        "w_branch_pool": w(ks[8], (L, POOL_WIDTH, D_MODEL), POOL_WIDTH),
        "w_out": w(ks[9], (L, D_MODEL, D_MODEL), D_MODEL),
        "norm_ffn": gain(ks[10], (L, D_MODEL)),
        "w_ffn_gate": w(ks[11], (L, D_MODEL, D_FF), D_MODEL),
        "w_ffn_up": w(ks[12], (L, D_MODEL, D_FF), D_MODEL),
        "w_ffn_down": w(ks[13], (L, D_FF, D_MODEL), D_FF),
    }

def reference(x, norm_mix, w_in, q_norm, k_norm, w_pool_group, pool_scale, w_branch_attn,
              w_branch_pool, w_out, norm_ffn, w_ffn_gate, w_ffn_up, w_ffn_down):
    B, S = x.shape[0], x.shape[1]
    for l in range(DEPTH):
        h = rms_norm(x, norm_mix[l])
        proj = h @ w_in[l]
        q, k, v, qi, ki, wi, u, gates = jnp.split(proj, IN_SPLITS, axis=-1)
        q = rms_norm(q.reshape(B, S, N_HEADS, HEAD_DIM), q_norm[l])
        k = rms_norm(k, k_norm[l])
        qi = qi.reshape(B, S, IDX_HEADS, IDX_DIM)
        wi = wi * IDX_SCALE
        a = dsa_attention(q, k, v, qi, ki, wi)
        p = multiscale_pool(u, w_pool_group[l], pool_scale[l])
        g_attn, g_pool = jnp.split(jax.nn.sigmoid(gates), N_BRANCHES, axis=-1)
        merged = g_attn * (a @ w_branch_attn[l]) + g_pool * (p @ w_branch_pool[l])
        x = x + merged @ w_out[l]
        h2 = rms_norm(x, norm_ffn[l])
        x = x + (jax.nn.silu(h2 @ w_ffn_gate[l]) * (h2 @ w_ffn_up[l])) @ w_ffn_down[l]
    return x


_drawn_inputs = setup_inputs


def setup_inputs(seed=0):
    import zlib

    import numpy as np

    out = dict(_drawn_inputs(seed))
    spreads = {}
    factors = {'q_norm': 8.0, 'k_norm': 8.0, 'pool_scale': 5.833, 'norm_ffn': 4.348}
    for name, (base, spread) in spreads.items():
        noise = np.random.default_rng([zlib.crc32(name.encode()), seed]).standard_normal(out[name].shape)
        drawn = base * np.exp(spread * noise) if base else spread * noise
        out[name] = __import__('jax').numpy.asarray(drawn.astype(out[name].dtype))
    for name, factor in factors.items():
        out[name] = (out[name] * factor).astype(out[name].dtype)
    return out
```

```python
from contextlib import ExitStack

import concourse.bass as bass
from concourse import mybir

F32 = mybir.dt.float32
F32R = mybir.dt.float32r
ALU = mybir.AluOpType
ACT = mybir.ActivationFunctionType
AX = mybir.AxisListType

P = 128
HALF = 512
SLOT = 1024
RMS_EPS = 1e-6
TOPK_MAX = 256
POOL_WINDOWS = (2, 4, 8, 16)
PAD = max(POOL_WINDOWS)
MASKED = -3.0e38
TAKEN = -3.4e38
PENALTY = -1e30


class Block:

    def __init__(self, at, i=0, step=0):
        self.slot = at % 2
        self.n = at + step * i
        self.turn = at // 2 + (step // 2) * i
        self.early = at < 2 and step == 0


def hybrid_block(nc, x, norm_mix, w_in, q_norm, k_norm, w_pool_group, pool_scale, w_branch_attn,
                 w_branch_pool, w_out, norm_ffn, w_ffn_gate, w_ffn_up, w_ffn_down, out):
    _, S, D = x.shape
    HD = q_norm.shape[1]
    AW = w_branch_attn.shape[1]
    NH = AW // HD
    PW = w_branch_pool.shape[1]
    G = PW // P
    F = w_ffn_gate.shape[2]
    IH = (w_in.shape[2] - AW - 2 * HD - HD - PW - 2 * D) // (HD + 1)
    NT, KD, KA, KP, NF = S // P, D // P, AW // P, PW // P, F // P
    KEEP = min(TOPK_MAX, S // 4)
    T0 = KEEP // P
    ROUNDS = KEEP // 8
    IDX_SCALE = (IH ** -0.5) * (HD ** -0.5)
    SLOPES = [2.0 ** (-8.0 * (h + 1) / NH) for h in range(NH)]
    assert (S, D, HD, NH, IH, G) == (1024, 1024, 64, 8, 8, 4) and NF % 2 == 0

    C_Q, C_KV, C_QI = 0, AW, AW + 2 * HD
    C_KI = C_QI + IH * HD
    C_U = C_KI + HD + IH
    C_GA = C_U + PW
    C_GP = C_GA + D

    w_in0 = w_in[0].rearrange("(c p) n -> p c n", p=P)
    w_bp = w_branch_pool[0].rearrange("(c p) n -> p c n", p=P)
    w_ba = w_branch_attn[0].rearrange("(c p) n -> p c n", p=P)
    w_o = w_out[0].rearrange("(c p) n -> p c n", p=P)
    w_g = w_ffn_gate[0].rearrange("(c p) n -> p c n", p=P)
    w_u = w_ffn_up[0].rearrange("(c p) n -> p c n", p=P)
    w_d = w_ffn_down[0].rearrange("(c p) n -> p c n", p=P)

    plan = []
    for b in range(IH // 2):
        plan.append(("qi", b, w_in0[:, :, C_QI + b * P:C_QI + (b + 1) * P]))
    for g in range(G):
        plan.append(("u", g, w_in0[:, :, C_U + g * P:C_U + (g + 1) * P]))
    for jj in range(KD // 2):
        for j in (2 * jj, 2 * jj + 1):
            plan.append(("gp", j, w_in0[:, :, C_GP + j * P:C_GP + (j + 1) * P]))
        plan.append(("bp", jj, w_bp[:, :, jj * 2 * P:(jj + 1) * 2 * P]))
    for j in range(KD):
        plan.append(("ga", j, w_in0[:, :, C_GA + j * P:C_GA + (j + 1) * P]))
    for m in range(KD // 2):
        plan.append(("q", m, w_in0[:, 2 * m:2 * m + 2, C_Q:C_Q + AW]))
    plan.append(("kv", 0, w_in0[:, :, C_KV:C_KV + 2 * HD]))
    for jj in range(KD // 2):
        plan.append(("ba", jj, w_ba[:, :, jj * 2 * P:(jj + 1) * 2 * P]))
    for j in range(2):
        for m in range(KD // 2):
            plan.append(("wo", 4 * j + m, w_o[:, 2 * m:2 * m + 2, j * HALF:(j + 1) * HALF]))
    at = {(kind, k): n for n, (kind, k, _) in enumerate(plan)}
    N_UP = len(plan)
    N_DN = N_UP + 2 * NF
    DR = NF // 2
    N_ALL = N_DN + 2 * DR

    with ExitStack() as ctx:
        def sem(name):
            return ctx.enter_context(nc.semaphore(name))

        BASE = (nc.sbuf_base + 63) // 64 * 64
        KB = 1024
        A_CONST = BASE
        A_G = A_CONST + 512 + 4 * KB
        A_STAGE = A_G + 4 * KB
        A_R2 = A_STAGE + 24 * KB
        A_R1 = A_R2 + 64 * KB
        A_SC = A_R1 + 40 * KB
        SC_AT = [0] * NT
        n = 0
        for t in range(T0, NT):
            SC_AT[t] = n
            n += (t + 1) * P
        A_R3 = A_SC + 4 * n
        A_WORK = A_R3 + 32 * KB
        A_SMALL = A_WORK + 20 * KB
        small = [A_SMALL]

        def sb(name, shape, dt, offset):
            return nc.alloc_sbuf_tensor_at(name, shape, dt, offset=offset)

        def tiny(name, n, dt=F32):
            a = sb(name, [P, n], dt, small[0])
            small[0] += (4 * n + 31) // 32 * 32
            return a

        ident = sb("ident", [P, P], F32, A_CONST)
        key_minus_row = sb("key_minus_row", [P, S], F32, A_CONST + 512)
        gain = sb("gain", [P, D], F32, A_G)
        raw = sb("raw", [P, 2, SLOT], F32, A_STAGE)
        w_hi = sb("w_hi", [P, 2, SLOT], F32R, A_STAGE + 8 * KB)
        w_lo = sb("w_lo", [P, 2, SLOT], F32R, A_STAGE + 16 * KB)
        h_hi = sb("h_hi", [P, KD, S], F32R, A_R2)
        h_lo = sb("h_lo", [P, KD, S], F32R, A_R2 + 32 * KB)
        qi = sb("qi", [P, IH, S], F32R, A_R1)
        ki_hi = sb("ki_hi", [P, S], F32R, A_R1 + 32 * KB)
        ki_lo = sb("ki_lo", [P, S], F32R, A_R1 + 36 * KB)
        scores = sb("scores", [P, n], F32, A_SC)
        x_in = sb("x_in", [P, 2, D], F32, A_WORK)
        xn = sb("xn", [P, 2, D], F32, A_WORK + 8 * KB)
        kw_raw = sb("kw_raw", [P, KD, HD + IH], F32, A_R3)
        kw_hi = sb("kw_hi", [P, KD, P + IH], F32R, A_R3 + 3 * KB)
        kw_lo = sb("kw_lo", [P, KD, P + IH], F32R, A_R3 + 8 * KB)
        relu = sb("relu", [P, 3, S], F32, A_WORK)
        u_pad = sb("u_pad", [P, PAD + S], F32, A_R3 + 13 * KB)
        win = [sb(f"win{k}", [P, PAD + S], F32, A_R3 + (17 + 4 * k) * KB + 64 * (k + 1)) for k in range(2)]
        pl_f = sb("pl_f", [P, S], F32, A_R3 + 26 * KB)
        pt_f = sb("pt_f", [P, S], F32, A_R1 + 32 * KB)
        pl_hi = sb("pl_hi", [P, S], F32R, A_R3)
        pl_lo = sb("pl_lo", [P, S], F32R, A_R3 + 4 * KB)
        pw_raw = sb("pw_raw", [P, G, P], F32, A_WORK + 16 * KB)
        pw_hi = sb("pw_hi", [P, G, P], F32R, A_WORK + 18 * KB)
        pw_lo = sb("pw_lo", [P, G, P], F32R, A_R3 + 30 * KB)
        pt_hi = sb("pt_hi", [P, KP, S], F32R, A_R1)
        pt_lo = sb("pt_lo", [P, KP, S], F32R, A_R1 + 16 * KB)
        gate = sb("gate", [P, 2, S], F32, A_WORK)
        bp = sb("bp", [P, 2, S], F32, A_WORK + 8 * KB)
        q_nat = sb("q_nat", [P, NT, AW], F32, A_R3)
        kv_nat = sb("kv_nat", [P, NT, 2 * HD], F32, A_R3 + 16 * KB)
        q_st = sb("q_st", [P, 2, NH, P], F32R, A_R3 + 20 * KB)
        bias = sb("bias", [P, S], F32, A_R3 + 28 * KB)
        k_sq = sb("k_sq", [P, NT, HD], F32, A_R3 + 28 * KB)
        probs = sb("probs", [P, 2, S], F32, A_WORK)
        kn = sb("kn", [P, NT, 2, HD], F32, A_WORK)
        probs_t = sb("probs_t", [P, 2, S], F32, A_WORK + 8 * KB)
        dist = sb("dist", [P, S], F32, A_WORK + 16 * KB)
        q_sq = sb("q_sq", [P, AW], F32, A_G)
        a_nat = sb("a_nat", [P, AW], F32, A_G)
        q_s = sb("q_s", [P, AW], F32, A_G + 2 * KB)
        a_hi = sb("a_hi", [P, KA, S], F32R, A_R1)
        a_lo = sb("a_lo", [P, KA, S], F32R, A_R1 + 16 * KB)
        k_hi = sb("k_hi", [P, S], F32R, A_R1 + 32 * KB)
        k_lo = sb("k_lo", [P, S], F32R, A_R1 + 36 * KB)
        g_attn = sb("g_attn", [P, KD, S], F32, A_R2)
        m_pool = sb("m_pool", [P, KD, S], F32, A_R2 + 32 * KB)
        m_f = sb("m_f", [P, 2, S], F32, A_R1 + 32 * KB)
        m_hi = sb("m_hi", [P, KD, S], F32R, A_SC)
        m_lo = sb("m_lo", [P, KD, S], F32R, A_SC + 32 * KB)
        x2 = sb("x2", [P, NT, D], F32, A_R2)
        xn2 = sb("xn2", [P, 2, D], F32, A_R1)
        h2_hi = sb("h2_hi", [P, KD, S], F32R, A_SC)
        h2_lo = sb("h2_lo", [P, KD, S], F32R, A_SC + 32 * KB)
        act_t = sb("act_t", [P, NF, S], F32, A_R2)
        silu = sb("silu", [P, 2, S], F32, A_R2 + 88 * KB)
        x2b = sb("x2b", [P, NT, D], F32, A_SC)
        ac_hi = sb("ac_hi", [P, 2, S], F32R, A_SC + 32 * KB)
        ac_lo = sb("ac_lo", [P, 2, S], F32R, A_SC + 40 * KB)
        y = sb("y", [P, NT, HALF], F32, A_SC + 48 * KB)

        ssq = tiny("ssq", NT)
        ms = tiny("ms", NT)
        rs = tiny("rs", NT)
        minus_half = tiny("minus_half", NT)
        w_idx = tiny("w_idx", NT * IH)
        edge = tiny("edge", G * PAD)
        top8 = tiny("top8", 8)
        kss = tiny("kss", NT)
        krs = tiny("krs", NT)
        qss = tiny("qss", NH)
        qrs = tiny("qrs", NH)
        row_max = tiny("row_max", 2)
        neg_max = tiny("neg_max", 2)
        row_sum = tiny("row_sum", NH)
        row_inv = tiny("row_inv", NH)
        gq = tiny("gq", 1)
        gk = tiny("gk", 1)
        psc = tiny("psc", G)
        assert small[0] <= nc.sbuf_usable_end, (small[0], nc.sbuf_usable_end)

        ps = ctx.enter_context(nc.psum_tensor("ps", [P, 8, HALF], F32))
        ga_dram = nc.dram_tensor("ga_scratch", [P, KD, S], F32, kind="Internal").ap()
        mp_dram = nc.dram_tensor("mp_scratch", [P, KD, S], F32, kind="Internal").ap()
        x2_dram = nc.dram_tensor("x2_scratch", [P, NT, D], F32, kind="Internal").ap()

        def pair(b):
            return ps[:, b:b + 2, :].rearrange("p b n -> p (b n)")

        raw_landed = [sem("raw_landed0"), sem("raw_landed1")]
        hi_done, lo_done, used = sem("hi_done"), sem("lo_done"), sem("used")
        consts_in, kw_in, pw_in = sem("consts_in"), sem("kw_in"), sem("pw_in")
        cst = sem("cst")
        ident_ready, edge_ready, gq_ready = sem("ident_ready"), sem("edge_ready"), sem("gq_ready")
        x_landed = [sem("x_landed0"), sem("x_landed1")]
        sq_done, ms_done, rs_done = sem("sq_done"), sem("ms_done"), sem("rs_done")
        xn_done, tr_done, xh_done, xl_done = sem("xn_done"), sem("tr_done"), sem("xh_done"), sem("xl_done")
        kwh_done, kwl_done = sem("kwh_done"), sem("kwl_done")
        ki_done, wi_done, kih_done, kil_done, widx_done = (sem("ki_done"), sem("wi_done"), sem("kih_done"),
                                                           sem("kil_done"), sem("widx_done"))
        qi_done, qih_done, qil_done = sem("qi_done"), sem("qih_done"), sem("qil_done")
        is_done, relu_done, acc_done, masked = sem("is_done"), sem("relu_done"), sem("acc_done"), sem("masked")
        max_found, replaced = sem("max_found"), sem("replaced")
        pwh_done, pwl_done, pads = sem("pwh_done"), sem("pwl_done"), sem("pads")
        u_done, ue_done, win_done, plf_done, plh_done, pll_done = (sem("u_done"), sem("ue_done"), sem("win_done"),
                                                                   sem("plf_done"), sem("plh_done"), sem("pll_done"))
        pm_done, ptf_done, pth_done, ptl_done = sem("pm_done"), sem("ptf_done"), sem("pth_done"), sem("ptl_done")
        gp_done, gate_done, bp_done, bpe_done, mp_done = (sem("gp_done"), sem("gate_done"), sem("bp_done"),
                                                          sem("bpe_done"), sem("mp_done"))
        mp_stored = [sem("mp_stored0"), sem("mp_stored1")]
        ga_stored = [sem("ga_stored0"), sem("ga_stored1")]
        ga_done, gae_done = sem("ga_done"), sem("gae_done")
        qp_done, qn_done, kvp_done, kvn_done = sem("qp_done"), sem("qn_done"), sem("kvp_done"), sem("kvn_done")
        ksq_done, kss_done, kms_done, krs_done = sem("ksq_done"), sem("kss_done"), sem("kms_done"), sem("krs_done")
        kn_done, kt_done, kh_done, kl_done = sem("kn_done"), sem("kt_done"), sem("kh_done"), sem("kl_done")
        qsq_done, qss_done, qms_done, qrs_done = sem("qsq_done"), sem("qss_done"), sem("qms_done"), sem("qrs_done")
        qs_done, qt_done, qh_done, ql_done = sem("qs_done"), sem("qt_done"), sem("qh_done"), sem("ql_done")
        pen_done, dist_done, bias_done = sem("pen_done"), sem("dist_done"), sem("bias_done")
        qk_done, lg_done, nm_done, ex_done = sem("qk_done"), sem("lg_done"), sem("nm_done"), sem("ex_done")
        tp_done, pt_done, pv_done = sem("tp_done"), sem("pt_done"), sem("pv_done")
        ri_done, an_done, at_done, ah_done, al_done = (sem("ri_done"), sem("an_done"), sem("at_done"),
                                                       sem("ah_done"), sem("al_done"))
        ga_loaded, mp_loaded, x_loaded, gain2_in = sem("ga_loaded"), sem("mp_loaded"), sem("x_loaded"), sem("gain2_in")
        ba_done, mg_done, mf_done, mh_done, ml_done = (sem("ba_done"), sem("mg_done"), sem("mf_done"),
                                                       sem("mh_done"), sem("ml_done"))
        wo_done, x2_done, x2_stored, x2_loaded = sem("wo_done"), sem("x2_done"), sem("x2_stored"), sem("x2_loaded")
        sq2_done, ms2_done, rs2_done = sem("sq2_done"), sem("ms2_done"), sem("rs2_done")
        xn2_done, tr2_done, xh2_done, xl2_done = sem("xn2_done"), sem("tr2_done"), sem("xh2_done"), sem("xl2_done")
        gu_done, silu_done, act_done = sem("gu_done"), sem("silu_done"), sem("act_done")
        ach_done, acl_done, ac_used = sem("ach_done"), sem("acl_done"), sem("ac_used")
        y_done, y_stored = sem("y_done"), sem("y_stored")

        block = ctx.enter_context(nc.Block())
        QH = range(T0, NT)
        IDX = [(t, h) for t in QH for h in range(IH)]
        ATT = [(t, h) for t in range(NT) for h in range(NH)]
        LATE = NT - 1
        SPREAD = 8 * (NT - 2)

        def score_tile(t):
            return scores[:, SC_AT[t]:SC_AT[t] + (t + 1) * P]

        def load(sp, b, src):
            if not b.early:
                sp.wait_ge(hi_done, b.n - 1)
                sp.wait_ge(lo_done, b.n - 1)
            dst = raw[:, b.slot, :].rearrange("p (c n) -> p c n", c=src.shape[1])
            sp.dma_start(dst, src).then_inc(raw_landed[b.slot], 16)

        def load_gate_up(sp, i):
            for b in range(2):
                for k, w in enumerate((w_g, w_u)):
                    f = 2 * i + b
                    cols = slice(f * P, (f + 1) * P) if isinstance(f, int) else bass.ds(f * P, P)
                    load(sp, Block(N_UP + 2 * b + k, i, 4), w[:, :, cols])

        def pool_lo(pool, g):
            pool.wait_ge(plh_done, g + 1)
            if g:
                pool.wait_ge(pm_done, g)
            pool.tensor_tensor(pl_lo[:], pl_f[:], pl_hi[:].bitcast(F32), ALU.subtract).then_inc(pll_done, 1)

        def pt_split_lo(pool, g):
            pool.wait_ge(pth_done, g + 1)
            pool.wait_ge(ptf_done, g + 1)
            pool.tensor_tensor(pt_lo[:, g, :], pt_f[:], pt_hi[:, g, :].bitcast(F32),
                               ALU.subtract).then_inc(ptl_done, 1)

        def a_hi_out(act, t):
            act.wait_ge(at_done, t + 1)
            act.activation(a_hi[:, :, t * P:(t + 1) * P], ps[:, 7, :].rearrange("p (c n) -> p c n", c=KA),
                           ACT.Copy).then_inc(ah_done, 1)

        def multiplied(eng, kind, k):
            eng.wait_ge(used, at[kind, k] + 1)

        def slot_free(eng, m, s):
            if s == 0:
                eng.wait_ge(ac_used, m)
            else:
                eng.wait_ge(used, N_DN + m)

        @block.sync
        def _(sp):
            sp.dma_start(gain[:], norm_mix.broadcast_to([P, D])).then_inc(consts_in, 16)
            for t in range(NT):
                if t >= 2:
                    sp.wait_ge(xn_done, t - 1)
                    sp.wait_ge(sq_done, t - 1)
                sp.dma_start(x_in[:, t % 2, :], x[0, t * P:(t + 1) * P, :]).then_inc(x_landed[t % 2], 16)
                if t < 2:
                    load(sp, Block(t), plan[t][2])
            for n in range(2, N_UP):
                load(sp, Block(n), plan[n][2])
            load_gate_up(sp, 0)
            with sp.Fori(1, NF // 2) as i:
                load_gate_up(sp, i)
            for j in range(2):
                cols = slice(j * HALF, (j + 1) * HALF)
                load(sp, Block(N_DN + j * DR), w_d[:, 0:2, cols])
                with sp.Fori(0, (DR - 1) // 2) as i:
                    for b in range(2):
                        load(sp, Block(N_DN + j * DR + 1 + b, i, 2),
                             w_d[:, bass.ds(2 + 2 * b + 4 * i, 2), cols])
            for j in range(2):
                for t in range(NT):
                    sp.wait_ge(y_done, j * NT + t + 1)
                    sp.dma_start(out[0, t * P:(t + 1) * P, j * HALF:(j + 1) * HALF],
                                 y[:, t, :]).then_inc(y_stored, 16)
            sp.wait_ge(y_stored, 16 * 2 * NT)

        @block.gpsimd
        def _(pool):
            state = {"n": 0}

            def split_lo(b):
                pool.wait_ge(hi_done, b.n + 1)
                pool.wait_ge(raw_landed[b.slot], 16 * (b.turn + 1))
                if not b.early:
                    pool.wait_ge(used, b.n - 1)
                pool.tensor_tensor(w_lo[:, b.slot, :], raw[:, b.slot, :], w_hi[:, b.slot, :].bitcast(F32),
                                   ALU.subtract).then_inc(lo_done, 1)

            def lo_until(n):
                while state["n"] < n:
                    split_lo(Block(state["n"]))
                    state["n"] += 1

            pool.memset(minus_half[:], -0.5).then_inc(cst, 1)
            pool.memset(ident[:], 0.0).then_inc(cst, 1)
            pool.iota(key_minus_row[:], [[1, S]], base=0, channel_multiplier=-1,
                      allow_small_or_imprecise_dtypes=True).then_inc(cst, 1)
            pool.wait_ge(cst, 2)
            pool.affine_select(out=ident[:], in_=ident[:], compare_op=ALU.not_equal, fill=1.0, base=0,
                               pattern=[[-1, P]], channel_multiplier=1).then_inc(ident_ready, 1)

            def rstd(k, n, sums, means, out_, ready, m_done, r_done, count):
                pool.wait_ge(ready, k)
                pool.tensor_scalar(means, sums, 1.0 / count, RMS_EPS, ALU.mult, ALU.add).then_inc(m_done, 1)
                pool.wait_ge(m_done, k)
                pool.tensor_tensor(out_, means, minus_half[:, 0:n], ALU.pow).then_inc(r_done, 1)

            pool.wait_ge(cst, 3)
            for t in range(NT):
                rstd(t + 1, 1, ssq[:, t:t + 1], ms[:, t:t + 1], rs[:, t:t + 1], sq_done, ms_done, rs_done, D)
                if t == 1:
                    lo_until(1)
                if t == 3:
                    lo_until(2)
            pool.wait_ge(kil_done, 1)
            lo_until(at["u", 1] + 1)
            for k, t in enumerate(QH):
                pool.wait_ge(acc_done, IH * (k + 1))
                diag = score_tile(t)[:, t * P:(t + 1) * P]
                pool.affine_select(out=diag, in_=diag, compare_op=ALU.is_ge, fill=MASKED, base=0,
                                   pattern=[[-1, P]], channel_multiplier=1).then_inc(masked, 1)
            for k, buf in enumerate((u_pad, win[0], win[1])):
                pool.memset(buf[:, 0:PAD], 0.0).then_inc(pads, 1)
            pool.wait_ge(pads, 3)
            pool.wait_ge(edge_ready, G * PAD)
            sums = 0
            for g in range(G):
                w = POOL_WINDOWS[g]
                lo_until(at["u", g] + 3)
                if g:
                    pool_lo(pool, g - 1)
                pool.wait_ge(ue_done, g + 1)
                src, d, k = u_pad, 1, 0
                while d < w:
                    pool.tensor_tensor(win[k][:, PAD:], src[:, PAD:], src[:, PAD - d:PAD + S - d],
                                       ALU.add).then_inc(win_done, 1)
                    sums += 1
                    pool.wait_ge(win_done, sums)
                    src, d, k = win[k], 2 * d, 1 - k
                pool.tensor_tensor(src[:, PAD:2 * PAD], src[:, PAD:2 * PAD], edge[:, g * PAD:(g + 1) * PAD],
                                   ALU.mult).then_inc(win_done, 1)
                pool.wait_ge(win_done, sums + 1)
                pool.tensor_scalar(src[:, PAD:], src[:, PAD:], 1.0 / w, None, ALU.mult).then_inc(win_done, 1)
                pool.wait_ge(win_done, sums + 2)
                sums += 2
                if g:
                    pool.wait_ge(pll_done, g)
                    pool.wait_ge(plh_done, g)
                pool.tensor_tensor(pl_f[:], src[:, PAD:], u_pad[:, PAD:], ALU.subtract).then_inc(plf_done, 1)
                if g:
                    pt_split_lo(pool, g - 1)
            pool_lo(pool, G - 1)
            pt_split_lo(pool, G - 1)
            for j in range(KD):
                if j % 2 == 0:
                    lo_until(at["bp", j // 2] + 3)
                pool.wait_ge(bpe_done, j + 1)
                pool.wait_ge(gate_done, j + 1)
                pool.tensor_tensor(bp[:, j % 2, :], bp[:, j % 2, :], gate[:, j % 2, :], ALU.mult).then_inc(mp_done, 1)
            lo_until(at["kv", 0] + 3)
            rstd(1, NT, kss[:], kss[:], krs[:], kss_done, kms_done, krs_done, HD)
            for t in range(NT):
                rstd(t + 1, NH, qss[:], qss[:], qrs[:], qss_done, qms_done, qrs_done, HD)
                if t < T0:
                    pool.wait_ge(dist_done, t + 1)
                    diag = dist[:, t * P:(t + 1) * P]
                    pool.affine_select(out=diag, in_=diag, compare_op=ALU.is_ge, fill=PENALTY, base=0,
                                       pattern=[[-1, P]], channel_multiplier=1).then_inc(pen_done, 1)
            for j in range(KD):
                if j % 2:
                    lo_until(at["ba", j // 2] + 3)
                pool.wait_ge(mh_done, j + 1)
                pool.tensor_tensor(m_lo[:, j, :], m_f[:, j % 2, :], m_hi[:, j, :].bitcast(F32),
                                   ALU.subtract).then_inc(ml_done, 1)
            lo_until(N_UP)
            for t in range(NT):
                rstd(t + 1, 1, ssq[:, t:t + 1], ms[:, t:t + 1], rs[:, t:t + 1], sq2_done, ms2_done, rs2_done, D)
            split_lo(Block(N_UP))
            split_lo(Block(N_UP + 1))
            with pool.Fori(0, (N_ALL - N_UP - 2) // 2) as i:
                split_lo(Block(N_UP + 2, i, 2))
                split_lo(Block(N_UP + 3, i, 2))

        @block.scalar
        def _(act):
            state = {"n": 0}

            def split_hi(b):
                act.wait_ge(raw_landed[b.slot], 16 * (b.turn + 1))
                if not b.early:
                    act.wait_ge(used, b.n - 1)
                    act.wait_ge(lo_done, b.n - 1)
                act.activation(w_hi[:, b.slot, :], raw[:, b.slot, :], ACT.Copy).then_inc(hi_done, 1)

            def hi_until(n):
                while state["n"] < n:
                    split_hi(Block(state["n"]))
                    state["n"] += 1

            act.dma_start(kw_raw[:], w_in0[:, :, C_KI:C_KI + HD + IH]).then_inc(kw_in, 16)
            act.dma_start(pw_raw[:], w_pool_group[0].rearrange("g c n -> c g n")).then_inc(pw_in, 16)
            for k in range(2):
                act.dma_start(gq[k * HD:(k + 1) * HD, :], q_norm.rearrange("a d -> d a")).then_inc(consts_in, 16)
                act.dma_start(gk[k * HD:(k + 1) * HD, :], k_norm.rearrange("a d -> d a")).then_inc(consts_in, 16)
            act.dma_start(psc[:], pool_scale.rearrange("a (g p) -> p (a g)", p=P),
                          allow_slow_non_contiguous=True).then_inc(consts_in, 16)

            for t in range(NT + 1):
                if t < NT:
                    act.wait_ge(x_landed[t % 2], 16 * (t // 2 + 1))
                    if t >= 2:
                        act.wait_ge(tr_done, t - 1)
                    act.activation(xn[:, t % 2, :], x_in[:, t % 2, :], ACT.Square,
                                   accum_out=ssq[:, t:t + 1]).then_inc(sq_done, 1)
                if t == 0:
                    act.wait_ge(kw_in, 16)
                    act.activation(kw_hi[:, :, 0:HD], kw_raw[:, :, 0:HD], ACT.Copy).then_inc(kwh_done, 1)
                    act.activation(kw_hi[:, :, HD:P], kw_raw[:, :, 0:HD], ACT.Copy).then_inc(kwh_done, 1)
                    act.activation(kw_hi[:, :, P:], kw_raw[:, :, HD:], ACT.Copy).then_inc(kwh_done, 1)
                if t >= 1:
                    s = t - 1
                    act.wait_ge(tr_done, s + 1)
                    act.activation(h_hi[:, :, s * P:(s + 1) * P],
                                   pair(4 + 2 * (s % 2)).rearrange("p (c n) -> p c n", c=KD),
                                   ACT.Copy).then_inc(xh_done, 1)
                if t in (1, 3):
                    hi_until(state["n"] + 1)
            act.wait_ge(ki_done, 1)
            act.activation(ki_hi[:], pair(4), ACT.Copy).then_inc(kih_done, 1)
            for b in range(IH // 2):
                hi_until(at["qi", b] + 3)
                multiplied(act, "qi", b)
                src = pair(2 * (b % 2))
                act.activation(qi[0:HD, 2 * b, :], src[0:HD, :], ACT.Copy).then_inc(qih_done, 1)
                act.activation(qi[HD:P, 2 * b + 1, :], src[HD:P, :], ACT.Copy).then_inc(qih_done, 1)
            for i, (t, h) in enumerate(IDX):
                act.wait_ge(is_done, i + 1)
                if i >= 3:
                    act.wait_ge(acc_done, i - 2)
                W = (t + 1) * P
                act.activation(relu[:, i % 3, :W], pair(2 * (i % 4))[:, :W], ACT.Relu).then_inc(relu_done, 1)
            act.wait_ge(pw_in, 16)
            act.activation(pw_hi[:], pw_raw[:], ACT.Copy).then_inc(pwh_done, 1)

            def pooled_hi(g):
                act.wait_ge(plf_done, g + 1)
                if g:
                    act.wait_ge(pm_done, g)
                act.activation(pl_hi[:], pl_f[:], ACT.Copy).then_inc(plh_done, 1)

            def mixed_out(g):
                act.wait_ge(pm_done, g + 1)
                if g:
                    act.wait_ge(ptl_done, g)
                src = pair(4 + 2 * (g % 2))
                act.activation(pt_f[:], src, ACT.Copy, scale=psc[:, g:g + 1]).then_inc(ptf_done, 1)
                act.activation(pt_hi[:, g, :], src, ACT.Copy, scale=psc[:, g:g + 1]).then_inc(pth_done, 1)

            for g in range(G):
                hi_until(at["u", g] + 3)
                multiplied(act, "u", g)
                if g:
                    act.wait_ge(plf_done, g)
                act.activation(u_pad[:, PAD:], pair(2 * (g % 2)), ACT.Copy).then_inc(ue_done, 1)
                if g:
                    mixed_out(g - 1)
                pooled_hi(g)
            mixed_out(G - 1)
            for jj in range(KD // 2):
                for j in (2 * jj, 2 * jj + 1):
                    hi_until(at["gp", j] + 3)
                    multiplied(act, "gp", j)
                    if j >= 2:
                        act.wait_ge(mp_done, j - 1)
                    act.activation(gate[:, j % 2, :], pair(2 * (j % 2)), ACT.Sigmoid).then_inc(gate_done, 1)
                hi_until(at["bp", jj] + 3)
                for j in (2 * jj, 2 * jj + 1):
                    if j % 2:
                        multiplied(act, "bp", jj)
                    else:
                        act.wait_ge(bp_done, jj + 1)
                    if j >= 2:
                        act.wait_ge(mp_stored[j % 2], 16 * (j // 2))
                    act.activation(bp[:, j % 2, :], pair(4 + 2 * (j % 2)), ACT.Copy).then_inc(bpe_done, 1)
                for j in (2 * jj, 2 * jj + 1):
                    act.wait_ge(mp_done, j + 1)
                    act.dma_start(mp_dram[:, j, :], bp[:, j % 2, :]).then_inc(mp_stored[j % 2], 16)
            for j in range(KD):
                hi_until(at["ga", j] + 3)
                multiplied(act, "ga", j)
                if j >= 2:
                    act.wait_ge(ga_stored[j % 2], 16 * (j // 2))
                act.activation(gate[:, j % 2, :], pair(2 * (j % 2)), ACT.Sigmoid).then_inc(gae_done, 1)
                act.wait_ge(gae_done, j + 1)
                act.dma_start(ga_dram[:, j, :], gate[:, j % 2, :]).then_inc(ga_stored[j % 2], 16)
            hi_until(at["kv", 0] + 1)
            multiplied(act, "q", KD // 2 - 1)
            for t in range(NT):
                act.activation(q_nat[:, t, :], ps[:, t, :], ACT.Copy).then_inc(qn_done, 1)
            hi_until(at["kv", 0] + 3)
            multiplied(act, "kv", 0)
            act.activation(kv_nat[:], pair(0).rearrange("p (t n) -> p t n", t=NT), ACT.Copy).then_inc(kvn_done, 1)
            for q in range(2):
                act.wait_ge(mp_stored[q], 16 * KD // 2)
                act.wait_ge(ga_stored[q], 16 * KD // 2)
            act.dma_start(g_attn[:], ga_dram).then_inc(ga_loaded, 16)
            act.dma_start(m_pool[:], mp_dram).then_inc(mp_loaded, 16)
            act.wait_ge(kvn_done, 1)
            act.activation(k_sq[:], kv_nat[:, :, 0:HD], ACT.Square).then_inc(ksq_done, 1)

            def q_squares(t):
                act.wait_ge(qn_done, t + 1)
                if t >= 1:
                    act.wait_ge(qss_done, t)
                if t >= 2:
                    act.wait_ge(at_done, t - 1)
                act.activation(q_sq[:], q_nat[:, t, :], ACT.Square).then_inc(qsq_done, 1)

            def q_hi(t):
                act.wait_ge(qt_done, t + 1)
                for o in range(2):
                    rows = slice(o * HD, (o + 1) * HD)
                    act.activation(q_st[rows, t % 2, o::2, :], ps[rows, 7, :].rearrange("p (c n) -> p c n", c=NH // 2),
                                   ACT.Copy, scale=gq[rows, :]).then_inc(qh_done, 1)

            def softmax_exp(i):
                t, h = ATT[i]
                W = (t + 1) * P
                act.wait_ge(nm_done, i + 1)
                act.activation(probs[:, i % 2, :W], probs[:, i % 2, :W], ACT.Exp, bias=neg_max[:, i % 2:i % 2 + 1],
                               accum_out=row_sum[:, h:h + 1]).then_inc(ex_done, 1)

            def probs_out(i):
                t, h = ATT[i]
                W = (t + 1) * P
                act.wait_ge(tp_done, i + 1)
                if i >= 2:
                    act.wait_ge(pv_done, i - 1)
                act.activation(probs_t[:, i % 2, :W], pair(4)[:, :W], ACT.Copy).then_inc(pt_done, 1)

            q_squares(0)
            act.wait_ge(gq_ready, 1)
            act.wait_ge(kt_done, 1)
            act.activation(k_hi[:], pair(2), ACT.Copy, scale=gk[:, 0:1]).then_inc(kh_done, 1)
            q_hi(0)
            for i, (t, h) in enumerate(ATT):
                if h == 0 and t:
                    act.wait_ge(ri_done, t)
                softmax_exp(i)
                if i >= 1:
                    probs_out(i - 1)
                if h == 2 and t + 1 < NT:
                    q_squares(t + 1)
                if h == 5 and t + 1 < NT:
                    q_hi(t + 1)
                if h == 1 and t:
                    a_hi_out(act, t - 1)
            probs_out(len(ATT) - 1)
            a_hi_out(act, NT - 1)
            act.wait_ge(at_done, NT)
            act.dma_start(gain[:], norm_ffn.broadcast_to([P, D])).then_inc(gain2_in, 16)
            for j in range(KD):
                if j % 2:
                    hi_until(at["ba", j // 2] + 3)
                act.wait_ge(mf_done, j + 1)
                act.activation(m_hi[:, j, :], m_f[:, j % 2, :], ACT.Copy).then_inc(mh_done, 1)
            act.wait_ge(mf_done, KD)
            act.dma_start(x2[:], x[0].rearrange("(t p) d -> p t d", p=P)).then_inc(x_loaded, 16)
            hi_until(N_UP)
            for t in range(NT + 1):
                if t < NT:
                    act.wait_ge(x2_done, NT + t + 1)
                    if t >= 2:
                        act.wait_ge(tr2_done, t - 1)
                    act.activation(xn2[:, t % 2, :], x2[:, t, :], ACT.Square,
                                   accum_out=ssq[:, t:t + 1]).then_inc(sq2_done, 1)
                    act.dma_start(x2_dram[:, t, :], x2[:, t, :]).then_inc(x2_stored, 16)
                if t >= 1:
                    s = t - 1
                    act.wait_ge(tr2_done, s + 1)
                    act.activation(h2_hi[:, :, s * P:(s + 1) * P],
                                   pair(4 + 2 * (s % 2)).rearrange("p (c n) -> p c n", c=KD),
                                   ACT.Copy).then_inc(xh2_done, 1)
                if t in (1, 2):
                    split_hi(Block(N_UP + t - 1))

            def gate_up(i):
                for b in range(2):
                    split_hi(Block(N_UP + 2 + 2 * b, i, 4))
                    act.wait_ge(used, N_UP + 4 * i + 2 * b + 1)
                    if not isinstance(i, int):
                        act.wait_ge(act_done, 2 * i + b - 1)
                    act.activation(silu[:, b, :], pair(4 * b), ACT.Silu).then_inc(silu_done, 1)
                    split_hi(Block(N_UP + 3 + 2 * b, i, 4))

            gate_up(0)
            with act.Fori(1, NF // 2) as i:
                gate_up(i)
            act.wait_ge(xl2_done, NT)

            def act_hi_split(m, f, s, first=False):
                if not first:
                    slot_free(act, m, s)
                    act.wait_ge(acl_done, 2 * m + s - 1)
                src = act_t[:, f, :] if isinstance(f, int) else act_t[:, bass.ds(f, 1), :].rearrange("p o n -> p (o n)")
                act.activation(ac_hi[:, s, :], src, ACT.Copy).then_inc(ach_done, 1)

            act.wait_ge(act_done, NF)
            act.wait_ge(used, N_DN)
            act.wait_ge(x2_stored, 16 * NT)
            act.dma_start(x2b[:], x2_dram).then_inc(x2_loaded, 16)
            act_hi_split(0, 0, 0, True)
            act_hi_split(0, 1, 1, True)

            def step(m, f, nxt):
                act_hi_split(m, f, 0)
                if nxt is not None:
                    split_hi(nxt)
                act_hi_split(m, f + 1, 1)

            for j in range(2):
                base = j * DR
                with act.Fori(0, (DR - 1) // 2 - j) as i:
                    for b in range(2):
                        step(base + 1 + b + 2 * i, 2 + 2 * b + 4 * i, Block(N_DN + base + 2 + b, i, 2))
                if j == 0:
                    step(DR, 0, Block(N_DN + DR + 1))
            step(2 * DR - 2, NF - 4, Block(N_ALL - 1))
            step(2 * DR - 1, NF - 2, None)

        @block.tensor
        def _(pe):
            def three(dst, s_hi, s_lo, m_hi_, m_lo_, first, last):
                nc.tensor.matmul(dst, s_hi, m_hi_, start=first, stop=False)
                nc.tensor.matmul(dst, s_hi, m_lo_, start=False, stop=False)
                return nc.tensor.matmul(dst, s_lo, m_hi_, start=False, stop=last)

            def ready(b):
                pe.wait_ge(hi_done, b.n + 1)
                pe.wait_ge(lo_done, b.n + 1)

            def views(b, chunks):
                return (w_hi[:, b.slot, :].rearrange("p (c n) -> p c n", c=chunks),
                        w_lo[:, b.slot, :].rearrange("p (c n) -> p c n", c=chunks))

            def by_column(b, bank, hi, lo):
                wh, wl = views(b, KD)
                for half in range(2):
                    cols = slice(half * HALF, (half + 1) * HALF)
                    for c in range(KD):
                        last = three(ps[:, bank + half, :], wh[:, c, :], wl[:, c, :], hi[:, c, cols], lo[:, c, cols],
                                     c == 0, c == KD - 1)
                return last

            def by_branch(b, bank, k, hi, lo):
                wh, wl = views(b, KA)
                for half in range(2):
                    cols = slice(half * HALF, (half + 1) * HALF)
                    for c in range(KA):
                        last = three(ps[:, bank + half, :], wh[:, c, k * P:(k + 1) * P], wl[:, c, k * P:(k + 1) * P],
                                     hi[:, c, cols], lo[:, c, cols], c == 0, c == KA - 1)
                return last

            def turn(t, src, bank):
                for c in range(KD):
                    last = nc.tensor.transpose(pair(bank)[:, c * P:(c + 1) * P], src[:, c * P:(c + 1) * P], ident[:])
                return last

            pe.wait_ge(ident_ready, 1)
            for t in range(NT):
                pe.wait_ge(xn_done, t + 1)
                if t >= 2:
                    pe.wait_ge(xl_done, t - 1)
                turn(t, xn[:, t % 2, :], 4 + 2 * (t % 2)).then_inc(tr_done, 1)
            pe.wait_ge(xl_done, NT)
            pe.wait_ge(xh_done, NT)
            pe.wait_ge(kwl_done, 3)
            for half in range(2):
                cols = slice(half * HALF, (half + 1) * HALF)
                for c in range(KD):
                    last = three(ps[:, 4 + half, :], kw_hi[:, c, 0:P], kw_lo[:, c, 0:P], h_hi[:, c, cols],
                                 h_lo[:, c, cols], c == 0, c == KD - 1)
            last.then_inc(ki_done, 1)
            for t in range(NT):
                rows = slice(t * P, (t + 1) * P)
                for c in range(KD):
                    last = three(ps[:, 6, t * IH:(t + 1) * IH], h_hi[:, c, rows], h_lo[:, c, rows], kw_hi[:, c, P:],
                                 kw_lo[:, c, P:], c == 0, c == KD - 1)
            last.then_inc(wi_done, 1)
            for k in range(IH // 2):
                b = Block(at["qi", k])
                ready(b)
                if k >= 2:
                    pe.wait_ge(qil_done, 2 * (k - 1))
                by_column(b, 2 * (k % 2), h_hi, h_lo).then_inc(used, 1)
            pe.wait_ge(qil_done, IH)
            pe.wait_ge(kil_done, 1)
            pe.wait_ge(widx_done, 1)
            for i, (t, h) in enumerate(IDX):
                if i >= 4:
                    pe.wait_ge(relu_done, i - 3)
                W = (t + 1) * P
                for s0 in range(0, W, HALF):
                    w = min(HALF, W - s0)
                    dst = pair(2 * (i % 4))[:, s0:s0 + w]
                    q = qi[:, h, t * P:(t + 1) * P]
                    nc.tensor.matmul(dst, q, ki_hi[:, s0:s0 + w], start=True, stop=False)
                    last = nc.tensor.matmul(dst, q, ki_lo[:, s0:s0 + w], start=False, stop=True)
                last.then_inc(is_done, 1)

            def mix(g):
                pe.wait_ge(plh_done, g + 1)
                pe.wait_ge(pll_done, g + 1)
                if g == 0:
                    pe.wait_ge(pwh_done, 1)
                    pe.wait_ge(pwl_done, 1)
                if g >= 2:
                    pe.wait_ge(pth_done, g - 1)
                for half in range(2):
                    cols = slice(half * HALF, (half + 1) * HALF)
                    last = three(ps[:, 4 + 2 * (g % 2) + half, :], pw_hi[:, g, :], pw_lo[:, g, :], pl_hi[:, cols],
                                 pl_lo[:, cols], True, True)
                last.then_inc(pm_done, 1)

            pe.wait_ge(relu_done, len(IDX))
            for g in range(G):
                b = Block(at["u", g])
                ready(b)
                if g >= 2:
                    pe.wait_ge(ue_done, g - 1)
                by_column(b, 2 * (g % 2), h_hi, h_lo).then_inc(used, 1)
                if g:
                    mix(g - 1)
            for jj in range(KD // 2):
                for j in (2 * jj, 2 * jj + 1):
                    b = Block(at["gp", j])
                    ready(b)
                    if j < 2:
                        pe.wait_ge(ue_done, G)
                    else:
                        pe.wait_ge(gate_done, j - 1)
                    by_column(b, 2 * (j % 2), h_hi, h_lo).then_inc(used, 1)
                    if j == 0:
                        mix(G - 1)
                b = Block(at["bp", jj])
                ready(b)
                pe.wait_ge(ptl_done, G)
                pe.wait_ge(pth_done, G)
                for j in (2 * jj, 2 * jj + 1):
                    if j >= 2:
                        pe.wait_ge(bpe_done, j - 1)
                    last = by_branch(b, 4 + 2 * (j % 2), j % 2, pt_hi, pt_lo)
                    last.then_inc(used if j % 2 else bp_done, 1)
            for j in range(KD):
                b = Block(at["ga", j])
                ready(b)
                if j < 2:
                    pe.wait_ge(gate_done, KD)
                else:
                    pe.wait_ge(gae_done, j - 1)
                by_column(b, 2 * (j % 2), h_hi, h_lo).then_inc(used, 1)
            pe.wait_ge(gae_done, KD)
            pe.wait_ge(bpe_done, KD)

            def by_token(b, m, hi, lo, chunks, first, last_block, free=None):
                wh, wl = views(b, 2)
                for c in range(2):
                    for t in range(NT):
                        if free is not None and first and c == 0:
                            pe.wait_ge(free[0], free[1] + t + 1)
                        rows = slice(t * P, (t + 1) * P)
                        last = three(ps[:, t, :], hi[:, 2 * m + c, rows], lo[:, 2 * m + c, rows], wh[:, c, :],
                                     wl[:, c, :], first and c == 0, last_block and c == 1)
                return last

            for m in range(KD // 2):
                b = Block(at["q", m])
                ready(b)
                last = by_token(b, m, h_hi, h_lo, KD, m == 0, m == KD // 2 - 1)
                last.then_inc(used, 1)
            b = Block(at["kv", 0])
            ready(b)
            pe.wait_ge(qn_done, 2)
            wh, wl = views(b, KD)
            for t in range(NT):
                rows = slice(t * P, (t + 1) * P)
                for c in range(KD):
                    last = three(pair(0)[:, t * P:(t + 1) * P], h_hi[:, c, rows], h_lo[:, c, rows], wh[:, c, :],
                                 wl[:, c, :], c == 0, c == KD - 1)
            last.then_inc(used, 1)
            pe.wait_ge(kn_done, 2)
            pe.wait_ge(qn_done, NT)
            for t in range(NT):
                last = nc.tensor.transpose(pair(2)[:, t * P:(t + 1) * P],
                                           kn[:, t, :, :].rearrange("p a d -> p (a d)"), ident[:])
            last.then_inc(kt_done, 1)

            def q_turn(t):
                pe.wait_ge(qs_done, t + 1)
                if t >= 2:
                    pe.wait_ge(al_done, t - 1)
                for c in range(KA):
                    last = nc.tensor.transpose(ps[:, 7, c * P:(c + 1) * P], q_s[:, c * P:(c + 1) * P], ident[:])
                last.then_inc(qt_done, 1)

            def qk(i):
                t, h = ATT[i]
                W = (t + 1) * P
                if h == 0:
                    pe.wait_ge(ql_done, 2 * (t + 1))
                    pe.wait_ge(qh_done, 2 * (t + 1))
                if i >= 2:
                    pe.wait_ge(lg_done, i - 1)
                for s0 in range(0, W, HALF):
                    w = min(HALF, W - s0)
                    dst = pair(2 * (i % 2))[:, s0:s0 + w]
                    q = q_st[:, t % 2, h, :]
                    nc.tensor.matmul(dst, q, k_hi[:, s0:s0 + w], start=True, stop=False)
                    last = nc.tensor.matmul(dst, q, k_lo[:, s0:s0 + w], start=False, stop=True)
                last.then_inc(qk_done, 1)

            def turn_probs(i):
                t, h = ATT[i]
                pe.wait_ge(ex_done, i + 1)
                if i >= 1:
                    pe.wait_ge(pt_done, i)
                for k in range(t + 1):
                    last = nc.tensor.transpose(pair(4)[:, k * P:(k + 1) * P], probs[:, i % 2, k * P:(k + 1) * P],
                                               ident[:])
                last.then_inc(tp_done, 1)

            def pv(i):
                t, h = ATT[i]
                pe.wait_ge(pt_done, i + 1)
                if h == 0 and t:
                    pe.wait_ge(an_done, t)
                for k in range(t + 1):
                    last = nc.tensor.matmul(ps[:, 6, h * HD:(h + 1) * HD], probs_t[:, i % 2, k * P:(k + 1) * P],
                                            kv_nat[:, k, HD:2 * HD], start=(k == 0), stop=(k == t))
                last.then_inc(pv_done, 1)

            def a_turn(t):
                pe.wait_ge(an_done, t + 1)
                if t + 1 < NT:
                    pe.wait_ge(ql_done, 2 * (t + 2))
                    pe.wait_ge(qh_done, 2 * (t + 2))
                for c in range(KA):
                    last = nc.tensor.transpose(ps[:, 7, c * P:(c + 1) * P], a_nat[:, c * P:(c + 1) * P], ident[:])
                last.then_inc(at_done, 1)

            q_turn(0)
            pe.wait_ge(kl_done, 1)
            qk(0)
            for i, (t, h) in enumerate(ATT):
                if i + 1 < len(ATT):
                    qk(i + 1)
                turn_probs(i)
                if i >= 1:
                    pv(i - 1)
                if h == 0 and t:
                    a_turn(t - 1)
                if h == 4 and t + 1 < NT:
                    q_turn(t + 1)
            pv(len(ATT) - 1)
            a_turn(NT - 1)
            pe.wait_ge(al_done, NT)
            pe.wait_ge(ah_done, NT)
            for jj in range(KD // 2):
                b = Block(at["ba", jj])
                ready(b)
                for j in (2 * jj, 2 * jj + 1):
                    if j >= 4:
                        pe.wait_ge(mg_done, j - 3)
                    last = by_branch(b, 2 * (j % 4), j % 2, a_hi, a_lo)
                    last.then_inc(used if j % 2 else ba_done, 1)
            pe.wait_ge(ml_done, KD)
            pe.wait_ge(mh_done, KD)
            pe.wait_ge(mg_done, KD)
            for j in range(2):
                for m in range(KD // 2):
                    b = Block(at["wo", 4 * j + m])
                    ready(b)
                    last = by_token(b, m, m_hi, m_lo, KD, m == 0, m == KD // 2 - 1, (x2_done, 0) if j else None)
                    last.then_inc(used, 1)
            for t in range(NT):
                pe.wait_ge(xn2_done, t + 1)
                if t >= 2:
                    pe.wait_ge(xl2_done, t - 1)
                turn(t, xn2[:, t % 2, :], 4 + 2 * (t % 2)).then_inc(tr2_done, 1)
            pe.wait_ge(xl2_done, NT)
            pe.wait_ge(xh2_done, NT)

            def gate_up(i):
                for b in range(2):
                    if not isinstance(i, int):
                        pe.wait_ge(act_done, 2 * i + b - 1)
                    for k in range(2):
                        blk = Block(N_UP + 2 * b + k, i, 4)
                        ready(blk)
                        by_column(blk, 4 * b + 2 * k, h2_hi, h2_lo).then_inc(used, 1)

            gate_up(0)
            with pe.Fori(1, NF // 2) as i:
                gate_up(i)
            pe.wait_ge(act_done, NF)

            def down(blk, c0, first, last_block, free=None):
                ready(blk)
                wh, wl = views(blk, 2)
                for c in range(2):
                    pe.wait_ge(ach_done, c0 + c + 1)
                    pe.wait_ge(acl_done, c0 + c + 1)
                    for t in range(NT):
                        if free is not None and c == 0:
                            pe.wait_ge(free, t + 1)
                        rows = slice(t * P, (t + 1) * P)
                        last = three(ps[:, t, :], ac_hi[:, c, rows], ac_lo[:, c, rows], wh[:, c, :], wl[:, c, :],
                                     first and c == 0, last_block and c == 1)
                    last.then_inc(used if c else ac_used, 1)

            for j in range(2):
                base = j * DR
                down(Block(N_DN + base), 2 * base, True, False, y_done if j else None)
                with pe.Fori(0, (DR - 1) // 2 - 1) as i:
                    for b in range(2):
                        down(Block(N_DN + base + 1 + b, i, 2), 2 * base + 2 + 2 * b + 4 * i, False, False)
                down(Block(N_DN + base + DR - 2), 2 * (base + DR - 2), False, False)
                down(Block(N_DN + base + DR - 1), 2 * (base + DR - 1), False, True)

        @block.vector
        def _(dve):
            def minus(dst, a, b):
                return nc.vector.tensor_tensor(dst, a, b, ALU.subtract)

            for g, w in enumerate(POOL_WINDOWS):
                for k in range(PAD):
                    nc.vector.memset(edge[:, g * PAD + k:g * PAD + k + 1],
                                     float(w) / min(k + 1, w)).then_inc(edge_ready, 1)
            dve.wait_ge(kw_in, 16)
            dve.wait_ge(kwh_done, 3)
            minus(kw_lo[:, :, 0:HD], kw_raw[:, :, 0:HD], kw_hi[:, :, 0:HD].bitcast(F32)).then_inc(kwl_done, 1)
            minus(kw_lo[:, :, HD:P], kw_raw[:, :, 0:HD], kw_hi[:, :, HD:P].bitcast(F32)).then_inc(kwl_done, 1)
            minus(kw_lo[:, :, P:], kw_raw[:, :, HD:], kw_hi[:, :, P:].bitcast(F32)).then_inc(kwl_done, 1)
            dve.wait_ge(consts_in, 16 * 6)
            for t in range(NT + 1):
                if t < NT:
                    dve.wait_ge(rs_done, t + 1)
                    dve.wait_ge(x_landed[t % 2], 16 * (t // 2 + 1))
                    if t >= 2:
                        dve.wait_ge(tr_done, t - 1)
                    nc.vector.scalar_tensor_tensor(xn[:, t % 2, :], x_in[:, t % 2, :], rs[:, t:t + 1], gain[:],
                                                   ALU.mult, ALU.mult).then_inc(xn_done, 1)
                if t >= 1:
                    s = t - 1
                    dve.wait_ge(xh_done, s + 1)
                    tile = slice(s * P, (s + 1) * P)
                    minus(h_lo[:, :, tile], pair(4 + 2 * (s % 2)).rearrange("p (c n) -> p c n", c=KD),
                          h_hi[:, :, tile].bitcast(F32)).then_inc(xl_done, 1)
            nc.vector.tensor_scalar(gq[:], gq[:], HD ** -0.5, None, ALU.mult).then_inc(gq_ready, 1)
            dve.wait_ge(pw_in, 16)
            dve.wait_ge(kih_done, 1)
            minus(ki_lo[:], pair(4), ki_hi[:].bitcast(F32)).then_inc(kil_done, 1)
            dve.wait_ge(wi_done, 1)
            nc.vector.tensor_scalar(w_idx[:], ps[:, 6, 0:NT * IH], IDX_SCALE, None, ALU.mult).then_inc(widx_done, 1)
            for b in range(IH // 2):
                src = pair(2 * (b % 2))
                dve.wait_ge(qih_done, 2 * b + 1)
                minus(qi[HD:P, 2 * b, :], src[0:HD, :], qi[0:HD, 2 * b, :].bitcast(F32)).then_inc(qil_done, 1)
                dve.wait_ge(qih_done, 2 * b + 2)
                minus(qi[0:HD, 2 * b + 1, :], src[HD:P, :], qi[HD:P, 2 * b + 1, :].bitcast(F32)).then_inc(qil_done, 1)
            dve.wait_ge(widx_done, 1)
            for i, (t, h) in enumerate(IDX):
                dve.wait_ge(relu_done, i + 1)
                W = (t + 1) * P
                w = w_idx[:, t * IH + h:t * IH + h + 1]
                s = score_tile(t)
                if h == 0:
                    nc.vector.tensor_scalar(s, relu[:, i % 3, :W], w, None, ALU.mult).then_inc(acc_done, 1)
                else:
                    dve.wait_ge(acc_done, i)
                    nc.vector.scalar_tensor_tensor(s, relu[:, i % 3, :W], w, s, ALU.mult, ALU.add).then_inc(acc_done, 1)
            dve.wait_ge(pwh_done, 1)
            minus(pw_lo[:], pw_raw[:], pw_hi[:].bitcast(F32)).then_inc(pwl_done, 1)

            def search_round(t, k):
                if k:
                    dve.wait_ge(replaced, k)
                nc.vector.max(top8[:], score_tile(t)).then_inc(max_found, 1)
                dve.wait_ge(max_found, k + 1)
                nc.vector.match_replace(score_tile(t), top8[:], score_tile(t), TAKEN).then_inc(replaced, 1)

            def end_rounds(k):
                dve.wait_ge(replaced, k)
                dve.wait_ge(max_found, k)
                dve.sem_clear(replaced)
                dve.sem_clear(max_found)

            UNROLL = 8
            for k, t in enumerate(QH):
                if t == LATE:
                    break
                dve.wait_ge(masked, k + 1)
                with dve.Fori(0, ROUNDS // UNROLL):
                    for r in range(UNROLL):
                        search_round(t, r)
                    end_rounds(UNROLL)
            late_round = [0]

            def search_late():
                if late_round[0] == 0:
                    dve.wait_ge(masked, len(QH))
                search_round(LATE, late_round[0])
                late_round[0] += 1

            dve.wait_ge(ksq_done, 1)
            nc.vector.tensor_reduce(kss[:], k_sq[:], AX.X, ALU.add).then_inc(kss_done, 1)
            dve.wait_ge(krs_done, 1)
            for o in range(2):
                nc.vector.tensor_tensor(kn[:, :, o, :], kv_nat[:, :, 0:HD], krs[:].unsqueeze(2).broadcast_to([P, NT, HD]),
                                        ALU.mult).then_inc(kn_done, 1)

            def q_norm_tile(t):
                dve.wait_ge(qsq_done, t + 1)
                if t:
                    dve.wait_ge(qrs_done, t)
                nc.vector.tensor_reduce(qss[:], q_sq[:].rearrange("p (h d) -> p h d", h=NH), AX.X,
                                        ALU.add).then_inc(qss_done, 1)

            def q_scale_tile(t):
                dve.wait_ge(qrs_done, t + 1)
                if t:
                    dve.wait_ge(qt_done, t)
                nc.vector.tensor_tensor(q_s[:].rearrange("p (h d) -> p h d", h=NH),
                                        q_nat[:, t, :].rearrange("p (h d) -> p h d", h=NH),
                                        qrs[:].unsqueeze(2).broadcast_to([P, NH, HD]), ALU.mult).then_inc(qs_done, 1)

            def q_lo(t):
                for o in range(2):
                    dve.wait_ge(qh_done, 2 * t + o + 1)
                    rows, other = slice(o * HD, (o + 1) * HD), slice((1 - o) * HD, (2 - o) * HD)
                    nc.vector.scalar_tensor_tensor(q_st[other, t % 2, o::2, :],
                                                   ps[rows, 7, :].rearrange("p (c n) -> p c n", c=NH // 2),
                                                   gq[rows, :], q_st[rows, t % 2, o::2, :].bitcast(F32),
                                                   ALU.mult, ALU.subtract).then_inc(ql_done, 1)

            def distances(t):
                W = (t + 1) * P
                if t < T0:
                    nc.vector.tensor_scalar(dist[:, :W], key_minus_row[:, :W], float(-t * P), None,
                                            ALU.add).then_inc(dist_done, 1)
                    dve.wait_ge(pen_done, t + 1)
                    return
                s = score_tile(t)
                if t == LATE:
                    dve.wait_ge(replaced, ROUNDS)
                nc.vector.tensor_scalar(s, s, TAKEN, PENALTY, ALU.is_gt, ALU.mult).then_inc(pen_done, 1)
                dve.wait_ge(pen_done, t + 1)
                nc.vector.scalar_tensor_tensor(dist[:, :W], key_minus_row[:, :W], float(-t * P), s, ALU.add,
                                               ALU.add).then_inc(dist_done, 1)
                dve.wait_ge(dist_done, t + 1)

            def logits(i):
                t, h = ATT[i]
                W = (t + 1) * P
                if i:
                    dve.wait_ge(lg_done, i)
                nc.vector.tensor_scalar(bias[:, :W], dist[:, :W], SLOPES[h], None, ALU.mult).then_inc(bias_done, 1)
                dve.wait_ge(bias_done, i + 1)
                dve.wait_ge(qk_done, i + 1)
                if i >= 2:
                    dve.wait_ge(tp_done, i - 1)
                nc.vector.tensor_tensor_reduce(probs[:, i % 2, :W], pair(2 * (i % 2))[:, :W], bias[:, :W], 1.0, MASKED,
                                               ALU.add, ALU.max, row_max[:, i % 2:i % 2 + 1]).then_inc(lg_done, 1)
                dve.wait_ge(lg_done, i + 1)
                if i >= 2:
                    dve.wait_ge(ex_done, i - 1)
                nc.vector.tensor_scalar(neg_max[:, i % 2:i % 2 + 1], row_max[:, i % 2:i % 2 + 1], -1.0, None,
                                        ALU.mult).then_inc(nm_done, 1)

            def attended(t):
                dve.wait_ge(ex_done, NH * (t + 1))
                nc.vector.reciprocal(row_inv[:], row_sum[:]).then_inc(ri_done, 1)
                dve.wait_ge(ri_done, t + 1)
                dve.wait_ge(pv_done, NH * (t + 1))
                if t + 1 < NT:
                    dve.wait_ge(qss_done, t + 2)
                nc.vector.tensor_tensor(a_nat[:].rearrange("p (h d) -> p h d", h=NH),
                                        ps[:, 6, :].rearrange("p (h d) -> p h d", h=NH),
                                        row_inv[:].unsqueeze(2).broadcast_to([P, NH, HD]), ALU.mult).then_inc(an_done, 1)

            def attended_lo(t):
                dve.wait_ge(ah_done, t + 1)
                tile = slice(t * P, (t + 1) * P)
                minus(a_lo[:, :, tile], ps[:, 7, :].rearrange("p (c n) -> p c n", c=KA),
                      a_hi[:, :, tile].bitcast(F32)).then_inc(al_done, 1)

            q_norm_tile(0)
            q_scale_tile(0)
            dve.wait_ge(kh_done, 1)
            nc.vector.scalar_tensor_tensor(k_lo[:], pair(2), gk[:, 0:1], k_hi[:].bitcast(F32), ALU.mult,
                                           ALU.subtract).then_inc(kl_done, 1)
            q_lo(0)
            for i, (t, h) in enumerate(ATT):
                if h == 0 and t == LATE:
                    while late_round[0] < ROUNDS:
                        search_late()
                if h == 0:
                    distances(t)
                logits(i)
                if t < LATE and i * ROUNDS // SPREAD >= late_round[0] and late_round[0] < ROUNDS:
                    search_late()
                if h == 3 and t + 1 < NT:
                    q_norm_tile(t + 1)
                if h == 4 and t + 1 < NT:
                    q_scale_tile(t + 1)
                if h == 6 and t + 1 < NT:
                    q_lo(t + 1)
                if h == 0 and t:
                    attended(t - 1)
                if h == 2 and t:
                    attended_lo(t - 1)
            attended(NT - 1)
            attended_lo(NT - 1)
            dve.wait_ge(ga_loaded, 16)
            dve.wait_ge(mp_loaded, 16)
            for j in range(KD):
                if j % 2:
                    multiplied(dve, "ba", j // 2)
                else:
                    dve.wait_ge(ba_done, j // 2 + 1)
                if j >= 2:
                    dve.wait_ge(ml_done, j - 1)
                nc.vector.tensor_tensor(m_f[:, j % 2, :], pair(2 * (j % 4)), g_attn[:, j, :], ALU.mult).then_inc(mg_done, 1)
                dve.wait_ge(mg_done, j + 1)
                nc.vector.tensor_tensor(m_f[:, j % 2, :], m_f[:, j % 2, :], m_pool[:, j, :], ALU.add).then_inc(mf_done, 1)
            dve.wait_ge(x_loaded, 16)
            for j in range(2):
                multiplied(dve, "wo", 4 * j + 3)
                for t in range(NT):
                    cols = slice(j * HALF, (j + 1) * HALF)
                    nc.vector.tensor_tensor(x2[:, t, cols], ps[:, t, :], x2[:, t, cols], ALU.add).then_inc(x2_done, 1)
            dve.wait_ge(gain2_in, 16)
            dve.wait_ge(x2_done, 2 * NT)
            for t in range(NT + 1):
                if t < NT:
                    dve.wait_ge(rs2_done, t + 1)
                    if t >= 2:
                        dve.wait_ge(tr2_done, t - 1)
                    nc.vector.scalar_tensor_tensor(xn2[:, t % 2, :], x2[:, t, :], rs[:, t:t + 1], gain[:],
                                                   ALU.mult, ALU.mult).then_inc(xn2_done, 1)
                if t >= 1:
                    s = t - 1
                    dve.wait_ge(xh2_done, s + 1)
                    tile = slice(s * P, (s + 1) * P)
                    minus(h2_lo[:, :, tile], pair(4 + 2 * (s % 2)).rearrange("p (c n) -> p c n", c=KD),
                          h2_hi[:, :, tile].bitcast(F32)).then_inc(xl2_done, 1)
            dve.wait_ge(x2_stored, 16 * NT)
            dve.wait_ge(tr2_done, NT)

            def gate_up(i):
                for b in range(2):
                    f = 2 * i + b
                    dve.wait_ge(silu_done, f + 1)
                    dve.wait_ge(used, N_UP + 4 * i + 2 * b + 2)
                    dst = act_t[:, f, :] if isinstance(f, int) else act_t[:, bass.ds(f, 1), :].rearrange("p o n -> p (o n)")
                    nc.vector.tensor_tensor(dst, pair(4 * b + 2), silu[:, b, :], ALU.mult).then_inc(act_done, 1)

            gate_up(0)
            with dve.Fori(1, NF // 2) as i:
                gate_up(i)
            def act_lo(m, f, s, first=False):
                dve.wait_ge(ach_done, 2 * m + s + 1)
                if not first:
                    slot_free(dve, m, s)
                src = act_t[:, f, :] if isinstance(f, int) else act_t[:, bass.ds(f, 1), :].rearrange("p o n -> p (o n)")
                minus(ac_lo[:, s, :], src, ac_hi[:, s, :].bitcast(F32)).then_inc(acl_done, 1)

            dve.wait_ge(act_done, NF)
            dve.wait_ge(used, N_DN)
            act_lo(0, 0, 0, True)
            act_lo(0, 1, 1, True)
            for j in range(2):
                with dve.Fori(0, (NF - 2) // 2) as i:
                    for b in range(2):
                        act_lo(j * DR + 1 + i, 2 + 2 * i + b, b)
                if j == 0:
                    act_lo(DR, 0, 0)
                    act_lo(DR, 1, 1)
                    dve.wait_ge(x2_loaded, 16)
                dve.wait_ge(used, N_DN + DR * (j + 1))
                for t in range(NT):
                    if j:
                        dve.wait_ge(y_stored, 16 * NT)
                    nc.vector.tensor_tensor(y[:, t, :], ps[:, t, :], x2b[:, t, j * HALF:(j + 1) * HALF],
                                            ALU.add).then_inc(y_done, 1)


_INS = ["x", "norm_mix", "w_in", "q_norm", "k_norm", "w_pool_group", "pool_scale", "w_branch_attn",
        "w_branch_pool", "w_out", "norm_ffn", "w_ffn_gate", "w_ffn_up", "w_ffn_down"]
_OUTS = [((1, 1024, 1024), "float32")]


def kernel(**inputs):
    import numpy as _np
    import concourse.bacc as _bacc
    from concourse import mybir as _mybir
    from concourse.bass_utils import run_bass_kernel_spmd as _run

    nc = _bacc.Bacc("TRN2", target_bir_lowering=False, num_devices=1)
    arrays, args = {}, []
    for name in _INS:
        a = _np.ascontiguousarray(inputs[name])
        arrays[f"in_{name}_dram"] = a
        args.append(nc.dram_tensor(f"in_{name}_dram", a.shape, _mybir.dt.from_np(a.dtype), kind="ExternalInput").ap())
    for i, (shape, dtype) in enumerate(_OUTS):
        dt = _mybir.dt.from_np(_np.dtype(dtype))
        args.append(nc.dram_tensor(f"out_{i}_dram", shape, dt, kind="ExternalOutput").ap())
    hybrid_block(nc, *args)
    r = _run(nc, [arrays], core_ids=[0])
    got = tuple(r.results[0][f"out_{i}_dram"] for i in range(len(_OUTS)))
    return got[0]
```

```python
from contextlib import ExitStack

import concourse.bass as bass
from concourse import mybir

F32 = mybir.dt.float32
F32R = mybir.dt.float32r
F16 = mybir.dt.float16
I32 = mybir.dt.int32
U8 = mybir.dt.uint8
ALU = mybir.AluOpType
ACT = mybir.ActivationFunctionType
AX = mybir.AxisListType

P = 128
HALF = 512
SLOT = 1024
RMS_EPS = 1e-6
TOPK_MAX = 256
POOL_WINDOWS = (2, 4, 8, 16)
PAD = max(POOL_WINDOWS)
MASKED = -3.0e38
PENALTY = -1e30


class Block:

    def __init__(self, products, at, i=0, step=0):
        self.slot = at % 2
        self.n = at + step * i
        self.turn = at // 2 + (step // 2) * i
        self.first = at < 2 and step == 0
        self.freed = None if self.first else products[at - 1] + step * i


def hybrid_block(nc, x, norm_mix, w_in, q_norm, k_norm, w_pool_group, pool_scale, w_branch_attn,
                 w_branch_pool, w_out, norm_ffn, w_ffn_gate, w_ffn_up, w_ffn_down, out):
    _, S, D = x.shape
    HD = q_norm.shape[1]
    AW = w_branch_attn.shape[1]
    NH = AW // HD
    PW = w_branch_pool.shape[1]
    G = PW // P
    F = w_ffn_gate.shape[2]
    IH = (w_in.shape[2] - AW - 2 * HD - HD - PW - 2 * D) // (HD + 1)
    NT, KD, KA, KP, NF = S // P, D // P, AW // P, PW // P, F // P
    KEEP = min(TOPK_MAX, S // 4)
    T0 = KEEP // P
    NS = NT - T0
    IDX_SCALE = (IH ** -0.5) * (HD ** -0.5)
    SLOPES = [2.0 ** (-8.0 * (h + 1) / NH) for h in range(NH)]
    assert (S, D, HD, NH, IH, G) == (1024, 1024, 64, 8, 8, 4) and NF % 2 == 0

    C_Q, C_KV, C_QI = 0, AW, AW + 2 * HD
    C_KI = C_QI + IH * HD
    C_U = C_KI + HD + IH
    C_GA = C_U + PW
    C_GP = C_GA + D

    w_in0 = w_in[0].rearrange("(c p) n -> p c n", p=P)
    w_bp = w_branch_pool[0].rearrange("(c p) n -> p c n", p=P)
    w_ba = w_branch_attn[0].rearrange("(c p) n -> p c n", p=P)
    w_o = w_out[0].rearrange("(c p) n -> p c n", p=P)
    w_g = w_ffn_gate[0].rearrange("(c p) n -> p c n", p=P)
    w_u = w_ffn_up[0].rearrange("(c p) n -> p c n", p=P)
    w_d = w_ffn_down[0].rearrange("(c p) n -> p c n", p=P)

    plan = []
    for b in range(IH // 2):
        plan.append(("qi", b, w_in0[:, :, C_QI + b * P:C_QI + (b + 1) * P], 2))
    plan.append(("kv", 0, w_in0[:, :, C_KV:C_KV + 2 * HD], 2))
    for c in range(KA):
        plan.append(("q", c, w_in0[:, :, C_Q + c * P:C_Q + (c + 1) * P], 2))
    for g in range(G):
        plan.append(("u", g, w_in0[:, :, C_U + g * P:C_U + (g + 1) * P], 2))
    plan.append(("ga", 0, w_in0[:, :, C_GA:C_GA + P], 2))
    for j in range(KD):
        plan.append(("gp", j, w_in0[:, :, C_GP + j * P:C_GP + (j + 1) * P], 2))
        plan.append(("bp", j, w_bp[:, :, j * P:(j + 1) * P], 2))
    for j in range(1, KD):
        plan.append(("ga", j, w_in0[:, :, C_GA + j * P:C_GA + (j + 1) * P], 2))
    for jj in range(KD // 2):
        plan.append(("ba", jj, w_ba[:, :, jj * 2 * P:(jj + 1) * 2 * P], 2))
    for j in range(2):
        for m in range(KD // 2):
            plan.append(("wo", 4 * j + m, w_o[:, 2 * m:2 * m + 2, j * HALF:(j + 1) * HALF], 1))
    at = {(kind, k): n for n, (kind, k, _, _) in enumerate(plan)}
    N_UP = len(plan)
    N_DN = N_UP + 2 * NF
    DR = NF // 2
    N_ALL = N_DN + 2 * DR
    PRODUCTS = [0]
    for n in range(N_ALL):
        PRODUCTS.append(PRODUCTS[-1] + (plan[n][3] if n < N_UP else 1))
    N_QI = PRODUCTS[at["kv", 0]]
    QI_ORDER = [(0, 0), (1, 0), (0, 1), (1, 1), (2, 0), (2, 1), (3, 0), (3, 1)]
    FIRST_SUM = [sum(k + 2 for k in range(g)) + 1 for g in range(G)]
    PRODUCTS[1] = 3

    def product(kind, k, part=0):
        return PRODUCTS[at[kind, k]] + part + 1

    def pooled_in(g):
        return g % 2

    def block(n, i=0, step=0):
        return Block(PRODUCTS, n, i, step)

    ATT = [(t, h) for t in range(NT) for h in range(NH)]
    QH = range(T0, NT)
    IDX = [(t, h) for t in QH for h in range(IH)]
    slots = []
    tied = {}
    for n in range(at["kv", 0], at["ba", 0]):
        kind, k = plan[n][:2]
        for q in range(2 if kind == "bp" else 4):
            if kind in ("kv", "q") and q in (1, 3):
                tied.setdefault(len(slots) + 1, []).append(("turn", kind, k, q // 2))
            if kind == "u" and q == 3:
                e = len(slots)
                tied.setdefault(e + 1, []).append(("window", k))
                tied.setdefault(e + 5, []).insert(0, ("pooled", k))
                tied.setdefault(e + 6, []).append(("mix", k, 0))
                tied.setdefault(e + 7, []).append(("mix", k, 1))
                if k == G - 1:
                    start_att = e + 9
            slots.append((n, q, []))
    n_stream = len(slots)
    us_pe = us_dve = 0.0
    idx = att = turned = prepped = 0
    TOP_BIT = 30
    search = [("sign",)] + [("bit", b) for b in range(TOP_BIT, -1, -1)] + [("select", t) for t in QH]
    found = 0
    s = 0
    while s < n_stream or att < len(ATT) + 3 or turned < NT:
        if s >= n_stream:
            slots.append((None, 0, []))
        side = slots[s][2]
        us_pe += 2.6 if s < n_stream else 0.5
        side.extend(tied.get(s, []))
        while idx < len(IDX) and us_dve < us_pe + 1:
            t, h = IDX[idx]
            side.append(("idx", idx))
            us_pe += 4 * (t + 1) * P / 2400
            us_dve = max(us_dve, us_pe) + (t + 1) * P / 960 + 0.1
            idx += 1
        if s == start_att:
            side += [("knorm",), ("qnorm", 0)]
        if s == start_att + 1:
            side += [("kturn", 0), ("qscale", 0)]
        if s == start_att + 2:
            side += [("kturn", 1), ("qturn", 0)]
        if s > start_att + 2 and att < len(ATT) + 3:
            i = att
            t, h = ATT[i] if i < len(ATT) else (NT, i - len(ATT))
            ready = t < T0 or t == NT or found >= TOP_BIT + 3 + t - T0
            if ready and (us_dve < us_pe + 3 or s >= n_stream):
                if h == 0 and t < T0:
                    side.append(("dist", t))
                    us_dve += 0.2
                if h == 2 and t:
                    side.append(("attend", t - 1))
                    us_dve += 0.8
                if i < len(ATT) + 2:
                    side.append(("att", i))
                    us_pe += 5 * (t + 1) * P / 2400
                    us_dve = max(us_dve, us_pe - 1) + 1.55 * (t + 1) * P / 960 + 0.4
                if t + 1 < NT:
                    side += {2: [("qnorm", t + 1)], 4: [("qscale", t + 1)], 5: [("qturn", t + 1)]}.get(h, [])
                    us_dve += {2: 0.6, 4: 0.6, 5: 1.3}.get(h, 0)
                att += 1
        if s > n_stream and turned < NT and att > NH * (turned + 1) + 2:
            side.append(("aturn", turned))
            us_dve += 0.6
            us_pe += 0.4
            turned += 1
        if idx == len(IDX):
            while found < len(search) and us_dve < us_pe + 1:
                side.append(search[found])
                if search[found][0] == "select":
                    us_dve += 8 * (search[found][1] + 1) * P / 960 + 0.5
                else:
                    us_dve += sum(P * (t + 1) for t in QH) / 1920 + 1.0
                found += 1
        if s >= n_stream:
            us_pe = max(us_pe, us_dve - 1)
        s += 1

    with ExitStack() as ctx:
        def sem(name):
            return ctx.enter_context(nc.semaphore(name))

        BASE = (nc.sbuf_base + 63) // 64 * 64
        KB = 1024
        A_CONST = BASE
        A_G = A_CONST + 512 + 2 * KB
        A_STAGE = A_G + 4 * KB
        A_R2 = A_STAGE + 24 * KB
        A_R1 = A_R2 + 64 * KB
        A_SC = A_R1 + 40 * KB
        SC_AT = [0] * NT
        n = 0
        for t in range(T0, NT):
            SC_AT[t] = n
            n += (t + 1) * P
        A_R3 = A_SC + 4 * n
        A_WORK = A_R3 + 28 * KB
        A_D01 = A_WORK + 16 * KB
        A_GB = A_D01 + 4 * 3 * P
        A_RANK = A_GB + 8 * KB
        A_SMALL = A_RANK + 2 * KB
        small = [A_SMALL]

        def sb(name, shape, dt, offset):
            return nc.alloc_sbuf_tensor_at(name, shape, dt, offset=offset)

        def tiny(name, n, dt=F32):
            a = sb(name, [P, n], dt, small[0])
            small[0] += (4 * n + 31) // 32 * 32
            return a

        ident = sb("ident", [P, P], F32, A_CONST)
        key_minus_row = sb("key_minus_row", [P, S], F16, A_CONST + 512)
        gain = sb("gain", [P, D], F32, A_G)
        raw = sb("raw", [P, 2, SLOT], F32, A_STAGE)
        w_hi = sb("w_hi", [P, 2, SLOT], F32R, A_STAGE + 8 * KB)
        w_lo = sb("w_lo", [P, 2, SLOT], F32R, A_STAGE + 16 * KB)
        h_hi = sb("h_hi", [P, KD, S], F32R, A_R2)
        h_lo = sb("h_lo", [P, KD, S], F32R, A_R2 + 32 * KB)
        qi = sb("qi", [P, IH, S], F32R, A_R1)
        ki_hi = sb("ki_hi", [P, S], F32R, A_R1 + 32 * KB)
        ki_lo = sb("ki_lo", [P, S], F32R, A_R1 + 36 * KB)
        scores = sb("scores", [P, n], F32, A_SC)
        rank = sb("rank", [P, S], F16, A_RANK)
        reached = sb("reached", [P, 2, S], U8, A_RANK)
        x_in = sb("x_in", [P, 4, D], F32, A_SC)
        xn = sb("xn", [P, 2, D], F32, A_WORK)
        x_sq = sb("x_sq", [P, D], F32, A_WORK + 8 * KB)
        KW = HD + IH
        kw_raw = sb("kw_raw", [P, KD, KW], F32, A_R3)
        kw_hi = sb("kw_hi", [P, KD, KW], F32R, A_R3 + 3 * KB)
        kw_lo = sb("kw_lo", [P, KD, KW], F32R, A_R3 + 6 * KB)
        wi_t = sb("wi_t", [P, S], F32, A_R3 + 20 * KB)
        relu = sb("relu", [P, 3, S], F32, A_WORK)
        u_raw = sb("u_raw", [P, 2, S], F32, A_R1 + 32 * KB)
        PADDED = 4 * (PAD + S)
        u_pad = sb("u_pad", [P, PAD + S], F32, A_WORK)
        win = [sb(f"win{k}", [P, PAD + S], F32, A_WORK + (k + 1) * PADDED) for k in range(2)]
        pt_f = sb("pt_f", [P, HALF], F32, A_WORK + 3 * PADDED)
        pl_hi = sb("pl_hi", [P, S], F32R, A_R3 + 20 * KB)
        pl_lo = sb("pl_lo", [P, S], F32R, A_R3 + 24 * KB)
        pw_raw = sb("pw_raw", [P, G, P], F32, A_R3 + 13 * KB)
        pw_hi = sb("pw_hi", [P, G, P], F32R, A_GB + 4 * KB)
        pw_lo = sb("pw_lo", [P, G, P], F32R, A_GB + 6 * KB)
        pt_hi = sb("pt_hi", [P, KP, S], F32R, A_R1)
        pt_lo = sb("pt_lo", [P, KP, S], F32R, A_R1 + 16 * KB)
        gate = sb("gate", [P, 2, HALF], F32, A_GB)
        bp = sb("bp", [P, 2, HALF], F32, A_GB + 4 * KB)
        nat_t = sb("nat_t", [P, 2, HALF], F32, A_G)
        q_nat = sb("q_nat", [P, NT, AW], F32, A_R3)
        kv_nat = sb("kv_nat", [P, NT, 2 * HD], F32, A_R3 + 16 * KB)
        q_st = sb("q_st", [P, 2, NH, P], F32R, A_R3 + 20 * KB)
        k_sq = sb("k_sq", [P, NT, HD], F32, A_WORK + 12 * KB)
        kn = sb("kn", [P, NT, 2, HD], F32, A_WORK + 8 * KB)
        probs = sb("probs", [P, 2, S], F32, A_WORK)
        probs_t = sb("probs_t", [P, 2, S], F32, A_WORK + 8 * KB)
        dist01 = sb("dist01", [P, 3 * P], F32, A_D01)
        q_sq = sb("q_sq", [P, AW], F32, A_G)
        q_s = sb("q_s", [P, AW], F32, A_G + 2 * KB)
        a_hi = sb("a_hi", [P, KA, S], F32R, A_R2)
        a_lo = sb("a_lo", [P, KA, S], F32R, A_R2 + 16 * KB)
        k_hi = sb("k_hi", [P, S], F32R, A_R1 + 32 * KB)
        k_lo = sb("k_lo", [P, S], F32R, A_R1 + 36 * KB)
        g_attn = sb("g_attn", [P, KD, S], F32, A_R2 + 32 * KB)
        m_pool = sb("m_pool", [P, KD, S], F32, A_R1)
        m_f = sb("m_f", [P, 2, S], F32, A_R1 + 32 * KB)
        m_hi = sb("m_hi", [P, KD, S], F32R, A_SC)
        m_lo = sb("m_lo", [P, KD, S], F32R, A_SC + 32 * KB)
        x2 = sb("x2", [P, NT, D], F32, A_R2)
        xn2 = sb("xn2", [P, 2, D], F32, A_R1)
        h2_hi = sb("h2_hi", [P, KD, S], F32R, A_SC)
        h2_lo = sb("h2_lo", [P, KD, S], F32R, A_SC + 32 * KB)
        act_t = sb("act_t", [P, NF, S], F32, A_R2)
        silu = sb("silu", [P, 2, S], F32, A_R2 + 88 * KB)
        x2b = sb("x2b", [P, NT, D], F32, A_SC)
        ac_hi = sb("ac_hi", [P, 2, S], F32R, A_SC + 32 * KB)
        ac_lo = sb("ac_lo", [P, 2, S], F32R, A_SC + 40 * KB)
        y = sb("y", [P, NT, HALF], F32, A_SC + 48 * KB)

        ssq = tiny("ssq", NT)
        ms = tiny("ms", NT)
        rs = tiny("rs", NT)
        minus_half = tiny("minus_half", NT)
        w_idx = tiny("w_idx", NT * IH)
        edge = tiny("edge", G * PAD)
        counts = tiny("counts", NS)
        above = tiny("above", NS)
        flips = tiny("flips", NS, I32)
        threshold = tiny("threshold", NS, I32)
        bit_value = tiny("bit_value", TOP_BIT + 1, I32)
        kss = tiny("kss", NT)
        krs = tiny("krs", NT)
        qss = tiny("qss", NH)
        qrs = tiny("qrs", NH)
        row_max = tiny("row_max", 2)
        neg_max = tiny("neg_max", 2)
        row_sum = tiny("row_sum", 2 * NH)
        row_inv = tiny("row_inv", NH)
        gq = tiny("gq", 1)
        gk = tiny("gk", 1)
        psc = tiny("psc", G)
        assert small[0] <= nc.sbuf_usable_end, (small[0], nc.sbuf_usable_end)

        ps = ctx.enter_context(nc.psum_tensor("ps", [P, 8, HALF], F32))
        ga_dram = nc.dram_tensor("ga_scratch", [P, KD, S], F32, kind="Internal").ap()
        mp_dram = nc.dram_tensor("mp_scratch", [P, KD, S], F32, kind="Internal").ap()
        x2_dram = nc.dram_tensor("x2_scratch", [P, NT, D], F32, kind="Internal").ap()

        def pair(b):
            return ps[:, b:b + 2, :].rearrange("p b n -> p (b n)")

        raw_landed = [sem("raw_landed0"), sem("raw_landed1")]
        hi_done, lo_done, products = sem("hi_done"), sem("lo_done"), sem("products")
        evac = sem("evac")
        consts_in, kw_in, pw_in, cst = sem("consts_in"), sem("kw_in"), sem("pw_in"), sem("cst")
        ident_ready, edge_ready, gq_ready = sem("ident_ready"), sem("edge_ready"), sem("gq_ready")
        x_landed = [sem(f"x_landed{k}") for k in range(4)]
        sq_done, ms_done, rs_done = sem("sq_done"), sem("ms_done"), sem("rs_done")
        xn_done, tr_done, xh_done, xl_done = sem("xn_done"), sem("tr_done"), sem("xh_done"), sem("xl_done")
        kwh_done, kwl_done = sem("kwh_done"), sem("kwl_done")
        ki_done, kih_done, kil_done = sem("ki_done"), sem("kih_done"), sem("kil_done")
        wit_done, wi_turned, widx_done = sem("wit_done"), sem("wi_turned"), sem("widx_done")
        qih_done, qil_done = sem("qih_done"), sem("qil_done")
        is_done, relu_done, acc_done, masked = sem("is_done"), sem("relu_done"), sem("acc_done"), sem("masked")
        bits_ready, counted, flips_done, threshold_done = (sem("bits_ready"), sem("counted"), sem("flips_done"),
                                                           sem("threshold_done"))
        select_step = sem("select_step")
        turned_up, nat_done = sem("turned_up"), sem("nat_done")
        pwh_done, pwl_done, pads = sem("pwh_done"), sem("pwl_done"), sem("pads")
        win_done, plf_done, plh_done, pll_done = sem("win_done"), sem("plf_done"), sem("plh_done"), sem("pll_done")
        u_copied = sem("u_copied")
        pm_done, ptf_done, pth_done, ptl_done = sem("pm_done"), sem("ptf_done"), sem("pth_done"), sem("ptl_done")
        mp_done = sem("mp_done")
        mp_stored = [sem("mp_stored0"), sem("mp_stored1")]
        ga_stored = [sem("ga_stored0"), sem("ga_stored1")]
        ksq_done, kss_done, kms_done, krs_done = sem("ksq_done"), sem("kss_done"), sem("kms_done"), sem("krs_done")
        kn_done, kt_done, kh_done, kl_done = sem("kn_done"), sem("kt_done"), sem("kh_done"), sem("kl_done")
        qsq_done, qss_done, qms_done, qrs_done = sem("qsq_done"), sem("qss_done"), sem("qms_done"), sem("qrs_done")
        qs_done, qt_done, qh_done, ql_done = sem("qs_done"), sem("qt_done"), sem("qh_done"), sem("ql_done")
        pen_done, dist_done, bias_done = sem("pen_done"), sem("dist_done"), sem("bias_done")
        qk_done, lg_done, nm_done, ex_done = sem("qk_done"), sem("lg_done"), sem("nm_done"), sem("ex_done")
        tp_done, pt_done, pv_done = sem("tp_done"), sem("pt_done"), sem("pv_done")
        ri_done, an_done, at_done, ah_done, al_done = (sem("ri_done"), sem("an_done"), sem("at_done"),
                                                       sem("ah_done"), sem("al_done"))
        ga_loaded, mp_loaded, x_loaded, gain2_in = sem("ga_loaded"), sem("mp_loaded"), sem("x_loaded"), sem("gain2_in")
        mg_done, mf_done, mh_done, ml_done = sem("mg_done"), sem("mf_done"), sem("mh_done"), sem("ml_done")
        x2_done, x2_stored, x2_loaded = sem("x2_done"), sem("x2_stored"), sem("x2_loaded")
        sq2_done, ms2_done, rs2_done = sem("sq2_done"), sem("ms2_done"), sem("rs2_done")
        xn2_done, tr2_done, xh2_done, xl2_done = sem("xn2_done"), sem("tr2_done"), sem("xh2_done"), sem("xl2_done")
        silu_done, act_done = sem("silu_done"), sem("act_done")
        ach_done, acl_done, ac_used = sem("ach_done"), sem("acl_done"), sem("ac_used")
        y_done, y_stored = sem("y_done"), sem("y_stored")

        engines = ctx.enter_context(nc.Block())

        def score_tile(t):
            return scores[:, SC_AT[t]:SC_AT[t] + (t + 1) * P]

        def dist_tile(t):
            return score_tile(t) if t >= T0 else dist01[:, t * P:(2 * t + 1) * P]

        def wait_evac(eng, kind, k, half):
            eng.wait_ge(evac, product(kind, k, half) - N_QI)

        def load(sp, b, src):
            if not b.first:
                sp.wait_ge(hi_done, b.n - 1)
                sp.wait_ge(lo_done, b.n - 1)
            c, n = src.shape[1], src.shape[2]
            dst = raw[:, b.slot, 0:c * n].rearrange("p (c n) -> p c n", c=c)
            sp.dma_start(dst, src).then_inc(raw_landed[b.slot], 16)

        def load_gate_up(sp, i):
            for b in range(2):
                for k, w in enumerate((w_g, w_u)):
                    f = 2 * i + b
                    cols = slice(f * P, (f + 1) * P) if isinstance(f, int) else bass.ds(f * P, P)
                    load(sp, block(N_UP + 2 * b + k, i, 4), w[:, :, cols])

        def multiplied(eng, kind, k, part=0):
            eng.wait_ge(products, product(kind, k, part))

        def slot_free(eng, m, s):
            if s == 0:
                eng.wait_ge(ac_used, m)
            else:
                eng.wait_ge(products, PRODUCTS[N_DN] + m)

        @engines.sync
        def _(sp):
            for t in range(NT):
                if t >= 4:
                    sp.wait_ge(xn_done, t - 3)
                    sp.wait_ge(sq_done, t - 3)
                sp.dma_start(x_in[:, t % 4, :], x[0, t * P:(t + 1) * P, :]).then_inc(x_landed[t % 4], 16)
                if t == 0:
                    sp.dma_start(gain[:], norm_mix.broadcast_to([P, D])).then_inc(consts_in, 16)
                if t in (3, 4):
                    load(sp, block(t - 3), plan[t - 3][2])
            for n in range(2, N_UP):
                load(sp, block(n), plan[n][2])
            load_gate_up(sp, 0)
            with sp.Fori(1, NF // 2) as i:
                load_gate_up(sp, i)
            for j in range(2):
                cols = slice(j * HALF, (j + 1) * HALF)
                load(sp, block(N_DN + j * DR), w_d[:, 0:2, cols])
                with sp.Fori(0, (DR - 1) // 2) as i:
                    for b in range(2):
                        load(sp, block(N_DN + j * DR + 1 + b, i, 2),
                             w_d[:, bass.ds(2 + 2 * b + 4 * i, 2), cols])
            for j in range(2):
                for t in range(NT):
                    sp.wait_ge(y_done, j * NT + t + 1)
                    sp.dma_start(out[0, t * P:(t + 1) * P, j * HALF:(j + 1) * HALF],
                                 y[:, t, :]).then_inc(y_stored, 16)
            sp.wait_ge(y_stored, 16 * 2 * NT)

        @engines.gpsimd
        def _(pool):
            state = {"n": 0}

            def split_lo(b, width=SLOT):
                pool.wait_ge(hi_done, b.n + 1)
                pool.wait_ge(raw_landed[b.slot], 16 * (b.turn + 1))
                if not b.first:
                    pool.wait_ge(products, b.freed)
                pool.tensor_tensor(w_lo[:, b.slot, :width], raw[:, b.slot, :width],
                                   w_hi[:, b.slot, :width].bitcast(F32), ALU.subtract).then_inc(lo_done, 1)

            def lo_until(n):
                while state["n"] < n:
                    k = state["n"]
                    src = plan[k][2] if k < N_UP else None
                    split_lo(block(k), src.shape[1] * src.shape[2] if src is not None else SLOT)
                    state["n"] += 1

            pool.memset(minus_half[:], -0.5).then_inc(cst, 1)
            pool.memset(ident[:], 0.0).then_inc(cst, 1)
            pool.iota(key_minus_row[:], [[1, S]], base=0, channel_multiplier=-1,
                      allow_small_or_imprecise_dtypes=True).then_inc(cst, 1)
            for b in range(TOP_BIT + 1):
                pool.memset(bit_value[:, b:b + 1], 1 << b).then_inc(bits_ready, 1)
            pool.wait_ge(cst, 2)
            pool.affine_select(out=ident[:], in_=ident[:], compare_op=ALU.not_equal, fill=1.0, base=0,
                               pattern=[[-1, P]], channel_multiplier=1).then_inc(ident_ready, 1)

            def rstd(k, n, sums, means, out_, ready, m_done, r_done, count):
                pool.wait_ge(ready, k)
                pool.tensor_scalar(means, sums, 1.0 / count, RMS_EPS, ALU.mult, ALU.add).then_inc(m_done, 1)
                pool.wait_ge(m_done, k)
                pool.tensor_tensor(out_, means, minus_half[:, 0:n], ALU.pow).then_inc(r_done, 1)

            def future(tile, t, fill, signal):
                diag = tile[:, t * P:(t + 1) * P]
                pool.affine_select(out=diag, in_=diag, compare_op=ALU.is_ge, fill=fill, base=0,
                                   pattern=[[-1, P]], channel_multiplier=1).then_inc(signal, 1)

            pool.wait_ge(cst, 3)
            for t in range(NT):
                rstd(t + 1, 1, ssq[:, t:t + 1], ms[:, t:t + 1], rs[:, t:t + 1], sq_done, ms_done, rs_done, D)
                if t == 4:
                    lo_until(1)
                if t == 6:
                    lo_until(2)
            lo_until(at["kv", 0] + 2)
            sums = 0
            for n, q, side in slots:
                if n is not None and q == 0:
                    lo_until(n + 2)
                if n is not None and q == 1 and plan[n][0] == "bp":
                    j = plan[n][1]
                    for half in range(2):
                        wait_evac(pool, "bp", j, half)
                        pool.tensor_tensor(bp[:, half, :], bp[:, half, :], gate[:, half, :],
                                           ALU.mult).then_inc(mp_done, 1)
                for what, *arg in side:
                    if what == "idx" and arg[0] % IH == IH - 1:
                        t = IDX[arg[0]][0]
                        pool.wait_ge(acc_done, arg[0] + 1)
                        future(score_tile(t), t, MASKED, masked)
                    elif what == "window":
                        g = arg[0]
                        w = POOL_WINDOWS[g]
                        if g == 0:
                            pool.wait_ge(acc_done, len(IDX))
                            for buf in (u_pad, win[0], win[1]):
                                pool.memset(buf[:, 0:PAD], 0.0).then_inc(pads, 1)
                            pool.wait_ge(pads, 3)
                            pool.wait_ge(edge_ready, G * PAD)
                        wait_evac(pool, "u", g, 1)
                        if g:
                            pool.wait_ge(pll_done, g)
                            pool.wait_ge(plh_done, g)
                        src, d, k = u_pad, 1, 0
                        while d < w:
                            pool.tensor_tensor(win[k][:, PAD:], src[:, PAD:], src[:, PAD - d:PAD + S - d],
                                               ALU.add).then_inc(win_done, 1)
                            sums += 1
                            pool.wait_ge(win_done, sums)
                            src, d, k = win[k], 2 * d, 1 - k
                        pool.tensor_tensor(src[:, PAD:2 * PAD], src[:, PAD:2 * PAD], edge[:, g * PAD:(g + 1) * PAD],
                                           ALU.mult).then_inc(win_done, 1)
                        sums += 1
                        pool.wait_ge(win_done, sums)
                        pool.wait_ge(u_copied, 2 * (g + 1))
                        pool.tensor_tensor(src[:, PAD:], src[:, PAD:], u_raw[:, g % 2, :],
                                           ALU.subtract).then_inc(plf_done, 1)
                    elif what == "pooled":
                        g = arg[0]
                        pool.wait_ge(plh_done, g + 1)
                        if g:
                            pool.wait_ge(pm_done, 2 * g)
                        pool.tensor_tensor(pl_lo[:], win[pooled_in(g)][:, PAD:], pl_hi[:].bitcast(F32),
                                           ALU.subtract).then_inc(pll_done, 1)
                    elif what == "mix":
                        g, half = arg
                        k = 2 * g + half
                        pool.wait_ge(pth_done, k + 1)
                        pool.wait_ge(ptf_done, k + 1)
                        cols = slice(half * HALF, (half + 1) * HALF)
                        pool.tensor_tensor(pt_lo[:, g, cols], pt_f[:], pt_hi[:, g, cols].bitcast(F32),
                                           ALU.subtract).then_inc(ptl_done, 1)
                    elif what == "knorm":
                        rstd(1, NT, kss[:], kss[:], krs[:], kss_done, kms_done, krs_done, HD)
                    elif what == "qnorm":
                        rstd(arg[0] + 1, NH, qss[:], qss[:], qrs[:], qss_done, qms_done, qrs_done, HD)
                    elif what == "dist" and arg[0] < T0:
                        t = arg[0]
                        pool.wait_ge(dist_done, t + 1)
                        future(dist_tile(t), t, PENALTY, pen_done)
            lo_until(at["ba", 0] + 2)
            for j in range(KD):
                if j % 2:
                    lo_until(at["ba", j // 2] + 3)
                pool.wait_ge(mh_done, j + 1)
                pool.tensor_tensor(m_lo[:, j, :], m_f[:, j % 2, :], m_hi[:, j, :].bitcast(F32),
                                   ALU.subtract).then_inc(ml_done, 1)
            lo_until(N_UP)
            for t in range(NT):
                rstd(t + 1, 1, ssq[:, t:t + 1], ms[:, t:t + 1], rs[:, t:t + 1], sq2_done, ms2_done, rs2_done, D)
            split_lo(block(N_UP))
            split_lo(block(N_UP + 1))
            with pool.Fori(0, (N_ALL - N_UP - 2) // 2) as i:
                split_lo(block(N_UP + 2, i, 2))
                split_lo(block(N_UP + 3, i, 2))

        @engines.scalar
        def _(act):
            state = {"n": 0}

            def split_hi(b, width=SLOT):
                act.wait_ge(raw_landed[b.slot], 16 * (b.turn + 1))
                if not b.first:
                    act.wait_ge(products, b.freed)
                    act.wait_ge(lo_done, b.n - 1)
                act.activation(w_hi[:, b.slot, :width], raw[:, b.slot, :width], ACT.Copy).then_inc(hi_done, 1)

            def hi_until(n):
                while state["n"] < n:
                    k = state["n"]
                    src = plan[k][2] if k < N_UP else None
                    split_hi(block(k), src.shape[1] * src.shape[2] if src is not None else SLOT)
                    state["n"] += 1

            act.dma_start(kw_raw[:], w_in0[:, :, C_KI:C_KI + KW]).then_inc(kw_in, 16)
            act.dma_start(pw_raw[:], w_pool_group[0].rearrange("g c n -> c g n")).then_inc(pw_in, 16)
            for k in range(2):
                act.dma_start(gq[k * HD:(k + 1) * HD, :], q_norm.rearrange("a d -> d a")).then_inc(consts_in, 16)
                act.dma_start(gk[k * HD:(k + 1) * HD, :], k_norm.rearrange("a d -> d a")).then_inc(consts_in, 16)
            act.dma_start(psc[:], pool_scale.rearrange("a (g p) -> p (a g)", p=P),
                          allow_slow_non_contiguous=True).then_inc(consts_in, 16)

            def indexer_keys(half):
                act.wait_ge(ki_done, half + 1)
                cols = slice(half * HALF, (half + 1) * HALF)
                for o in range(2):
                    act.activation(ki_hi[o * HD:(o + 1) * HD, cols], ps[0:HD, 2 + half, :], ACT.Copy).then_inc(kih_done, 1)
                act.activation(wi_t[HD:KW, cols], ps[HD:KW, 2 + half, :], ACT.Copy, scale=IDX_SCALE).then_inc(wit_done, 1)

            def indexer_queries(u):
                act.wait_ge(products, u + 1)
                b, half = QI_ORDER[u]
                cols = slice(half * HALF, (half + 1) * HALF)
                act.activation(qi[0:HD, 2 * b, cols], ps[0:HD, u % 2, :], ACT.Copy).then_inc(qih_done, 1)
                act.activation(qi[HD:P, 2 * b + 1, cols], ps[HD:P, u % 2, :], ACT.Copy).then_inc(qih_done, 1)

            for t in range(NT + 1):
                if t < NT:
                    act.wait_ge(x_landed[t % 4], 16 * (t // 4 + 1))
                    if t:
                        act.wait_ge(sq_done, t)
                    act.activation(x_sq[:], x_in[:, t % 4, :], ACT.Square,
                                   accum_out=ssq[:, t:t + 1]).then_inc(sq_done, 1)
                if t == 0:
                    act.wait_ge(kw_in, 16)
                    act.activation(kw_hi[:], kw_raw[:], ACT.Copy).then_inc(kwh_done, 1)
                if t >= 1:
                    s = t - 1
                    act.wait_ge(tr_done, s + 1)
                    act.activation(h_hi[:, :, s * P:(s + 1) * P],
                                   pair(4 + 2 * (s % 2)).rearrange("p (c n) -> p c n", c=KD),
                                   ACT.Copy).then_inc(xh_done, 1)
                if t == 3:
                    hi_until(1)
                if t == 4:
                    hi_until(2)
                    act.wait_ge(pw_in, 16)
                    act.activation(pw_hi[:], pw_raw[:], ACT.Copy).then_inc(pwh_done, 1)
                if t == 6:
                    indexer_keys(0)
                    indexer_queries(0)
            indexer_queries(1)
            indexer_keys(1)
            for u in range(2, N_QI):
                hi_until({2: 2, 3: 3, 4: 4, 5: 4, 6: 5, 7: 5}[u])
                indexer_queries(u)
            hi_until(at["kv", 0] + 2)

            def q_squares(t):
                if t == 0:
                    act.wait_ge(nat_done, 2 * (KA + 1))
                else:
                    act.wait_ge(qss_done, t)
                act.activation(q_sq[:], q_nat[:, t, :], ACT.Square).then_inc(qsq_done, 1)

            def q_hi(t):
                act.wait_ge(qt_done, t + 1)
                if t == 0:
                    act.wait_ge(gq_ready, 1)
                for o in range(2):
                    rows = slice(o * HD, (o + 1) * HD)
                    act.activation(q_st[rows, t % 2, o::2, :], ps[rows, 7, :].rearrange("p (c n) -> p c n", c=NH // 2),
                                   ACT.Copy, scale=gq[rows, :]).then_inc(qh_done, 1)

            def softmax_exp(i):
                t, h = ATT[i]
                W = (t + 1) * P
                act.wait_ge(nm_done, i + 1)
                if h == 0 and t >= 2:
                    act.wait_ge(ri_done, t - 1)
                k = (t % 2) * NH + h
                act.activation(probs[:, i % 2, :W], probs[:, i % 2, :W], ACT.Exp, bias=neg_max[:, i % 2:i % 2 + 1],
                               accum_out=row_sum[:, k:k + 1]).then_inc(ex_done, 1)

            def probs_out(i):
                t, h = ATT[i]
                W = (t + 1) * P
                act.wait_ge(tp_done, i + 1)
                if i >= 2:
                    act.wait_ge(pv_done, i - 1)
                act.activation(probs_t[:, i % 2, :W], pair(4)[:, :W], ACT.Copy).then_inc(pt_done, 1)

            def stream_out(kind, k, half):
                multiplied(act, kind, k, half)
                src = ps[:, half, :]
                cols = slice(half * HALF, (half + 1) * HALF)
                if kind in ("kv", "q"):
                    u = 2 * (k + 1) + half if kind == "q" else half
                    if u >= 2:
                        act.wait_ge(turned_up, u - 1)
                    act.activation(nat_t[:, half, :], src, ACT.Copy).then_inc(evac, 1)
                elif kind == "u":
                    if k == 0 and half == 0:
                        act.wait_ge(acc_done, len(IDX))
                        act.wait_ge(is_done, len(IDX))
                    if k >= 1:
                        act.wait_ge(win_done, FIRST_SUM[k - 1])
                    if k >= 2:
                        act.wait_ge(plf_done, k - 1)
                    act.activation(u_raw[:, k % 2, cols], src, ACT.Copy).then_inc(u_copied, 1)
                    act.activation(u_pad[:, PAD + half * HALF:PAD + (half + 1) * HALF], src, ACT.Copy,
                                   scale=1.0 / POOL_WINDOWS[k]).then_inc(evac, 1)
                elif kind == "gp":
                    if k:
                        act.wait_ge(mp_done, 2 * (k - 1) + half + 1)
                    else:
                        act.wait_ge(ga_stored[half], 16)
                    act.activation(gate[:, half, :], src, ACT.Sigmoid).then_inc(evac, 1)
                elif kind == "bp":
                    if k:
                        act.wait_ge(mp_stored[half], 16 * k)
                    act.activation(bp[:, half, :], src, ACT.Copy).then_inc(evac, 1)
                elif kind == "ga":
                    if k >= 1:
                        act.wait_ge(mp_done, 2 * KD - 1 + half)
                        act.wait_ge(ga_stored[half], 16 * k)
                    act.activation(gate[:, half, :], src, ACT.Sigmoid).then_inc(evac, 1)
                    wait_evac(act, "ga", k, half)
                    act.dma_start(ga_dram[:, k, cols], gate[:, half, :]).then_inc(ga_stored[half], 16)

            for n, q, side in slots:
                if n is not None:
                    kind, k = plan[n][:2]
                    if kind == "ga" and q == 0 and k == 1:
                        for half in range(2):
                            act.wait_ge(mp_done, 2 * (KD - 1) + half + 1)
                            act.dma_start(mp_dram[:, KD - 1, half * HALF:(half + 1) * HALF],
                                          bp[:, half, :]).then_inc(mp_stored[half], 16)
                    if kind == "gp" and q == 0 and k:
                        for half in range(2):
                            act.wait_ge(mp_done, 2 * (k - 1) + half + 1)
                            act.dma_start(mp_dram[:, k - 1, half * HALF:(half + 1) * HALF],
                                          bp[:, half, :]).then_inc(mp_stored[half], 16)
                    if q == 0:
                        hi_until(n + 2)
                    if kind == "bp":
                        stream_out(kind, k, q)
                    elif q % 2:
                        stream_out(kind, k, q // 2)
                    if n == at["ba", 0] - 1 and q == 3:
                        for half in range(2):
                            act.wait_ge(mp_stored[half], 16 * KD)
                            act.wait_ge(ga_stored[half], 16 * KD)
                        act.dma_start(g_attn[:], ga_dram).then_inc(ga_loaded, 16)
                        act.dma_start(m_pool[:], mp_dram).then_inc(mp_loaded, 16)
                for what, *arg in side:
                    if what == "turn":
                        kind, k, half = arg
                        u = 2 * (k + 1) + half if kind == "q" else half
                        act.wait_ge(turned_up, u + 1)
                        dst = (kv_nat[:, 4 * half:4 * half + 4, :] if kind == "kv" else
                               q_nat[:, 4 * half:4 * half + 4, k * P:(k + 1) * P])
                        act.activation(dst, ps[:, 6, :].rearrange("p (t n) -> p t n", t=4), ACT.Copy).then_inc(nat_done, 1)
                    elif what == "idx":
                        i = arg[0]
                        t, h = IDX[i]
                        W = (t + 1) * P
                        act.wait_ge(is_done, i + 1)
                        if i >= 3:
                            act.wait_ge(acc_done, i - 2)
                        act.activation(relu[:, i % 3, :W], pair(2 + 2 * (i % 2))[:, :W], ACT.Relu).then_inc(relu_done, 1)
                    elif what == "pooled":
                        g = arg[0]
                        act.wait_ge(plf_done, g + 1)
                        if g:
                            act.wait_ge(pm_done, 2 * g)
                        act.activation(pl_hi[:], win[pooled_in(g)][:, PAD:], ACT.Copy).then_inc(plh_done, 1)
                    elif what == "mix":
                        g, half = arg
                        i = 2 * g + half
                        act.wait_ge(pm_done, i + 1)
                        if i:
                            act.wait_ge(ptl_done, i)
                        act.activation(pt_f[:], ps[:, 7, :], ACT.Copy, scale=psc[:, g:g + 1]).then_inc(ptf_done, 1)
                        act.activation(pt_hi[:, g, half * HALF:(half + 1) * HALF], ps[:, 7, :], ACT.Copy,
                                       scale=psc[:, g:g + 1]).then_inc(pth_done, 1)
                    elif what == "knorm":
                        act.wait_ge(nat_done, 2)
                        act.wait_ge(ptl_done, 2 * G)
                        act.wait_ge(pm_done, 2 * G)
                        act.wait_ge(pll_done, G)
                        act.activation(k_sq[:], kv_nat[:, :, 0:HD], ACT.Square).then_inc(ksq_done, 1)
                    elif what == "kturn":
                        half = arg[0]
                        act.wait_ge(kt_done, half + 1)
                        act.activation(k_hi[:, half * HALF:(half + 1) * HALF], ps[:, 7, :], ACT.Copy,
                                       scale=gk[:, 0:1]).then_inc(kh_done, 1)
                    elif what == "qnorm":
                        q_squares(arg[0])
                    elif what == "qturn":
                        q_hi(arg[0])
                    elif what == "att":
                        i = arg[0]
                        if 1 <= i <= len(ATT):
                            probs_out(i - 1)
                        if i < len(ATT):
                            softmax_exp(i)
                    elif what == "aturn":
                        t = arg[0]
                        act.wait_ge(at_done, t + 1)
                        act.activation(a_hi[:, :, t * P:(t + 1) * P], ps[:, 7, :].rearrange("p (c n) -> p c n", c=KA),
                                       ACT.Copy).then_inc(ah_done, 1)
            act.wait_ge(at_done, NT)
            act.dma_start(gain[:], norm_ffn.broadcast_to([P, D])).then_inc(gain2_in, 16)
            hi_until(at["ba", 0] + 2)
            for j in range(KD):
                if j % 2:
                    hi_until(at["ba", j // 2] + 3)
                act.wait_ge(mf_done, j + 1)
                act.activation(m_hi[:, j, :], m_f[:, j % 2, :], ACT.Copy).then_inc(mh_done, 1)
            act.wait_ge(mf_done, KD)
            act.dma_start(x2[:], x[0].rearrange("(t p) d -> p t d", p=P)).then_inc(x_loaded, 16)
            hi_until(N_UP)
            for t in range(NT + 1):
                if t < NT:
                    act.wait_ge(x2_done, NT + t + 1)
                    if t >= 2:
                        act.wait_ge(tr2_done, t - 1)
                    act.activation(xn2[:, t % 2, :], x2[:, t, :], ACT.Square,
                                   accum_out=ssq[:, t:t + 1]).then_inc(sq2_done, 1)
                    act.dma_start(x2_dram[:, t, :], x2[:, t, :]).then_inc(x2_stored, 16)
                if t >= 1:
                    s = t - 1
                    act.wait_ge(tr2_done, s + 1)
                    act.activation(h2_hi[:, :, s * P:(s + 1) * P],
                                   pair(4 + 2 * (s % 2)).rearrange("p (c n) -> p c n", c=KD),
                                   ACT.Copy).then_inc(xh2_done, 1)
                if t in (1, 2):
                    split_hi(block(N_UP + t - 1))

            def gate_up(i):
                for b in range(2):
                    split_hi(block(N_UP + 2 + 2 * b, i, 4))
                    act.wait_ge(products, PRODUCTS[N_UP] + 4 * i + 2 * b + 1)
                    if not isinstance(i, int):
                        act.wait_ge(act_done, 2 * i + b - 1)
                    act.activation(silu[:, b, :], pair(4 * b), ACT.Silu).then_inc(silu_done, 1)
                    split_hi(block(N_UP + 3 + 2 * b, i, 4))

            gate_up(0)
            with act.Fori(1, NF // 2) as i:
                gate_up(i)
            act.wait_ge(xl2_done, NT)

            def act_hi_split(m, f, s, first=False):
                if not first:
                    slot_free(act, m, s)
                    act.wait_ge(acl_done, 2 * m + s - 1)
                src = act_t[:, f, :] if isinstance(f, int) else act_t[:, bass.ds(f, 1), :].rearrange("p o n -> p (o n)")
                act.activation(ac_hi[:, s, :], src, ACT.Copy).then_inc(ach_done, 1)

            act.wait_ge(act_done, NF)
            act.wait_ge(products, PRODUCTS[N_DN])
            act.wait_ge(x2_stored, 16 * NT)
            act.dma_start(x2b[:], x2_dram).then_inc(x2_loaded, 16)
            act_hi_split(0, 0, 0, True)
            act_hi_split(0, 1, 1, True)

            def step(m, f, nxt):
                act_hi_split(m, f, 0)
                if nxt is not None:
                    split_hi(nxt)
                act_hi_split(m, f + 1, 1)

            for j in range(2):
                base = j * DR
                with act.Fori(0, (DR - 1) // 2 - j) as i:
                    for b in range(2):
                        step(base + 1 + b + 2 * i, 2 + 2 * b + 4 * i, block(N_DN + base + 2 + b, i, 2))
                if j == 0:
                    step(DR, 0, block(N_DN + DR + 1))
            step(2 * DR - 2, NF - 4, block(N_ALL - 1))
            step(2 * DR - 1, NF - 2, None)

        @engines.tensor
        def _(pe):
            def three(dst, s_hi, s_lo, m_hi_, m_lo_, first, last):
                nc.tensor.matmul(dst, s_hi, m_hi_, start=first, stop=False)
                nc.tensor.matmul(dst, s_hi, m_lo_, start=False, stop=False)
                return nc.tensor.matmul(dst, s_lo, m_hi_, start=False, stop=last)

            def ready(b):
                pe.wait_ge(hi_done, b.n + 1)
                pe.wait_ge(lo_done, b.n + 1)

            def views(b, chunks):
                return (w_hi[:, b.slot, :].rearrange("p (c n) -> p c n", c=chunks),
                        w_lo[:, b.slot, :].rearrange("p (c n) -> p c n", c=chunks))

            def by_half(b, half, bank, hi, lo, chunks=None, width=KD):
                wh, wl = (a[:, b.slot, 0:width * P].rearrange("p (c n) -> p c n", c=width) for a in (w_hi, w_lo))
                cols = slice(half * HALF, (half + 1) * HALF)
                for c in chunks if chunks is not None else range(width):
                    last = three(ps[:, bank, :], wh[:, c, :], wl[:, c, :], hi[:, c, cols], lo[:, c, cols],
                                 c == 0, c == width - 1)
                return last

            def by_column(b, bank, hi, lo):
                for half in range(2):
                    last = by_half(b, half, bank + half, hi, lo)
                return last

            def by_branch(b, bank, k, hi, lo):
                wh, wl = views(b, KA)
                for half in range(2):
                    cols = slice(half * HALF, (half + 1) * HALF)
                    for c in range(KA):
                        last = three(ps[:, bank + half, :], wh[:, c, k * P:(k + 1) * P], wl[:, c, k * P:(k + 1) * P],
                                     hi[:, c, cols], lo[:, c, cols], c == 0, c == KA - 1)
                return last

            def turn(t, src, bank):
                for c in range(KD):
                    last = nc.tensor.transpose(pair(bank)[:, c * P:(c + 1) * P], src[:, c * P:(c + 1) * P], ident[:])
                return last

            def turn_x(t):
                pe.wait_ge(xn_done, t + 1)
                if t >= 2:
                    pe.wait_ge(xl_done, t - 1)
                turn(t, xn[:, t % 2, :], 4 + 2 * (t % 2)).then_inc(tr_done, 1)

            def normed(half):
                pe.wait_ge(xh_done, NT // 2 * (half + 1))
                pe.wait_ge(xl_done, NT // 2 * (half + 1))

            def keys_and_weights(half):
                normed(half)
                pe.wait_ge(kwl_done, 1)
                cols = slice(half * HALF, (half + 1) * HALF)
                for c in range(KD):
                    last = three(ps[0:KW, 2 + half, :], kw_hi[:, c, :], kw_lo[:, c, :], h_hi[:, c, cols],
                                 h_lo[:, c, cols], c == 0, c == KD - 1)
                last.then_inc(ki_done, 1)

            def queries(u):
                b, half = QI_ORDER[u]
                normed(half)
                ready(block(at["qi", b]))
                if u >= 2:
                    pe.wait_ge(qil_done, 2 * (u - 1))
                by_half(block(at["qi", b]), half, u % 2, h_hi, h_lo).then_inc(products, 1)

            pe.wait_ge(ident_ready, 1)
            for t in range(4):
                turn_x(t)
            keys_and_weights(0)
            queries(0)
            turn_x(4)
            turn_x(5)
            queries(1)
            turn_x(6)
            turn_x(7)
            keys_and_weights(1)
            queries(2)
            queries(3)
            pe.wait_ge(wit_done, 2)
            for t in range(NT):
                last = nc.tensor.transpose(ps[:, 6, t * IH:(t + 1) * IH], wi_t[HD:KW, t * P:(t + 1) * P],
                                           ident[HD:KW, HD:KW])
            last.then_inc(wi_turned, 1)
            for u in range(4, N_QI):
                queries(u)

            def bank_7(*readers):
                for signal, count in seven["readers"]:
                    pe.wait_ge(signal, count)
                seven["readers"] = readers

            seven = {"readers": ()}

            def qk(i):
                t, h = ATT[i]
                W = (t + 1) * P
                if i == 0:
                    pe.wait_ge(relu_done, len(IDX))
                    pe.wait_ge(kh_done, 2)
                    pe.wait_ge(kl_done, 2)
                if h == 0:
                    pe.wait_ge(qh_done, 2 * (t + 1))
                    pe.wait_ge(ql_done, 2 * (t + 1))
                if i:
                    pe.wait_ge(lg_done, i)
                for s0 in range(0, W, HALF):
                    w = min(HALF, W - s0)
                    dst = pair(2)[:, s0:s0 + w]
                    q = q_st[:, t % 2, h, :]
                    nc.tensor.matmul(dst, q, k_hi[:, s0:s0 + w], start=True, stop=False)
                    last = nc.tensor.matmul(dst, q, k_lo[:, s0:s0 + w], start=False, stop=True)
                last.then_inc(qk_done, 1)

            def turn_probs(i):
                t, h = ATT[i]
                pe.wait_ge(ex_done, i + 1)
                if i:
                    pe.wait_ge(pt_done, i)
                for k in range(t + 1):
                    last = nc.tensor.transpose(pair(4)[:, k * P:(k + 1) * P], probs[:, i % 2, k * P:(k + 1) * P],
                                               ident[:])
                last.then_inc(tp_done, 1)

            def pv(i):
                t, h = ATT[i]
                pe.wait_ge(pt_done, i + 1)
                if i == 0:
                    pe.wait_ge(nat_done, 2 * (KA + 1))
                elif h == 0:
                    pe.wait_ge(an_done, t)
                for k in range(t + 1):
                    last = nc.tensor.matmul(ps[:, 6, h * HD:(h + 1) * HD], probs_t[:, i % 2, k * P:(k + 1) * P],
                                            kv_nat[:, k, HD:2 * HD], start=(k == 0), stop=(k == t))
                last.then_inc(pv_done, 1)

            unit = 0
            for n, q, side in slots:
                if n is not None:
                    kind, k = plan[n][:2]
                    half = q if kind == "bp" else q // 2
                    begins = kind == "bp" or q % 2 == 0
                    if q == 0:
                        ready(block(n))
                    if kind == "bp" and k == 0 and q == 0:
                        pe.wait_ge(pth_done, 2 * G)
                        pe.wait_ge(ptl_done, 2 * G)
                    if begins:
                        if unit < 2:
                            pe.wait_ge(qil_done, 2 * (N_QI - 1 + unit))
                        else:
                            pe.wait_ge(evac, unit - 1)
                        unit += 1
                    if kind == "bp":
                        by_half(block(n), half, half, pt_hi, pt_lo, width=KP).then_inc(products, 1)
                    elif begins:
                        by_half(block(n), half, half, h_hi, h_lo, range(KD // 2))
                    else:
                        by_half(block(n), half, half, h_hi, h_lo, range(KD // 2, KD)).then_inc(products, 1)
                for what, *arg in side:
                    if what == "turn":
                        kind, k, half = arg
                        u = 2 * (k + 1) + half if kind == "q" else half
                        wait_evac(pe, kind, k, half)
                        if u:
                            pe.wait_ge(nat_done, u)
                        else:
                            pe.wait_ge(widx_done, 1)
                        for c in range(4):
                            last = nc.tensor.transpose(ps[:, 6, c * P:(c + 1) * P], nat_t[:, half, c * P:(c + 1) * P],
                                                       ident[:])
                        last.then_inc(turned_up, 1)
                    elif what == "idx":
                        i = arg[0]
                        t, h = IDX[i]
                        if i == 0:
                            pe.wait_ge(qil_done, 2 * N_QI)
                            pe.wait_ge(kil_done, 4)
                            pe.wait_ge(wit_done, 2)
                        if i >= 2:
                            pe.wait_ge(relu_done, i - 1)
                        W = (t + 1) * P
                        for s0 in range(0, W, HALF):
                            w = min(HALF, W - s0)
                            dst = pair(2 + 2 * (i % 2))[:, s0:s0 + w]
                            q_i = qi[:, h, t * P:(t + 1) * P]
                            nc.tensor.matmul(dst, q_i, ki_hi[:, s0:s0 + w], start=True, stop=False)
                            last = nc.tensor.matmul(dst, q_i, ki_lo[:, s0:s0 + w], start=False, stop=True)
                        last.then_inc(is_done, 1)
                    elif what == "mix":
                        g, half = arg
                        pe.wait_ge(plh_done, g + 1)
                        pe.wait_ge(pll_done, g + 1)
                        if g == 0:
                            pe.wait_ge(pwh_done, 1)
                            pe.wait_ge(pwl_done, 1)
                        bank_7((ptf_done, 2 * g + half + 1), (pth_done, 2 * g + half + 1))
                        cols = slice(half * HALF, (half + 1) * HALF)
                        three(ps[:, 7, :], pw_hi[:, g, :], pw_lo[:, g, :], pl_hi[:, cols], pl_lo[:, cols],
                              True, True).then_inc(pm_done, 1)
                    elif what == "kturn":
                        half = arg[0]
                        pe.wait_ge(kn_done, 2)
                        bank_7((kh_done, half + 1), (kl_done, half + 1))
                        for c in range(4):
                            last = nc.tensor.transpose(ps[:, 7, c * P:(c + 1) * P],
                                                       kn[:, 4 * half + c, :, :].rearrange("p a d -> p (a d)"), ident[:])
                        last.then_inc(kt_done, 1)
                    elif what == "qturn":
                        t = arg[0]
                        pe.wait_ge(qs_done, t + 1)
                        bank_7((qh_done, 2 * (t + 1)), (ql_done, 2 * (t + 1)))
                        for c in range(KA):
                            last = nc.tensor.transpose(ps[:, 7, c * P:(c + 1) * P], q_s[:, c * P:(c + 1) * P], ident[:])
                        last.then_inc(qt_done, 1)
                    elif what == "att":
                        i = arg[0]
                        if i < len(ATT):
                            qk(i)
                        if 1 <= i <= len(ATT):
                            turn_probs(i - 1)
                        if i >= 2:
                            pv(i - 2)
                    elif what == "aturn":
                        t = arg[0]
                        pe.wait_ge(an_done, t + 1)
                        bank_7((ah_done, t + 1), (al_done, t + 1))
                        for c in range(KA):
                            last = nc.tensor.transpose(ps[:, 7, c * P:(c + 1) * P], q_nat[:, t, c * P:(c + 1) * P],
                                                       ident[:])
                        last.then_inc(at_done, 1)
            pe.wait_ge(evac, PRODUCTS[at["ba", 0]] - N_QI)
            pe.wait_ge(al_done, NT)
            pe.wait_ge(ah_done, NT)
            for j in range(KD):
                b = block(at["ba", j // 2])
                ready(b)
                if j >= 4:
                    pe.wait_ge(mg_done, j - 3)
                by_branch(b, 2 * (j % 4), j % 2, a_hi, a_lo).then_inc(products, 1)

            def by_token(b, m, hi, lo, first, last_block, free=None):
                wh, wl = views(b, 2)
                for c in range(2):
                    for t in range(NT):
                        if free is not None and first and c == 0:
                            pe.wait_ge(free, t + 1)
                        rows = slice(t * P, (t + 1) * P)
                        last = three(ps[:, t, :], hi[:, 2 * m + c, rows], lo[:, 2 * m + c, rows], wh[:, c, :],
                                     wl[:, c, :], first and c == 0, last_block and c == 1)
                return last

            pe.wait_ge(ml_done, KD)
            pe.wait_ge(mh_done, KD)
            pe.wait_ge(mg_done, KD)
            for j in range(2):
                for m in range(KD // 2):
                    b = block(at["wo", 4 * j + m])
                    ready(b)
                    by_token(b, m, m_hi, m_lo, m == 0, m == KD // 2 - 1, x2_done if j else None).then_inc(products, 1)
            for t in range(NT):
                pe.wait_ge(xn2_done, t + 1)
                if t >= 2:
                    pe.wait_ge(xl2_done, t - 1)
                turn(t, xn2[:, t % 2, :], 4 + 2 * (t % 2)).then_inc(tr2_done, 1)
            pe.wait_ge(xl2_done, NT)
            pe.wait_ge(xh2_done, NT)

            def gate_up(i):
                for b in range(2):
                    if not isinstance(i, int):
                        pe.wait_ge(act_done, 2 * i + b - 1)
                    for k in range(2):
                        blk = block(N_UP + 2 * b + k, i, 4)
                        ready(blk)
                        by_column(blk, 4 * b + 2 * k, h2_hi, h2_lo).then_inc(products, 1)

            gate_up(0)
            with pe.Fori(1, NF // 2) as i:
                gate_up(i)
            pe.wait_ge(act_done, NF)

            def down(blk, c0, first, last_block, free=None):
                ready(blk)
                wh, wl = views(blk, 2)
                for c in range(2):
                    pe.wait_ge(ach_done, c0 + c + 1)
                    pe.wait_ge(acl_done, c0 + c + 1)
                    for t in range(NT):
                        if free is not None and c == 0:
                            pe.wait_ge(free, t + 1)
                        rows = slice(t * P, (t + 1) * P)
                        last = three(ps[:, t, :], ac_hi[:, c, rows], ac_lo[:, c, rows], wh[:, c, :], wl[:, c, :],
                                     first and c == 0, last_block and c == 1)
                    last.then_inc(products if c else ac_used, 1)

            for j in range(2):
                base = j * DR
                down(block(N_DN + base), 2 * base, True, False, y_done if j else None)
                with pe.Fori(0, (DR - 1) // 2 - 1) as i:
                    for b in range(2):
                        down(block(N_DN + base + 1 + b, i, 2), 2 * base + 2 + 2 * b + 4 * i, False, False)
                down(block(N_DN + base + DR - 2), 2 * (base + DR - 2), False, False)
                down(block(N_DN + base + DR - 1), 2 * (base + DR - 1), False, True)

        @engines.vector
        def _(dve):
            def minus(dst, a, b):
                return nc.vector.tensor_tensor(dst, a, b, ALU.subtract)

            for g, w in enumerate(POOL_WINDOWS):
                for k in range(PAD):
                    nc.vector.memset(edge[:, g * PAD + k:g * PAD + k + 1],
                                     float(w) / min(k + 1, w)).then_inc(edge_ready, 1)
            dve.wait_ge(kw_in, 16)
            dve.wait_ge(kwh_done, 1)
            minus(kw_lo[:], kw_raw[:], kw_hi[:].bitcast(F32)).then_inc(kwl_done, 1)

            def indexer_keys(half):
                cols = slice(half * HALF, (half + 1) * HALF)
                dve.wait_ge(kih_done, 2 * half + 2)
                dve.wait_ge(wit_done, half + 1)
                for o in range(2):
                    minus(ki_lo[o * HD:(o + 1) * HD, cols], ps[0:HD, 2 + half, :],
                          ki_hi[0:HD, cols].bitcast(F32)).then_inc(kil_done, 1)

            def indexer_queries(u):
                b, half = QI_ORDER[u]
                cols = slice(half * HALF, (half + 1) * HALF)
                dve.wait_ge(qih_done, 2 * u + 1)
                minus(qi[HD:P, 2 * b, cols], ps[0:HD, u % 2, :], qi[0:HD, 2 * b, cols].bitcast(F32)).then_inc(qil_done, 1)
                dve.wait_ge(qih_done, 2 * u + 2)
                minus(qi[0:HD, 2 * b + 1, cols], ps[HD:P, u % 2, :],
                      qi[HD:P, 2 * b + 1, cols].bitcast(F32)).then_inc(qil_done, 1)

            dve.wait_ge(consts_in, 16 * 6)
            for t in range(NT + 1):
                if t < NT:
                    dve.wait_ge(rs_done, t + 1)
                    dve.wait_ge(x_landed[t % 4], 16 * (t // 4 + 1))
                    if t >= 2:
                        dve.wait_ge(tr_done, t - 1)
                    nc.vector.scalar_tensor_tensor(xn[:, t % 2, :], x_in[:, t % 4, :], rs[:, t:t + 1], gain[:],
                                                   ALU.mult, ALU.mult).then_inc(xn_done, 1)
                if t >= 1:
                    s = t - 1
                    dve.wait_ge(xh_done, s + 1)
                    tile = slice(s * P, (s + 1) * P)
                    minus(h_lo[:, :, tile], pair(4 + 2 * (s % 2)).rearrange("p (c n) -> p c n", c=KD),
                          h_hi[:, :, tile].bitcast(F32)).then_inc(xl_done, 1)
                if t == 6:
                    indexer_keys(0)
                    indexer_queries(0)
            indexer_queries(1)
            indexer_keys(1)
            indexer_queries(2)
            indexer_queries(3)
            dve.wait_ge(wi_turned, 1)
            nc.vector.tensor_scalar(w_idx[:], ps[:, 6, 0:NT * IH], 1.0, None, ALU.mult).then_inc(widx_done, 1)
            dve.wait_ge(pw_in, 16)
            dve.wait_ge(pwh_done, 1)
            minus(pw_lo[:], pw_raw[:], pw_hi[:].bitcast(F32)).then_inc(pwl_done, 1)
            nc.vector.tensor_scalar(gq[:], gq[:], HD ** -0.5, None, ALU.mult).then_inc(gq_ready, 1)
            for u in range(4, N_QI):
                indexer_queries(u)
            dve.wait_ge(widx_done, 1)

            def score_sum(i):
                t, h = IDX[i]
                dve.wait_ge(relu_done, i + 1)
                w = w_idx[:, t * IH + h:t * IH + h + 1]
                s = score_tile(t)
                r = relu[:, i % 3, :(t + 1) * P]
                if h == 0:
                    nc.vector.tensor_scalar(s, r, w, None, ALU.mult).then_inc(acc_done, 1)
                else:
                    dve.wait_ge(acc_done, i)
                    nc.vector.scalar_tensor_tensor(s, r, w, s, ALU.mult, ALU.add).then_inc(acc_done, 1)

            def count_reached(i, k, value, compare, into):
                if i >= 2:
                    dve.wait_ge(counted, i - 1)
                nc.vector.tensor_scalar(reached[:, i % 2, :(T0 + k + 1) * P], score_tile(T0 + k), value, 0.0,
                                        compare, ALU.add, accum_out=into[:, k:k + 1]).then_inc(counted, 1)

            def search_sign():
                dve.wait_ge(masked, NS)
                for k in range(NS):
                    count_reached(k, k, 0.0, ALU.is_ge, counts)
                dve.wait_ge(counted, NS)
                dve.wait_ge(bits_ready, TOP_BIT + 1)
                nc.vector.tensor_scalar(flips[:], counts[:], float(KEEP), -1.0, ALU.is_lt,
                                        ALU.mult).then_inc(flips_done, 1)
                dve.wait_ge(flips_done, 1)
                nc.vector.tensor_tensor(threshold[:], flips[:], bit_value[:, TOP_BIT:].broadcast_to([P, NS]),
                                        ALU.bitwise_xor).then_inc(threshold_done, 1)

            def search_bit(b):
                done = TOP_BIT - b + 1
                dve.wait_ge(threshold_done, done)
                for k in range(NS):
                    count_reached(NS * done + k, k, threshold[:, k:k + 1].bitcast(F32), ALU.is_ge, counts)
                dve.wait_ge(counted, NS * (done + 1))
                nc.vector.tensor_scalar(flips[:], counts[:], float(KEEP), float(1 << b), ALU.is_lt,
                                        ALU.mult).then_inc(flips_done, 1)
                dve.wait_ge(flips_done, done + 1)
                if b:
                    nc.vector.scalar_tensor_tensor(threshold[:], flips[:], bit_value[:, b - 1:b], threshold[:],
                                                   ALU.bitwise_xor, ALU.bitwise_xor).then_inc(threshold_done, 1)
                else:
                    nc.vector.tensor_tensor(threshold[:], flips[:], threshold[:],
                                            ALU.bitwise_xor).then_inc(threshold_done, 1)

            def select(t):
                k = t - T0
                s = score_tile(t)
                r = rank[:, :(t + 1) * P]
                v = threshold[:, k:k + 1].bitcast(F32)
                step = 7 * k
                dve.wait_ge(threshold_done, TOP_BIT + 2)
                if k:
                    dve.wait_ge(select_step, step)
                count_reached(NS * (TOP_BIT + 2) + k, k, v, ALU.is_gt, above)
                dve.wait_ge(counted, NS * (TOP_BIT + 2) + k + 1)
                nc.vector.tensor_scalar(above[:, k:k + 1], above[:, k:k + 1], -1.0, float(KEEP), ALU.mult,
                                        ALU.add).then_inc(select_step, 1)
                nc.vector.tensor_scalar(r, s, v, None, ALU.is_equal).then_inc(select_step, 1)
                dve.wait_ge(select_step, step + 2)
                nc.vector.tensor_tensor_scan(r, r, r, 0.0, ALU.add, ALU.max).then_inc(select_step, 1)
                dve.wait_ge(select_step, step + 3)
                nc.vector.tensor_scalar(r, r, above[:, k:k + 1], None, ALU.is_le).then_inc(select_step, 1)
                dve.wait_ge(select_step, step + 4)
                nc.vector.scalar_tensor_tensor(r, s, v, r, ALU.is_equal, ALU.mult).then_inc(select_step, 1)
                dve.wait_ge(select_step, step + 5)
                nc.vector.scalar_tensor_tensor(s, s, v, r, ALU.is_le, ALU.subtract).then_inc(select_step, 1)
                dve.wait_ge(select_step, step + 6)
                nc.vector.scalar_tensor_tensor(s, s, PENALTY, key_minus_row[:, :(t + 1) * P], ALU.mult,
                                               ALU.add).then_inc(select_step, 1)

            def distances(t):
                nc.vector.tensor_scalar(dist_tile(t), key_minus_row[:, :(t + 1) * P], 1.0, None,
                                        ALU.mult).then_inc(dist_done, 1)

            def logits(i):
                t, h = ATT[i]
                W = (t + 1) * P
                row = probs[:, i % 2, :W]
                if i == 0:
                    dve.wait_ge(pm_done, 2 * G)
                    dve.wait_ge(ptl_done, 2 * G)
                if h == 0 and t < T0:
                    dve.wait_ge(pen_done, t + 1)
                elif h == 0:
                    dve.wait_ge(select_step, 7 * (t - T0 + 1))
                if i >= 2:
                    dve.wait_ge(tp_done, i - 1)
                nc.vector.tensor_scalar(row, dist_tile(t), float(-t * P), SLOPES[h], ALU.add, ALU.mult).then_inc(bias_done, 1)
                dve.wait_ge(bias_done, i + 1)
                dve.wait_ge(qk_done, i + 1)
                nc.vector.tensor_tensor_reduce(row, pair(2)[:, :W], row, 1.0, MASKED, ALU.add, ALU.max,
                                               row_max[:, i % 2:i % 2 + 1]).then_inc(lg_done, 1)
                dve.wait_ge(lg_done, i + 1)
                if i >= 2:
                    dve.wait_ge(ex_done, i - 1)
                nc.vector.tensor_scalar(neg_max[:, i % 2:i % 2 + 1], row_max[:, i % 2:i % 2 + 1], -1.0, None,
                                        ALU.mult).then_inc(nm_done, 1)

            for n, q, side in slots:
                for what, *arg in side:
                    if what == "idx":
                        score_sum(arg[0])
                    elif what == "sign":
                        search_sign()
                    elif what == "bit":
                        search_bit(arg[0])
                    elif what == "select":
                        select(arg[0])
                    elif what == "knorm":
                        dve.wait_ge(ksq_done, 1)
                        nc.vector.tensor_reduce(kss[:], k_sq[:], AX.X, ALU.add).then_inc(kss_done, 1)
                        dve.wait_ge(krs_done, 1)
                        for o in range(2):
                            nc.vector.tensor_tensor(kn[:, :, o, :], kv_nat[:, :, 0:HD],
                                                    krs[:].unsqueeze(2).broadcast_to([P, NT, HD]),
                                                    ALU.mult).then_inc(kn_done, 1)
                    elif what == "kturn":
                        half = arg[0]
                        cols = slice(half * HALF, (half + 1) * HALF)
                        dve.wait_ge(kh_done, half + 1)
                        nc.vector.scalar_tensor_tensor(k_lo[:, cols], ps[:, 7, :], gk[:, 0:1], k_hi[:, cols].bitcast(F32),
                                                       ALU.mult, ALU.subtract).then_inc(kl_done, 1)
                    elif what == "qnorm":
                        t = arg[0]
                        dve.wait_ge(qsq_done, t + 1)
                        if t:
                            dve.wait_ge(qrs_done, t)
                        nc.vector.tensor_reduce(qss[:], q_sq[:].rearrange("p (h d) -> p h d", h=NH), AX.X,
                                                ALU.add).then_inc(qss_done, 1)
                    elif what == "qscale":
                        t = arg[0]
                        dve.wait_ge(qrs_done, t + 1)
                        if t:
                            dve.wait_ge(qt_done, t)
                        nc.vector.tensor_tensor(q_s[:].rearrange("p (h d) -> p h d", h=NH),
                                                q_nat[:, t, :].rearrange("p (h d) -> p h d", h=NH),
                                                qrs[:].unsqueeze(2).broadcast_to([P, NH, HD]),
                                                ALU.mult).then_inc(qs_done, 1)
                    elif what == "qturn":
                        t = arg[0]
                        for o in range(2):
                            dve.wait_ge(qh_done, 2 * t + o + 1)
                            rows, other = slice(o * HD, (o + 1) * HD), slice((1 - o) * HD, (2 - o) * HD)
                            nc.vector.scalar_tensor_tensor(q_st[other, t % 2, o::2, :],
                                                           ps[rows, 7, :].rearrange("p (c n) -> p c n", c=NH // 2),
                                                           gq[rows, :], q_st[rows, t % 2, o::2, :].bitcast(F32),
                                                           ALU.mult, ALU.subtract).then_inc(ql_done, 1)
                    elif what == "dist":
                        distances(arg[0])
                    elif what == "att" and arg[0] < len(ATT):
                        logits(arg[0])
                    elif what == "attend":
                        t = arg[0]
                        dve.wait_ge(ex_done, NH * (t + 1))
                        nc.vector.reciprocal(row_inv[:], row_sum[:, (t % 2) * NH:(t % 2 + 1) * NH]).then_inc(ri_done, 1)
                        dve.wait_ge(ri_done, t + 1)
                        dve.wait_ge(pv_done, NH * (t + 1))
                        nc.vector.tensor_tensor(q_nat[:, t, :].rearrange("p (h d) -> p h d", h=NH),
                                                ps[:, 6, :].rearrange("p (h d) -> p h d", h=NH),
                                                row_inv[:].unsqueeze(2).broadcast_to([P, NH, HD]),
                                                ALU.mult).then_inc(an_done, 1)
                    elif what == "aturn":
                        t = arg[0]
                        dve.wait_ge(ah_done, t + 1)
                        tile = slice(t * P, (t + 1) * P)
                        minus(a_lo[:, :, tile], ps[:, 7, :].rearrange("p (c n) -> p c n", c=KA),
                              a_hi[:, :, tile].bitcast(F32)).then_inc(al_done, 1)
            dve.wait_ge(ga_loaded, 16)
            dve.wait_ge(mp_loaded, 16)
            for j in range(KD):
                multiplied(dve, "ba", j // 2, j % 2)
                if j >= 2:
                    dve.wait_ge(ml_done, j - 1)
                nc.vector.tensor_tensor(m_f[:, j % 2, :], pair(2 * (j % 4)), g_attn[:, j, :], ALU.mult).then_inc(mg_done, 1)
                dve.wait_ge(mg_done, j + 1)
                nc.vector.tensor_tensor(m_f[:, j % 2, :], m_f[:, j % 2, :], m_pool[:, j, :], ALU.add).then_inc(mf_done, 1)
            dve.wait_ge(x_loaded, 16)
            for j in range(2):
                multiplied(dve, "wo", 4 * j + 3)
                for t in range(NT):
                    cols = slice(j * HALF, (j + 1) * HALF)
                    nc.vector.tensor_tensor(x2[:, t, cols], ps[:, t, :], x2[:, t, cols], ALU.add).then_inc(x2_done, 1)
            dve.wait_ge(gain2_in, 16)
            dve.wait_ge(x2_done, 2 * NT)
            for t in range(NT + 1):
                if t < NT:
                    dve.wait_ge(rs2_done, t + 1)
                    if t >= 2:
                        dve.wait_ge(tr2_done, t - 1)
                    nc.vector.scalar_tensor_tensor(xn2[:, t % 2, :], x2[:, t, :], rs[:, t:t + 1], gain[:],
                                                   ALU.mult, ALU.mult).then_inc(xn2_done, 1)
                if t >= 1:
                    s = t - 1
                    dve.wait_ge(xh2_done, s + 1)
                    tile = slice(s * P, (s + 1) * P)
                    minus(h2_lo[:, :, tile], pair(4 + 2 * (s % 2)).rearrange("p (c n) -> p c n", c=KD),
                          h2_hi[:, :, tile].bitcast(F32)).then_inc(xl2_done, 1)
            dve.wait_ge(x2_stored, 16 * NT)
            dve.wait_ge(tr2_done, NT)

            def gate_up(i):
                for b in range(2):
                    f = 2 * i + b
                    dve.wait_ge(silu_done, f + 1)
                    dve.wait_ge(products, PRODUCTS[N_UP] + 4 * i + 2 * b + 2)
                    dst = act_t[:, f, :] if isinstance(f, int) else act_t[:, bass.ds(f, 1), :].rearrange("p o n -> p (o n)")
                    nc.vector.tensor_tensor(dst, pair(4 * b + 2), silu[:, b, :], ALU.mult).then_inc(act_done, 1)

            gate_up(0)
            with dve.Fori(1, NF // 2) as i:
                gate_up(i)
            def act_lo(m, f, s, first=False):
                dve.wait_ge(ach_done, 2 * m + s + 1)
                if not first:
                    slot_free(dve, m, s)
                src = act_t[:, f, :] if isinstance(f, int) else act_t[:, bass.ds(f, 1), :].rearrange("p o n -> p (o n)")
                minus(ac_lo[:, s, :], src, ac_hi[:, s, :].bitcast(F32)).then_inc(acl_done, 1)

            dve.wait_ge(act_done, NF)
            dve.wait_ge(products, PRODUCTS[N_DN])
            act_lo(0, 0, 0, True)
            act_lo(0, 1, 1, True)
            for j in range(2):
                with dve.Fori(0, (NF - 2) // 2) as i:
                    for b in range(2):
                        act_lo(j * DR + 1 + i, 2 + 2 * i + b, b)
                if j == 0:
                    act_lo(DR, 0, 0)
                    act_lo(DR, 1, 1)
                    dve.wait_ge(x2_loaded, 16)
                dve.wait_ge(products, PRODUCTS[N_DN] + DR * (j + 1))
                for t in range(NT):
                    if j:
                        dve.wait_ge(y_stored, 16 * NT)
                    nc.vector.tensor_tensor(y[:, t, :], ps[:, t, :], x2b[:, t, j * HALF:(j + 1) * HALF],
                                            ALU.add).then_inc(y_done, 1)


_INS = ["x", "norm_mix", "w_in", "q_norm", "k_norm", "w_pool_group", "pool_scale", "w_branch_attn",
        "w_branch_pool", "w_out", "norm_ffn", "w_ffn_gate", "w_ffn_up", "w_ffn_down"]
_OUTS = [((1, 1024, 1024), "float32")]


def kernel(**inputs):
    import numpy as _np
    import concourse.bacc as _bacc
    from concourse import mybir as _mybir
    from concourse.bass_utils import run_bass_kernel_spmd as _run

    nc = _bacc.Bacc("TRN2", target_bir_lowering=False, num_devices=1)
    arrays, args = {}, []
    for name in _INS:
        a = _np.ascontiguousarray(inputs[name])
        arrays[f"in_{name}_dram"] = a
        args.append(nc.dram_tensor(f"in_{name}_dram", a.shape, _mybir.dt.from_np(a.dtype), kind="ExternalInput").ap())
    for i, (shape, dtype) in enumerate(_OUTS):
        dt = _mybir.dt.from_np(_np.dtype(dtype))
        args.append(nc.dram_tensor(f"out_{i}_dram", shape, dt, kind="ExternalOutput").ap())
    hybrid_block(nc, *args)
    r = _run(nc, [arrays], core_ids=[0])
    got = tuple(r.results[0][f"out_{i}_dram"] for i in range(len(_OUTS)))
    return got[0]
```

```python
from contextlib import ExitStack

import concourse.bass as bass
from concourse import mybir

F32 = mybir.dt.float32
F32R = mybir.dt.float32r
F16 = mybir.dt.float16
I32 = mybir.dt.int32
U8 = mybir.dt.uint8
ALU = mybir.AluOpType
ACT = mybir.ActivationFunctionType
AX = mybir.AxisListType

P = 128
HALF = 512
SLOT = 1024
RMS_EPS = 1e-6
TOPK_MAX = 256
POOL_WINDOWS = (2, 4, 8, 16)
PAD = max(POOL_WINDOWS)
MASKED = -3.0e38
PENALTY = -1e30


class Block:

    def __init__(self, products, at, i=0, step=0):
        self.slot = at % 2
        self.n = at + step * i
        self.turn = at // 2 + (step // 2) * i
        self.first = at < 2 and step == 0
        self.freed = None if self.first else products[at - 1] + step * i


def hybrid_block(nc, x, norm_mix, w_in, q_norm, k_norm, w_pool_group, pool_scale, w_branch_attn,
                 w_branch_pool, w_out, norm_ffn, w_ffn_gate, w_ffn_up, w_ffn_down, out):
    _, S, D = x.shape
    HD = q_norm.shape[1]
    AW = w_branch_attn.shape[1]
    NH = AW // HD
    PW = w_branch_pool.shape[1]
    G = PW // P
    F = w_ffn_gate.shape[2]
    IH = (w_in.shape[2] - AW - 2 * HD - HD - PW - 2 * D) // (HD + 1)
    NT, KD, KA, KP, NF = S // P, D // P, AW // P, PW // P, F // P
    KEEP = min(TOPK_MAX, S // 4)
    T0 = KEEP // P
    NS = NT - T0
    IDX_SCALE = (IH ** -0.5) * (HD ** -0.5)
    SLOPES = [2.0 ** (-8.0 * (h + 1) / NH) for h in range(NH)]
    assert (S, D, HD, NH, IH, G) == (1024, 1024, 64, 8, 8, 4) and NF % 2 == 0

    C_Q, C_KV, C_QI = 0, AW, AW + 2 * HD
    C_KI = C_QI + IH * HD
    C_U = C_KI + HD + IH
    C_GA = C_U + PW
    C_GP = C_GA + D

    w_in0 = w_in[0].rearrange("(c p) n -> p c n", p=P)
    w_bp = w_branch_pool[0].rearrange("(c p) n -> p c n", p=P)
    w_ba = w_branch_attn[0].rearrange("(c p) n -> p c n", p=P)
    w_o = w_out[0].rearrange("(c p) n -> p c n", p=P)
    w_g = w_ffn_gate[0].rearrange("(c p) n -> p c n", p=P)
    w_u = w_ffn_up[0].rearrange("(c p) n -> p c n", p=P)
    w_d = w_ffn_down[0].rearrange("(c p) n -> p c n", p=P)

    plan = []
    for b in range(IH // 2):
        plan.append(("qi", b, w_in0[:, :, C_QI + b * P:C_QI + (b + 1) * P], 2))
    plan.append(("kv", 0, w_in0[:, :, C_KV:C_KV + 2 * HD], 2))
    for c in range(KA):
        plan.append(("q", c, w_in0[:, :, C_Q + c * P:C_Q + (c + 1) * P], 2))
    def gate_attn(j):
        plan.append(("ga", j, w_in0[:, :, C_GA + j * P:C_GA + (j + 1) * P], 2))

    EARLY_GA = G + 1
    for g in range(G):
        plan.append(("u", g, w_in0[:, :, C_U + g * P:C_U + (g + 1) * P], 2))
        gate_attn(g)
    gate_attn(G)
    for j in range(KD):
        plan.append(("gp", j, w_in0[:, :, C_GP + j * P:C_GP + (j + 1) * P], 2))
        plan.append(("bp", j, w_bp[:, :, j * P:(j + 1) * P], 2))
    for j in range(EARLY_GA, KD):
        gate_attn(j)
    for jj in range(KD // 2):
        plan.append(("ba", jj, w_ba[:, :, jj * 2 * P:(jj + 1) * 2 * P], 2))
    QUARTERS = [(half, j) for half in range(2) for j in range(2)]
    for g, (half, j) in enumerate(QUARTERS):
        for m in range(KD // 2):
            plan.append(("wo", KD // 2 * g + m, w_o[:, 2 * m:2 * m + 2, j * HALF:(j + 1) * HALF], 1))
    at = {(kind, k): n for n, (kind, k, _, _) in enumerate(plan)}
    N_UP = len(plan)
    N_DN = N_UP + 2 * NF
    DR = NF // 2
    N_ALL = N_DN + 2 * DR
    DOWN_TILES = [(t + NT // 2) % NT for t in range(NT)]
    PRODUCTS = [0]
    for n in range(N_ALL):
        PRODUCTS.append(PRODUCTS[-1] + (plan[n][3] if n < N_UP else 1))
    N_QI = PRODUCTS[at["kv", 0]]
    QI_ORDER = [(0, 0), (1, 0), (0, 1), (1, 1), (2, 0), (2, 1), (3, 0), (3, 1)]
    FIRST_SUM = [sum(k + 2 for k in range(g)) + 1 for g in range(G)]
    PRODUCTS[1] = 3

    def product(kind, k, part=0):
        return PRODUCTS[at[kind, k]] + part + 1

    def pooled_in(g):
        return g % 2

    def block(n, i=0, step=0):
        return Block(PRODUCTS, n, i, step)

    ATT = [(t, h) for t in range(NT) for h in range(NH)]
    QH = range(T0, NT)
    IDX = [(t, h) for t in QH for h in range(IH)]
    PIECE = 2
    slots = []
    tied = {}

    def pieces(kind):
        return (KP if kind == "bp" else KD) // PIECE

    for n in range(at["kv", 0], at["ba", 0]):
        kind, k = plan[n][:2]
        per = pieces(kind)
        for q in range(2 * per):
            if kind in ("kv", "q") and q % per == per - 1:
                tied.setdefault(len(slots) + 2, []).append(("turn", kind, k, q // per))
            if kind == "u" and q == 2 * per - 1:
                e = len(slots)
                tied.setdefault(e + 2, []).append(("window", k))
                late = 12 + 2 * k
                tied.setdefault(e + late, []).insert(0, ("pooled", k))
                tied.setdefault(e + late + 2, []).append(("mix", k, 0))
                tied.setdefault(e + late + 4, []).append(("mix", k, 1))
                if k == G - 1:
                    start_att = e + late + 7
            slots.append((n, q, []))
        if kind == "bp":
            pooled_end = len(slots)
    n_stream = len(slots)
    us_pe = us_dve = 0.0
    IDX_PER_SLOT = 2
    K_TURN_0, K_TURN_1, Q_TURN, ATT_AFTER = 8, 11, 14, 18
    AHEAD_ATT, AHEAD_SEARCH = 1, 0
    idx = att = turned = 0
    TOP_BIT = 30
    search = [("sign",)] + [("bit", b, part) for b in range(TOP_BIT, -1, -1) for part in range(2)]
    search += [("select", t, part) for t in QH for part in range(2)]
    found = 0
    s = 0
    while s < n_stream or att < len(ATT) + 3 or turned < NT:
        if s >= n_stream:
            slots.append((None, 0, []))
        side = slots[s][2]
        us_pe += 1.3 if s < n_stream else 0.5
        side.extend(tied.get(s, []))
        for _ in range(IDX_PER_SLOT):
            if idx == len(IDX):
                break
            t, h = IDX[idx]
            side.append(("idx", idx))
            us_pe += 2 * (t + 1) * P / 2400
            us_dve = max(us_dve, us_pe) + (t + 1) * P / 960 + 0.1
            idx += 1
        if s == start_att:
            side += [("knorm",), ("qnorm", 0)]
            us_dve += 3
        if s == start_att + K_TURN_0:
            side += [("kturn", 0), ("qscale", 0)]
        if s == start_att + K_TURN_1:
            side += [("kturn", 1)]
        if s == start_att + Q_TURN:
            side += [("qturn", 0)]
        if s > start_att + ATT_AFTER and att < len(ATT) + 3:
            i = att
            t, h = ATT[i] if i < len(ATT) else (NT, i - len(ATT))
            ready = t < T0 or t == NT or found >= 2 * (TOP_BIT + 1) + 1 + 2 * (t - T0 + 1)
            if ready and (us_dve < us_pe + AHEAD_ATT or s >= n_stream):
                if h == 0 and t < T0:
                    side.append(("dist", t))
                    us_dve += 0.2
                if h == 2 and t:
                    side.append(("attend", t - 1))
                    us_dve += 0.8
                if i < len(ATT) + 2:
                    side.append(("att", i))
                    us_pe += 6 * (t + 1) * P / 2400
                    us_dve = max(us_dve, us_pe - 1) + 1.55 * (t + 1) * P / 960 + 0.4
                if t + 1 < NT:
                    side += {2: [("qnorm", t + 1)], 4: [("qscale", t + 1)], 5: [("qturn", t + 1)]}.get(h, [])
                    us_dve += {2: 0.6, 4: 0.6, 5: 1.3}.get(h, 0)
                att += 1
        if s > pooled_end and turned < NT and att > NH * (turned + 1) + 2:
            side.append(("aturn", turned))
            us_dve += 0.6
            us_pe += 0.4
            turned += 1
        if idx == len(IDX):
            while found < len(search) and us_dve < us_pe + AHEAD_SEARCH:
                side.append(search[found])
                us_dve += (3.5 * (search[found][1] + 1) * P / 960 + 0.3 if search[found][0] == "select" else
                           sum(P * (t + 1) for t in QH) / 1920 + 0.7)
                found += 1
        if s >= n_stream:
            us_pe = max(us_pe, us_dve - 1)
        s += 1

    with ExitStack() as ctx:
        def sem(name):
            return ctx.enter_context(nc.semaphore(name))

        BASE = (nc.sbuf_base + 63) // 64 * 64
        KB = 1024
        A_CONST = BASE
        A_G = A_CONST + 512 + 2 * KB
        A_STAGE = A_G + 4 * KB
        A_R2 = A_STAGE + 24 * KB
        A_R1 = A_R2 + 64 * KB
        A_SC = A_R1 + 40 * KB
        SC_AT = [0] * NT
        n = 0
        for t in range(T0, NT):
            SC_AT[t] = n
            n += (t + 1) * P
        A_R3 = A_SC + 4 * n
        A_WORK = A_R3 + 28 * KB
        A_D01 = A_WORK + 16 * KB
        A_GB = A_D01 + 4 * 3 * P
        A_RANK = A_GB + 8 * KB
        A_SMALL = A_RANK + 2 * KB
        small = [A_SMALL]

        def sb(name, shape, dt, offset):
            return nc.alloc_sbuf_tensor_at(name, shape, dt, offset=offset)

        def tiny(name, n, dt=F32):
            a = sb(name, [P, n], dt, small[0])
            small[0] += (4 * n + 31) // 32 * 32
            return a

        ident = sb("ident", [P, P], F32, A_CONST)
        key_minus_row = sb("key_minus_row", [P, S], F16, A_CONST + 512)
        gain = sb("gain", [P, D], F32, A_G)
        raw = sb("raw", [P, 2, SLOT], F32, A_STAGE)
        w_hi = sb("w_hi", [P, 2, SLOT], F32R, A_STAGE + 8 * KB)
        w_lo = sb("w_lo", [P, 2, SLOT], F32R, A_STAGE + 16 * KB)
        h_hi = sb("h_hi", [P, KD, S], F32R, A_R2)
        h_lo = sb("h_lo", [P, KD, S], F32R, A_R2 + 32 * KB)
        qi = sb("qi", [P, IH, S], F32R, A_R1)
        ki_hi = sb("ki_hi", [P, S], F32R, A_R1 + 32 * KB)
        ki_lo = sb("ki_lo", [P, S], F32R, A_R1 + 36 * KB)
        scores = sb("scores", [P, n], F32, A_SC)
        rank = sb("rank", [P, S], F16, A_RANK)
        reached = sb("reached", [P, 2, S], U8, A_RANK)
        x_in = sb("x_in", [P, 4, D], F32, A_SC)
        xn = sb("xn", [P, 2, D], F32, A_WORK)
        x_sq = sb("x_sq", [P, D], F32, A_WORK + 8 * KB)
        KW = HD + IH
        kw_raw = sb("kw_raw", [P, KD, KW], F32, A_R3)
        kw_hi = sb("kw_hi", [P, KD, KW], F32R, A_R3 + 3 * KB)
        kw_lo = sb("kw_lo", [P, KD, KW], F32R, A_R3 + 6 * KB)
        wi_t = sb("wi_t", [P, S], F32, A_R3 + 20 * KB)
        relu = sb("relu", [P, 3, S], F32, A_WORK)
        u_raw = sb("u_raw", [P, 2, S], F32, A_R1 + 32 * KB)
        PADDED = 4 * (PAD + S)
        u_pad = sb("u_pad", [P, PAD + S], F32, A_WORK)
        win = [sb(f"win{k}", [P, PAD + S], F32, A_WORK + (k + 1) * PADDED) for k in range(2)]
        pt_f = sb("pt_f", [P, HALF], F32, A_WORK + 3 * PADDED)
        pl_hi = sb("pl_hi", [P, S], F32R, A_R3 + 20 * KB)
        pl_lo = sb("pl_lo", [P, S], F32R, A_R3 + 24 * KB)
        pw_raw = sb("pw_raw", [P, G, P], F32, A_R3 + 13 * KB)
        pw_hi = sb("pw_hi", [P, G, P], F32R, A_GB + 4 * KB)
        pw_lo = sb("pw_lo", [P, G, P], F32R, A_GB + 6 * KB)
        pt_hi = sb("pt_hi", [P, KP, S], F32R, A_R1)
        pt_lo = sb("pt_lo", [P, KP, S], F32R, A_R1 + 16 * KB)
        gate = sb("gate", [P, 2, HALF], F32, A_GB)
        bp = sb("bp", [P, 2, HALF], F32, A_GB + 4 * KB)
        nat_t = sb("nat_t", [P, 2, HALF], F32, A_G)
        q_nat = sb("q_nat", [P, NT, AW], F32, A_R3)
        kv_nat = sb("kv_nat", [P, NT, 2 * HD], F32, A_R3 + 16 * KB)
        q_st = sb("q_st", [P, 2, NH, P], F32R, A_R3 + 20 * KB)
        k_sq = sb("k_sq", [P, NT, HD], F32, A_WORK + 12 * KB)
        kn = sb("kn", [P, NT, 2, HD], F32, A_WORK + 8 * KB)
        probs = sb("probs", [P, 2, S], F32, A_WORK)
        probs_t = sb("probs_t", [P, 2, S], F32, A_WORK + 8 * KB)
        dist01 = sb("dist01", [P, 3 * P], F32, A_D01)
        q_sq = sb("q_sq", [P, AW], F32, A_G)
        q_s = sb("q_s", [P, AW], F32, A_G + 2 * KB)
        a_hi = sb("a_hi", [P, KA, S], F32R, A_R1)
        a_lo = sb("a_lo", [P, KA, S], F32R, A_R1 + 16 * KB)
        k_hi = sb("k_hi", [P, S], F32R, A_R1 + 32 * KB)
        k_lo = sb("k_lo", [P, S], F32R, A_R1 + 36 * KB)
        g_attn = sb("g_attn", [P, KD, S], F32, A_R2 + 32 * KB)
        m_pool = sb("m_pool", [P, KD, S], F32, A_R2)
        m_f = sb("m_f", [P, 2, S], F32, A_R1 + 32 * KB)
        m_hi = sb("m_hi", [P, KD, S], F32R, A_SC)
        m_lo = sb("m_lo", [P, KD, S], F32R, A_SC + 32 * KB)
        x2 = sb("x2", [P, NT, D], F32, A_R2)
        xn2 = sb("xn2", [P, 2, D], F32, A_R1 + 24 * KB)
        h2_hi = sb("h2_hi", [P, KD, S], F32R, A_SC)
        h2_lo = sb("h2_lo", [P, KD, S], F32R, A_SC + 32 * KB)
        act_t = sb("act_t", [P, NF, S], F32, A_R2)
        silu = sb("silu", [P, 2, S], F32, A_R2 + 88 * KB)
        x2b = sb("x2b", [P, NT, D], F32, A_SC)
        ac_hi = sb("ac_hi", [P, 2, S], F32R, A_R2 + 96 * KB)
        ac_lo = sb("ac_lo", [P, 2, S], F32R, A_SC + 64 * KB)
        y = sb("y", [P, NT, HALF], F32, A_SC + 48 * KB)

        ssq = tiny("ssq", NT)
        ms = tiny("ms", NT)
        rs = tiny("rs", NT)
        minus_half = tiny("minus_half", NT)
        w_idx = tiny("w_idx", NT * IH)
        edge = tiny("edge", G * PAD)
        counts = tiny("counts", NS)
        above = tiny("above", NS)
        flips = tiny("flips", NS, I32)
        threshold = tiny("threshold", NS, I32)
        bit_value = tiny("bit_value", TOP_BIT + 1, I32)
        kss = tiny("kss", NT)
        krs = tiny("krs", NT)
        qss = tiny("qss", NH)
        qrs = tiny("qrs", NH)
        row_max = tiny("row_max", 2)
        neg_max = tiny("neg_max", 2)
        row_sum = tiny("row_sum", 2 * NH)
        row_inv = tiny("row_inv", NH)
        gq = tiny("gq", 1)
        gk = tiny("gk", 1)
        psc = tiny("psc", G)
        assert small[0] <= nc.sbuf_usable_end, (small[0], nc.sbuf_usable_end)

        ps = ctx.enter_context(nc.psum_tensor("ps", [P, 8, HALF], F32))
        ga_dram = nc.dram_tensor("ga_scratch", [P, KD, S], F32, kind="Internal").ap()
        mp_dram = nc.dram_tensor("mp_scratch", [P, KD, S], F32, kind="Internal").ap()
        x2_dram = nc.dram_tensor("x2_scratch", [P, NT, D], F32, kind="Internal").ap()

        def pair(b):
            return ps[:, b:b + 2, :].rearrange("p b n -> p (b n)")

        raw_landed = [sem("raw_landed0"), sem("raw_landed1")]
        hi_done, lo_done, products = sem("hi_done"), sem("lo_done"), sem("products")
        evac = sem("evac")
        gain_in, consts_in, kw_in, pw_in, cst = sem("gain_in"), sem("consts_in"), sem("kw_in"), sem("pw_in"), sem("cst")
        ident_ready, edge_ready, gq_ready = sem("ident_ready"), sem("edge_ready"), sem("gq_ready")
        x_landed = [sem(f"x_landed{k}") for k in range(4)]
        sq_done, ms_done, rs_done = sem("sq_done"), sem("ms_done"), sem("rs_done")
        xn_done, tr_done, xh_done, xl_done = sem("xn_done"), sem("tr_done"), sem("xh_done"), sem("xl_done")
        kwh_done, kwl_done = sem("kwh_done"), sem("kwl_done")
        ki_done, kih_done, kil_done = sem("ki_done"), sem("kih_done"), sem("kil_done")
        wit_done, wi_turned, widx_done = sem("wit_done"), sem("wi_turned"), sem("widx_done")
        qih_done, qil_done = sem("qih_done"), sem("qil_done")
        is_done, relu_done, acc_done, masked = sem("is_done"), sem("relu_done"), sem("acc_done"), sem("masked")
        bits_ready, counted, flips_done, threshold_done = (sem("bits_ready"), sem("counted"), sem("flips_done"),
                                                           sem("threshold_done"))
        select_step = sem("select_step")
        turned_up, nat_done = sem("turned_up"), sem("nat_done")
        pwh_done, pwl_done, pads = sem("pwh_done"), sem("pwl_done"), sem("pads")
        win_done, plf_done, plh_done, pll_done = sem("win_done"), sem("plf_done"), sem("plh_done"), sem("pll_done")
        u_copied = sem("u_copied")
        pm_done, ptf_done, pth_done, ptl_done = sem("pm_done"), sem("ptf_done"), sem("pth_done"), sem("ptl_done")
        mp_done = sem("mp_done")
        mp_stored = [sem("mp_stored0"), sem("mp_stored1")]
        ga_stored = [sem("ga_stored0"), sem("ga_stored1")]
        ksq_done, kss_done, kms_done, krs_done = sem("ksq_done"), sem("kss_done"), sem("kms_done"), sem("krs_done")
        kn_done, kt_done, kh_done, kl_done = sem("kn_done"), sem("kt_done"), sem("kh_done"), sem("kl_done")
        qsq_done, qss_done, qms_done, qrs_done = sem("qsq_done"), sem("qss_done"), sem("qms_done"), sem("qrs_done")
        qs_done, qt_done, qh_done, ql_done = sem("qs_done"), sem("qt_done"), sem("qh_done"), sem("ql_done")
        pen_done, dist_done, bias_done = sem("pen_done"), sem("dist_done"), sem("bias_done")
        qk_done, lg_done, nm_done, ex_done = sem("qk_done"), sem("lg_done"), sem("nm_done"), sem("ex_done")
        tp_done, pt_done, pv_done = sem("tp_done"), sem("pt_done"), sem("pv_done")
        ri_done, an_done, at_done, ah_done, al_done = (sem("ri_done"), sem("an_done"), sem("at_done"),
                                                       sem("ah_done"), sem("al_done"))
        merge_in = [sem(f"merge_in{j}") for j in range(KD)]
        x_loaded = [sem("x_loaded0"), sem("x_loaded1")]
        gain2_in = sem("gain2_in")
        mg_done, mf_done, mh_done, ml_done = sem("mg_done"), sem("mf_done"), sem("mh_done"), sem("ml_done")
        x2_done, x2_stored, x2_loaded = sem("x2_done"), sem("x2_stored"), sem("x2_loaded")
        sq2_done, ms2_done, rs2_done = sem("sq2_done"), sem("ms2_done"), sem("rs2_done")
        xn2_done, tr2_done, xh2_done, xl2_done = sem("xn2_done"), sem("tr2_done"), sem("xh2_done"), sem("xl2_done")
        silu_done, act_done = sem("silu_done"), sem("act_done")
        ach_done, acl_done, ac_used = sem("ach_done"), sem("acl_done"), sem("ac_used")
        summed, y_done, y_stored = sem("summed"), sem("y_done"), sem("y_stored")

        engines = ctx.enter_context(nc.Block())

        def score_tile(t):
            return scores[:, SC_AT[t]:SC_AT[t] + (t + 1) * P]

        def dist_tile(t):
            return score_tile(t) if t >= T0 else dist01[:, t * P:(2 * t + 1) * P]

        def wait_evac(eng, kind, k, half):
            eng.wait_ge(evac, product(kind, k, half) - N_QI)

        def load(sp, b, src):
            if not b.first:
                sp.wait_ge(hi_done, b.n - 1)
                sp.wait_ge(lo_done, b.n - 1)
            c, n = src.shape[1], src.shape[2]
            dst = raw[:, b.slot, 0:c * n].rearrange("p (c n) -> p c n", c=c)
            sp.dma_start(dst, src).then_inc(raw_landed[b.slot], 16)

        def load_gate_up(sp, i):
            for b in range(2):
                for k, w in enumerate((w_g, w_u)):
                    f = 2 * i + b
                    cols = slice(f * P, (f + 1) * P) if isinstance(f, int) else bass.ds(f * P, P)
                    load(sp, block(N_UP + 2 * b + k, i, 4), w[:, :, cols])

        def multiplied(eng, kind, k, part=0):
            eng.wait_ge(products, product(kind, k, part))

        def turned_x2(t):
            return pair((4 if t < NT // 2 else 0) + 2 * (t % 2))

        def slot_free(eng, m, s):
            if s == 0:
                eng.wait_ge(ac_used, m)
            else:
                eng.wait_ge(products, PRODUCTS[N_DN] + m)

        @engines.sync
        def _(sp):
            for t in range(NT):
                if t >= 4:
                    sp.wait_ge(xn_done, t - 3)
                    sp.wait_ge(sq_done, t - 3)
                sp.dma_start(x_in[:, t % 4, :], x[0, t * P:(t + 1) * P, :]).then_inc(x_landed[t % 4], 16)
                if t == 0:
                    sp.dma_start(gain[:], norm_mix.broadcast_to([P, D])).then_inc(gain_in, 16)
                if t == 3:
                    sp.dma_start(kw_raw[:], w_in0[:, :, C_KI:C_KI + KW]).then_inc(kw_in, 16)
                if t in (4, 5):
                    load(sp, block(t - 4), plan[t - 4][2])
            sp.dma_start(pw_raw[:], w_pool_group[0].rearrange("g c n -> c g n")).then_inc(pw_in, 16)
            for k in range(2):
                sp.dma_start(gq[k * HD:(k + 1) * HD, :], q_norm.rearrange("a d -> d a")).then_inc(consts_in, 16)
                sp.dma_start(gk[k * HD:(k + 1) * HD, :], k_norm.rearrange("a d -> d a")).then_inc(consts_in, 16)
            sp.dma_start(psc[:], pool_scale.rearrange("a (g p) -> p (a g)", p=P),
                         allow_slow_non_contiguous=True).then_inc(consts_in, 16)
            for n in range(2, N_UP):
                if n == at["ba", 2]:
                    sp.wait_ge(products, PRODUCTS[at["ba", 0]])
                    for half in range(2):
                        sp.wait_ge(ga_stored[half], 16 * KD)
                        sp.wait_ge(mp_stored[half], 16 * KD)
                    for j in range(KD):
                        sp.dma_start(g_attn[:, j, :], ga_dram[:, j, :]).then_inc(merge_in[j], 16)
                        sp.dma_start(m_pool[:, j, :], mp_dram[:, j, :]).then_inc(merge_in[j], 16)
                load(sp, block(n), plan[n][2])
            load_gate_up(sp, 0)
            with sp.Fori(1, NF // 2) as i:
                load_gate_up(sp, i)
            for j in range(2):
                cols = slice(j * HALF, (j + 1) * HALF)
                load(sp, block(N_DN + j * DR), w_d[:, 0:2, cols])
                with sp.Fori(0, (DR - 1) // 2) as i:
                    for b in range(2):
                        load(sp, block(N_DN + j * DR + 1 + b, i, 2),
                             w_d[:, bass.ds(2 + 2 * b + 4 * i, 2), cols])
            for j in range(2):
                for k, t in enumerate(DOWN_TILES):
                    sp.wait_ge(y_done, j * NT + k + 1)
                    sp.dma_start(out[0, t * P:(t + 1) * P, j * HALF:(j + 1) * HALF],
                                 y[:, t, :]).then_inc(y_stored, 16)
            sp.wait_ge(y_stored, 16 * 2 * NT)

        @engines.gpsimd
        def _(pool):
            state = {"n": 0}

            def split_lo(b, width=SLOT):
                pool.wait_ge(hi_done, b.n + 1)
                pool.wait_ge(raw_landed[b.slot], 16 * (b.turn + 1))
                if not b.first:
                    pool.wait_ge(products, b.freed)
                pool.tensor_tensor(w_lo[:, b.slot, :width], raw[:, b.slot, :width],
                                   w_hi[:, b.slot, :width].bitcast(F32), ALU.subtract).then_inc(lo_done, 1)

            def lo_until(n):
                while state["n"] < n:
                    k = state["n"]
                    src = plan[k][2] if k < N_UP else None
                    split_lo(block(k), src.shape[1] * src.shape[2] if src is not None else SLOT)
                    state["n"] += 1

            pool.memset(minus_half[:], -0.5).then_inc(cst, 1)
            pool.memset(ident[:], 0.0).then_inc(cst, 1)
            pool.iota(key_minus_row[:], [[1, S]], base=0, channel_multiplier=-1,
                      allow_small_or_imprecise_dtypes=True).then_inc(cst, 1)
            pool.wait_ge(cst, 2)
            pool.affine_select(out=ident[:], in_=ident[:], compare_op=ALU.not_equal, fill=1.0, base=0,
                               pattern=[[-1, P]], channel_multiplier=1).then_inc(ident_ready, 1)

            def rstd(k, n, sums, means, out_, ready, m_done, r_done, count):
                pool.wait_ge(ready, k)
                pool.tensor_scalar(means, sums, 1.0 / count, RMS_EPS, ALU.mult, ALU.add).then_inc(m_done, 1)
                pool.wait_ge(m_done, k)
                pool.tensor_tensor(out_, means, minus_half[:, 0:n], ALU.pow).then_inc(r_done, 1)

            def future(tile, t, fill, signal):
                diag = tile[:, t * P:(t + 1) * P]
                pool.affine_select(out=diag, in_=diag, compare_op=ALU.is_ge, fill=fill, base=0,
                                   pattern=[[-1, P]], channel_multiplier=1).then_inc(signal, 1)

            pool.wait_ge(cst, 3)
            for t in range(NT):
                rstd(t + 1, 1, ssq[:, t:t + 1], ms[:, t:t + 1], rs[:, t:t + 1], sq_done, ms_done, rs_done, D)
                if t == 5:
                    lo_until(1)
                if t == 7:
                    lo_until(2)
            for b in range(TOP_BIT + 1):
                pool.memset(bit_value[:, b:b + 1], 1 << b).then_inc(bits_ready, 1)
            lo_until(at["kv", 0] + 2)
            sums = 0
            for n, q, side in slots:
                if n is not None and q == 0:
                    lo_until(n + 2)
                if n is not None and plan[n][0] == "bp" and q == 2 * pieces("bp") - 1:
                    j = plan[n][1]
                    for half in range(2):
                        wait_evac(pool, "bp", j, half)
                        pool.tensor_tensor(bp[:, half, :], bp[:, half, :], gate[:, half, :],
                                           ALU.mult).then_inc(mp_done, 1)
                for what, *arg in side:
                    if what == "idx" and arg[0] % IH == IH - 1:
                        t = IDX[arg[0]][0]
                        pool.wait_ge(acc_done, arg[0] + 1)
                        future(score_tile(t), t, MASKED, masked)
                    elif what == "window":
                        g = arg[0]
                        w = POOL_WINDOWS[g]
                        if g == 0:
                            pool.wait_ge(acc_done, len(IDX))
                            for buf in (u_pad, win[0], win[1]):
                                pool.memset(buf[:, 0:PAD], 0.0).then_inc(pads, 1)
                            pool.wait_ge(pads, 3)
                            pool.wait_ge(edge_ready, G * PAD)
                        wait_evac(pool, "u", g, 1)
                        if g:
                            pool.wait_ge(pll_done, g)
                            pool.wait_ge(plh_done, g)
                        src, d, k = u_pad, 1, 0
                        while d < w:
                            pool.tensor_tensor(win[k][:, PAD:], src[:, PAD:], src[:, PAD - d:PAD + S - d],
                                               ALU.add).then_inc(win_done, 1)
                            sums += 1
                            pool.wait_ge(win_done, sums)
                            src, d, k = win[k], 2 * d, 1 - k
                        pool.tensor_tensor(src[:, PAD:2 * PAD], src[:, PAD:2 * PAD], edge[:, g * PAD:(g + 1) * PAD],
                                           ALU.mult).then_inc(win_done, 1)
                        sums += 1
                        pool.wait_ge(win_done, sums)
                        pool.wait_ge(u_copied, 2 * (g + 1))
                        pool.tensor_tensor(src[:, PAD:], src[:, PAD:], u_raw[:, g % 2, :],
                                           ALU.subtract).then_inc(plf_done, 1)
                    elif what == "pooled":
                        g = arg[0]
                        pool.wait_ge(plh_done, g + 1)
                        if g:
                            pool.wait_ge(pm_done, 2 * g)
                        pool.tensor_tensor(pl_lo[:], win[pooled_in(g)][:, PAD:], pl_hi[:].bitcast(F32),
                                           ALU.subtract).then_inc(pll_done, 1)
                    elif what == "mix":
                        g, half = arg
                        k = 2 * g + half
                        pool.wait_ge(pth_done, k + 1)
                        pool.wait_ge(ptf_done, k + 1)
                        cols = slice(half * HALF, (half + 1) * HALF)
                        pool.tensor_tensor(pt_lo[:, g, cols], pt_f[:], pt_hi[:, g, cols].bitcast(F32),
                                           ALU.subtract).then_inc(ptl_done, 1)
                    elif what == "knorm":
                        rstd(1, NT, kss[:], kss[:], krs[:], kss_done, kms_done, krs_done, HD)
                    elif what == "qnorm":
                        rstd(arg[0] + 1, NH, qss[:], qss[:], qrs[:], qss_done, qms_done, qrs_done, HD)
                    elif what == "dist" and arg[0] < T0:
                        t = arg[0]
                        pool.wait_ge(dist_done, t + 1)
                        future(dist_tile(t), t, PENALTY, pen_done)
            lo_until(at["ba", 0] + 2)
            for j in range(KD):
                if j % 2:
                    lo_until(at["ba", j // 2] + 3)
                pool.wait_ge(mh_done, j + 1)
                pool.tensor_tensor(m_lo[:, j, :], m_f[:, j % 2, :], m_hi[:, j, :].bitcast(F32),
                                   ALU.subtract).then_inc(ml_done, 1)
            first_wo = at["wo", 0]
            lo_until(first_wo + KD + 2)
            for t in range(NT):
                rstd(t + 1, 1, ssq[:, t:t + 1], ms[:, t:t + 1], rs[:, t:t + 1], sq2_done, ms2_done, rs2_done, D)
                lo_until({2: first_wo + KD + 3, 3: N_UP + 1, 5: N_UP + 2}.get(t, 0))
            with pool.Fori(0, (N_ALL - N_UP - 2) // 2) as i:
                split_lo(block(N_UP + 2, i, 2))
                split_lo(block(N_UP + 3, i, 2))

        @engines.scalar
        def _(act):
            state = {"n": 0}

            def split_hi(b, width=SLOT):
                act.wait_ge(raw_landed[b.slot], 16 * (b.turn + 1))
                if not b.first:
                    act.wait_ge(products, b.freed)
                    act.wait_ge(lo_done, b.n - 1)
                act.activation(w_hi[:, b.slot, :width], raw[:, b.slot, :width], ACT.Copy).then_inc(hi_done, 1)

            def hi_until(n):
                while state["n"] < n:
                    k = state["n"]
                    src = plan[k][2] if k < N_UP else None
                    split_hi(block(k), src.shape[1] * src.shape[2] if src is not None else SLOT)
                    state["n"] += 1

            def indexer_keys(half):
                act.wait_ge(ki_done, half + 1)
                cols = slice(half * HALF, (half + 1) * HALF)
                for o in range(2):
                    act.activation(ki_hi[o * HD:(o + 1) * HD, cols], ps[0:HD, 2 + half, :], ACT.Copy).then_inc(kih_done, 1)
                act.activation(wi_t[HD:KW, cols], ps[HD:KW, 2 + half, :], ACT.Copy, scale=IDX_SCALE).then_inc(wit_done, 1)

            def indexer_queries(u):
                act.wait_ge(products, u + 1)
                b, half = QI_ORDER[u]
                cols = slice(half * HALF, (half + 1) * HALF)
                act.activation(qi[0:HD, 2 * b, cols], ps[0:HD, u % 2, :], ACT.Copy).then_inc(qih_done, 1)
                act.activation(qi[HD:P, 2 * b + 1, cols], ps[HD:P, u % 2, :], ACT.Copy).then_inc(qih_done, 1)

            for t in range(NT + 3):
                if t < NT:
                    act.wait_ge(x_landed[t % 4], 16 * (t // 4 + 1))
                    if t:
                        act.wait_ge(sq_done, t)
                    act.activation(x_sq[:], x_in[:, t % 4, :], ACT.Square,
                                   accum_out=ssq[:, t:t + 1]).then_inc(sq_done, 1)
                if t == 3:
                    act.wait_ge(kw_in, 16)
                    act.activation(kw_hi[:], kw_raw[:], ACT.Copy).then_inc(kwh_done, 1)
                if t >= 3:
                    s = t - 3
                    act.wait_ge(tr_done, s + 1)
                    act.activation(h_hi[:, :, s * P:(s + 1) * P],
                                   pair(4 + 2 * (s % 2)).rearrange("p (c n) -> p c n", c=KD),
                                   ACT.Copy).then_inc(xh_done, 1)
                    if s == 2:
                        hi_until(1)
                    if s == 3:
                        hi_until(2)
                    if s == 5:
                        indexer_keys(0)
                        indexer_queries(0)
            indexer_queries(1)
            indexer_keys(1)
            for u in range(2, N_QI):
                hi_until({2: 2, 3: 3, 4: 4, 5: 4, 6: 5, 7: 5}[u])
                indexer_queries(u)
            hi_until(at["kv", 0] + 2)

            act.wait_ge(pw_in, 16)
            act.activation(pw_hi[:], pw_raw[:], ACT.Copy).then_inc(pwh_done, 1)

            def q_squares(t):
                if t == 0:
                    act.wait_ge(nat_done, 2 * (KA + 1))
                else:
                    act.wait_ge(qss_done, t)
                act.activation(q_sq[:], q_nat[:, t, :], ACT.Square).then_inc(qsq_done, 1)

            def q_hi(t):
                act.wait_ge(qt_done, t + 1)
                if t == 0:
                    act.wait_ge(gq_ready, 1)
                for o in range(2):
                    rows = slice(o * HD, (o + 1) * HD)
                    act.activation(q_st[rows, t % 2, o::2, :], ps[rows, 7, :].rearrange("p (c n) -> p c n", c=NH // 2),
                                   ACT.Copy, scale=gq[rows, :]).then_inc(qh_done, 1)

            def softmax_exp(i):
                t, h = ATT[i]
                W = (t + 1) * P
                act.wait_ge(nm_done, i + 1)
                if h == 0 and t >= 2:
                    act.wait_ge(ri_done, t - 1)
                k = (t % 2) * NH + h
                act.activation(probs[:, i % 2, :W], probs[:, i % 2, :W], ACT.Exp, bias=neg_max[:, i % 2:i % 2 + 1],
                               accum_out=row_sum[:, k:k + 1]).then_inc(ex_done, 1)

            def probs_out(i):
                t, h = ATT[i]
                W = (t + 1) * P
                act.wait_ge(tp_done, i + 1)
                if i >= 2:
                    act.wait_ge(pv_done, i - 1)
                act.activation(probs_t[:, i % 2, :W], pair(4)[:, :W], ACT.Copy).then_inc(pt_done, 1)

            def stream_out(kind, k, half):
                multiplied(act, kind, k, half)
                src = ps[:, half, :]
                cols = slice(half * HALF, (half + 1) * HALF)
                if kind in ("kv", "q"):
                    u = 2 * (k + 1) + half if kind == "q" else half
                    if u >= 2:
                        act.wait_ge(turned_up, u - 1)
                    act.activation(nat_t[:, half, :], src, ACT.Copy).then_inc(evac, 1)
                elif kind == "u":
                    if k == 0 and half == 0:
                        act.wait_ge(acc_done, len(IDX))
                        act.wait_ge(is_done, len(IDX))
                    if k >= 1:
                        act.wait_ge(win_done, FIRST_SUM[k - 1])
                    if k >= 2:
                        act.wait_ge(plf_done, k - 1)
                    act.activation(u_raw[:, k % 2, cols], src, ACT.Copy).then_inc(u_copied, 1)
                    act.activation(u_pad[:, PAD + half * HALF:PAD + (half + 1) * HALF], src, ACT.Copy,
                                   scale=1.0 / POOL_WINDOWS[k]).then_inc(evac, 1)
                elif kind == "gp":
                    if k:
                        act.wait_ge(mp_done, 2 * (k - 1) + half + 1)
                    else:
                        act.wait_ge(ga_stored[half], 16 * EARLY_GA)
                    act.activation(gate[:, half, :], src, ACT.Sigmoid).then_inc(evac, 1)
                elif kind == "bp":
                    if k:
                        act.wait_ge(mp_stored[half], 16 * k)
                    act.activation(bp[:, half, :], src, ACT.Copy).then_inc(evac, 1)
                elif kind == "ga":
                    if k >= EARLY_GA:
                        act.wait_ge(mp_done, 2 * KD - 1 + half)
                    if k:
                        act.wait_ge(ga_stored[half], 16 * k)
                    act.activation(gate[:, half, :], src, ACT.Sigmoid).then_inc(evac, 1)
                    wait_evac(act, "ga", k, half)
                    act.dma_start(ga_dram[:, k, cols], gate[:, half, :]).then_inc(ga_stored[half], 16)

            for n, q, side in slots:
                if n is not None:
                    kind, k = plan[n][:2]
                    if kind == "ga" and q == 0 and k == EARLY_GA:
                        for half in range(2):
                            act.wait_ge(mp_done, 2 * (KD - 1) + half + 1)
                            act.dma_start(mp_dram[:, KD - 1, half * HALF:(half + 1) * HALF],
                                          bp[:, half, :]).then_inc(mp_stored[half], 16)
                    if kind == "gp" and q == 0 and k:
                        for half in range(2):
                            act.wait_ge(mp_done, 2 * (k - 1) + half + 1)
                            act.dma_start(mp_dram[:, k - 1, half * HALF:(half + 1) * HALF],
                                          bp[:, half, :]).then_inc(mp_stored[half], 16)
                    if q == 0:
                        hi_until(n + 2)
                    half, piece = divmod(q, pieces(kind))
                    if piece == pieces(kind) - 1:
                        stream_out(kind, k, half)
                for what, *arg in side:
                    if what == "turn":
                        kind, k, half = arg
                        u = 2 * (k + 1) + half if kind == "q" else half
                        act.wait_ge(turned_up, u + 1)
                        dst = (kv_nat[:, 4 * half:4 * half + 4, :] if kind == "kv" else
                               q_nat[:, 4 * half:4 * half + 4, k * P:(k + 1) * P])
                        act.activation(dst, ps[:, 6, :].rearrange("p (t n) -> p t n", t=4), ACT.Copy).then_inc(nat_done, 1)
                    elif what == "idx":
                        i = arg[0]
                        t, h = IDX[i]
                        W = (t + 1) * P
                        act.wait_ge(is_done, i + 1)
                        if i >= 3:
                            act.wait_ge(acc_done, i - 2)
                        act.activation(relu[:, i % 3, :W], pair(2 + 2 * (i % 2))[:, :W], ACT.Relu).then_inc(relu_done, 1)
                    elif what == "pooled":
                        g = arg[0]
                        act.wait_ge(plf_done, g + 1)
                        if g:
                            act.wait_ge(pm_done, 2 * g)
                        act.activation(pl_hi[:], win[pooled_in(g)][:, PAD:], ACT.Copy).then_inc(plh_done, 1)
                    elif what == "mix":
                        g, half = arg
                        i = 2 * g + half
                        act.wait_ge(pm_done, i + 1)
                        if i:
                            act.wait_ge(ptl_done, i)
                        act.activation(pt_f[:], ps[:, 7, :], ACT.Copy, scale=psc[:, g:g + 1]).then_inc(ptf_done, 1)
                        act.activation(pt_hi[:, g, half * HALF:(half + 1) * HALF], ps[:, 7, :], ACT.Copy,
                                       scale=psc[:, g:g + 1]).then_inc(pth_done, 1)
                    elif what == "knorm":
                        act.wait_ge(nat_done, 2)
                        act.wait_ge(ptl_done, 2 * G)
                        act.wait_ge(pm_done, 2 * G)
                        act.wait_ge(pll_done, G)
                        act.activation(k_sq[:], kv_nat[:, :, 0:HD], ACT.Square).then_inc(ksq_done, 1)
                    elif what == "kturn":
                        half = arg[0]
                        act.wait_ge(kt_done, half + 1)
                        act.activation(k_hi[:, half * HALF:(half + 1) * HALF], ps[:, 7, :], ACT.Copy,
                                       scale=gk[:, 0:1]).then_inc(kh_done, 1)
                    elif what == "qnorm":
                        q_squares(arg[0])
                    elif what == "qturn":
                        q_hi(arg[0])
                    elif what == "att":
                        i = arg[0]
                        if 1 <= i <= len(ATT):
                            probs_out(i - 1)
                        if i < len(ATT):
                            softmax_exp(i)
                    elif what == "aturn":
                        t = arg[0]
                        act.wait_ge(at_done, t + 1)
                        act.activation(a_hi[:, :, t * P:(t + 1) * P], ps[:, 7, :].rearrange("p (c n) -> p c n", c=KA),
                                       ACT.Copy).then_inc(ah_done, 1)
            act.wait_ge(at_done, NT)
            act.dma_start(gain[:], norm_ffn.broadcast_to([P, D])).then_inc(gain2_in, 16)
            hi_until(at["ba", 0] + 2)
            for j in range(KD):
                if j % 2:
                    hi_until(at["ba", j // 2] + 3)
                act.wait_ge(mf_done, j + 1)
                act.activation(m_hi[:, j, :], m_f[:, j % 2, :], ACT.Copy).then_inc(mh_done, 1)
            act.wait_ge(mf_done, KD)
            first_wo = at["wo", 0]
            for half in range(2):
                hi_until(first_wo + (3, 6)[half])
                act.dma_start(x2[:, 4 * half:4 * half + 4, :],
                              x[0, half * HALF:(half + 1) * HALF, :].rearrange("(t p) d -> p t d", p=P)
                              ).then_inc(x_loaded[half], 16)
            hi_until(first_wo + KD + 2)
            for t in [0, 1, 2, 3, None, 4, 5, 6, 7, NT]:
                if t is None:
                    s = 3
                elif t < NT:
                    s = t - 1 if t % 4 else None
                    act.wait_ge(x2_done, 4 + t + 1 if t < 4 else 8 + t + 1)
                    if t >= 2:
                        act.wait_ge(tr2_done, t - 1)
                    act.activation(xn2[:, t % 2, :], x2[:, t, :], ACT.Square,
                                   accum_out=ssq[:, t:t + 1]).then_inc(sq2_done, 1)
                    act.dma_start(x2_dram[:, t, :], x2[:, t, :]).then_inc(x2_stored, 16)
                else:
                    s = NT - 1
                hi_until({2: first_wo + KD + 3, 3: first_wo + KD + 4, None: first_wo + KD + 5}.get(t, 0))
                if s is not None:
                    act.wait_ge(tr2_done, s + 1)
                    act.activation(h2_hi[:, :, s * P:(s + 1) * P],
                                   turned_x2(s).rearrange("p (c n) -> p c n", c=KD),
                                   ACT.Copy).then_inc(xh2_done, 1)
                if t is None:
                    hi_until(N_UP + 2)

            def gate_up(i):
                for b in range(2):
                    split_hi(block(N_UP + 2 + 2 * b, i, 4))
                    act.wait_ge(products, PRODUCTS[N_UP] + 4 * i + 2 * b + 1)
                    if not isinstance(i, int):
                        act.wait_ge(act_done, 2 * i + b - 1)
                    act.activation(silu[:, b, :], pair(4 * (1 - b)), ACT.Silu).then_inc(silu_done, 1)
                    split_hi(block(N_UP + 3 + 2 * b, i, 4))

            def act_hi_split(m, f, s, first=False):
                if not first:
                    slot_free(act, m, s)
                    act.wait_ge(acl_done, 2 * m + s - 1)
                else:
                    act.wait_ge(act_done, 2)
                src = act_t[:, f, :] if isinstance(f, int) else act_t[:, bass.ds(f, 1), :].rearrange("p o n -> p (o n)")
                act.activation(ac_hi[:, s, :], src, ACT.Copy).then_inc(ach_done, 1)

            gate_up(0)
            act_hi_split(0, 0, 0, True)
            act_hi_split(0, 1, 1, True)
            with act.Fori(1, NF // 2) as i:
                gate_up(i)
            act.wait_ge(products, PRODUCTS[N_DN])
            act.wait_ge(x2_stored, 16 * NT)
            act.dma_start(x2b[:], x2_dram).then_inc(x2_loaded, 16)

            def step(m, f, nxt):
                act_hi_split(m, f, 0)
                if nxt is not None:
                    split_hi(nxt)
                act_hi_split(m, f + 1, 1)

            act.wait_ge(act_done, NF)
            for j in range(2):
                base = j * DR
                with act.Fori(0, (DR - 1) // 2 - j) as i:
                    for b in range(2):
                        step(base + 1 + b + 2 * i, 2 + 2 * b + 4 * i, block(N_DN + base + 2 + b, i, 2))
                if j == 0:
                    step(DR, 0, block(N_DN + DR + 1))
            step(2 * DR - 2, NF - 4, block(N_ALL - 1))
            step(2 * DR - 1, NF - 2, None)

        @engines.tensor
        def _(pe):
            def three(dst, s_hi, s_lo, m_hi_, m_lo_, first, last):
                nc.tensor.matmul(dst, s_hi, m_hi_, start=first, stop=False)
                nc.tensor.matmul(dst, s_hi, m_lo_, start=False, stop=False)
                return nc.tensor.matmul(dst, s_lo, m_hi_, start=False, stop=last)

            def ready(b):
                pe.wait_ge(hi_done, b.n + 1)
                pe.wait_ge(lo_done, b.n + 1)

            def views(b, chunks):
                return (w_hi[:, b.slot, :].rearrange("p (c n) -> p c n", c=chunks),
                        w_lo[:, b.slot, :].rearrange("p (c n) -> p c n", c=chunks))

            def by_half(b, half, bank, hi, lo, chunks=None, width=KD):
                wh, wl = (a[:, b.slot, 0:width * P].rearrange("p (c n) -> p c n", c=width) for a in (w_hi, w_lo))
                cols = slice(half * HALF, (half + 1) * HALF)
                for c in chunks if chunks is not None else range(width):
                    last = three(ps[:, bank, :], wh[:, c, :], wl[:, c, :], hi[:, c, cols], lo[:, c, cols],
                                 c == 0, c == width - 1)
                return last

            def by_column(b, bank, hi, lo):
                for half in range(2):
                    last = by_half(b, half, bank + half, hi, lo)
                return last

            def by_branch(b, bank, k, hi, lo):
                wh, wl = views(b, KA)
                for half in range(2):
                    cols = slice(half * HALF, (half + 1) * HALF)
                    for c in range(KA):
                        last = three(ps[:, bank + half, :], wh[:, c, k * P:(k + 1) * P], wl[:, c, k * P:(k + 1) * P],
                                     hi[:, c, cols], lo[:, c, cols], c == 0, c == KA - 1)
                return last

            def turn(t, src, bank):
                for c in range(KD):
                    last = nc.tensor.transpose(pair(bank)[:, c * P:(c + 1) * P], src[:, c * P:(c + 1) * P], ident[:])
                return last

            def turn_x(t):
                pe.wait_ge(xn_done, t + 1)
                if t >= 2:
                    pe.wait_ge(xl_done, t - 1)
                turn(t, xn[:, t % 2, :], 4 + 2 * (t % 2)).then_inc(tr_done, 1)

            def normed(half):
                pe.wait_ge(xh_done, NT // 2 * (half + 1))
                pe.wait_ge(xl_done, NT // 2 * (half + 1))

            def keys_and_weights(half):
                normed(half)
                pe.wait_ge(kwl_done, 1)
                cols = slice(half * HALF, (half + 1) * HALF)
                for c in range(KD):
                    last = three(ps[0:KW, 2 + half, :], kw_hi[:, c, :], kw_lo[:, c, :], h_hi[:, c, cols],
                                 h_lo[:, c, cols], c == 0, c == KD - 1)
                last.then_inc(ki_done, 1)

            def queries(u):
                b, half = QI_ORDER[u]
                normed(half)
                ready(block(at["qi", b]))
                if u >= 2:
                    pe.wait_ge(qil_done, 2 * (u - 1))
                by_half(block(at["qi", b]), half, u % 2, h_hi, h_lo).then_inc(products, 1)

            pe.wait_ge(ident_ready, 1)
            for t in range(4):
                turn_x(t)
            keys_and_weights(0)
            queries(0)
            turn_x(4)
            turn_x(5)
            queries(1)
            turn_x(6)
            turn_x(7)
            keys_and_weights(1)
            queries(2)
            queries(3)
            pe.wait_ge(wit_done, 2)
            for t in range(NT):
                last = nc.tensor.transpose(ps[:, 6, t * IH:(t + 1) * IH], wi_t[HD:KW, t * P:(t + 1) * P],
                                           ident[HD:KW, HD:KW])
            last.then_inc(wi_turned, 1)
            for u in range(4, N_QI):
                queries(u)

            def bank_7(*readers):
                for signal, count in seven["readers"]:
                    pe.wait_ge(signal, count)
                seven["readers"] = readers

            seven = {"readers": ()}

            def qk(i):
                t, h = ATT[i]
                W = (t + 1) * P
                if i == 0:
                    pe.wait_ge(relu_done, len(IDX))
                    pe.wait_ge(kh_done, 2)
                    pe.wait_ge(kl_done, 2)
                if h == 0:
                    pe.wait_ge(qh_done, 2 * (t + 1))
                    pe.wait_ge(ql_done, 2 * (t + 1))
                if i:
                    pe.wait_ge(lg_done, i)
                for s0 in range(0, W, HALF):
                    w = min(HALF, W - s0)
                    dst = pair(2)[:, s0:s0 + w]
                    q = q_st[:, t % 2, h, :]
                    nc.tensor.matmul(dst, q, k_hi[:, s0:s0 + w], start=True, stop=False)
                    last = nc.tensor.matmul(dst, q, k_lo[:, s0:s0 + w], start=False, stop=True)
                last.then_inc(qk_done, 1)

            def turn_probs(i):
                t, h = ATT[i]
                pe.wait_ge(ex_done, i + 1)
                if i:
                    pe.wait_ge(pt_done, i)
                for k in range(t + 1):
                    last = nc.tensor.transpose(pair(4)[:, k * P:(k + 1) * P], probs[:, i % 2, k * P:(k + 1) * P],
                                               ident[:])
                last.then_inc(tp_done, 1)

            def pv(i):
                t, h = ATT[i]
                pe.wait_ge(pt_done, i + 1)
                if i == 0:
                    pe.wait_ge(nat_done, 2 * (KA + 1))
                elif h == 0:
                    pe.wait_ge(an_done, t)
                for k in range(t + 1):
                    last = nc.tensor.matmul(ps[:, 6, h * HD:(h + 1) * HD], probs_t[:, i % 2, k * P:(k + 1) * P],
                                            kv_nat[:, k, HD:2 * HD], start=(k == 0), stop=(k == t))
                last.then_inc(pv_done, 1)

            unit = 0
            for n, q, side in slots:
                if n is not None:
                    kind, k = plan[n][:2]
                    half, piece = divmod(q, pieces(kind))
                    begins, ends = piece == 0, piece == pieces(kind) - 1
                    if q == 0:
                        ready(block(n))
                    if kind == "bp" and k == 0 and q == 0:
                        pe.wait_ge(pth_done, 2 * G)
                        pe.wait_ge(ptl_done, 2 * G)
                    if begins:
                        if unit < 2:
                            pe.wait_ge(qil_done, 2 * (N_QI - 1 + unit))
                        else:
                            pe.wait_ge(evac, unit - 1)
                        unit += 1
                    hi, lo, width = (pt_hi, pt_lo, KP) if kind == "bp" else (h_hi, h_lo, KD)
                    last = by_half(block(n), half, half, hi, lo, range(PIECE * piece, PIECE * (piece + 1)), width)
                    if ends:
                        last.then_inc(products, 1)
                for what, *arg in side:
                    if what == "turn":
                        kind, k, half = arg
                        u = 2 * (k + 1) + half if kind == "q" else half
                        wait_evac(pe, kind, k, half)
                        if u:
                            pe.wait_ge(nat_done, u)
                        else:
                            pe.wait_ge(widx_done, 1)
                        for c in range(4):
                            last = nc.tensor.transpose(ps[:, 6, c * P:(c + 1) * P], nat_t[:, half, c * P:(c + 1) * P],
                                                       ident[:])
                        last.then_inc(turned_up, 1)
                    elif what == "idx":
                        i = arg[0]
                        t, h = IDX[i]
                        if i == 0:
                            pe.wait_ge(qil_done, 2 * N_QI)
                            pe.wait_ge(kil_done, 4)
                            pe.wait_ge(wit_done, 2)
                        if i >= 2:
                            pe.wait_ge(relu_done, i - 1)
                        W = (t + 1) * P
                        for s0 in range(0, W, HALF):
                            w = min(HALF, W - s0)
                            dst = pair(2 + 2 * (i % 2))[:, s0:s0 + w]
                            q_i = qi[:, h, t * P:(t + 1) * P]
                            nc.tensor.matmul(dst, q_i, ki_hi[:, s0:s0 + w], start=True, stop=False)
                            last = nc.tensor.matmul(dst, q_i, ki_lo[:, s0:s0 + w], start=False, stop=True)
                        last.then_inc(is_done, 1)
                    elif what == "mix":
                        g, half = arg
                        pe.wait_ge(plh_done, g + 1)
                        pe.wait_ge(pll_done, g + 1)
                        if g == 0:
                            pe.wait_ge(pwh_done, 1)
                            pe.wait_ge(pwl_done, 1)
                        bank_7((ptf_done, 2 * g + half + 1), (pth_done, 2 * g + half + 1))
                        cols = slice(half * HALF, (half + 1) * HALF)
                        three(ps[:, 7, :], pw_hi[:, g, :], pw_lo[:, g, :], pl_hi[:, cols], pl_lo[:, cols],
                              True, True).then_inc(pm_done, 1)
                    elif what == "kturn":
                        half = arg[0]
                        pe.wait_ge(kn_done, 2)
                        bank_7((kh_done, half + 1), (kl_done, half + 1))
                        for c in range(4):
                            last = nc.tensor.transpose(ps[:, 7, c * P:(c + 1) * P],
                                                       kn[:, 4 * half + c, :, :].rearrange("p a d -> p (a d)"), ident[:])
                        last.then_inc(kt_done, 1)
                    elif what == "qturn":
                        t = arg[0]
                        pe.wait_ge(qs_done, t + 1)
                        bank_7((qh_done, 2 * (t + 1)), (ql_done, 2 * (t + 1)))
                        for c in range(KA):
                            last = nc.tensor.transpose(ps[:, 7, c * P:(c + 1) * P], q_s[:, c * P:(c + 1) * P], ident[:])
                        last.then_inc(qt_done, 1)
                    elif what == "att":
                        i = arg[0]
                        if i < len(ATT):
                            qk(i)
                        if 1 <= i <= len(ATT):
                            turn_probs(i - 1)
                        if i >= 2:
                            pv(i - 2)
                    elif what == "aturn":
                        t = arg[0]
                        pe.wait_ge(an_done, t + 1)
                        bank_7((ah_done, t + 1), (al_done, t + 1))
                        for c in range(KA):
                            last = nc.tensor.transpose(ps[:, 7, c * P:(c + 1) * P], q_nat[:, t, c * P:(c + 1) * P],
                                                       ident[:])
                        last.then_inc(at_done, 1)
            pe.wait_ge(evac, PRODUCTS[at["ba", 0]] - N_QI)
            pe.wait_ge(al_done, NT)
            pe.wait_ge(ah_done, NT)
            for j in range(KD):
                b = block(at["ba", j // 2])
                ready(b)
                if j >= 4:
                    pe.wait_ge(mg_done, j - 3)
                by_branch(b, 2 * (j % 4), j % 2, a_hi, a_lo).then_inc(products, 1)

            def turn_x2(t, bank):
                pe.wait_ge(xn2_done, t + 1)
                if t % 4 >= 2:
                    pe.wait_ge(xl2_done, t - 1)
                turn(t, xn2[:, t % 2, :], bank).then_inc(tr2_done, 1)

            pe.wait_ge(mg_done, 6)
            for g, (half, j) in enumerate(QUARTERS):
                for m in range(KD // 2):
                    b = block(at["wo", KD // 2 * g + m])
                    ready(b)
                    if g == 0:
                        pe.wait_ge(mh_done, 2 * m + 2)
                        pe.wait_ge(ml_done, 2 * m + 2)
                    if g == 1 and m == 0:
                        pe.wait_ge(mg_done, KD)
                    if g == 3 and m == 0:
                        pe.wait_ge(xl2_done, NT // 2)
                    wh, wl = views(b, 2)
                    for k in range(4):
                        if g >= 2 and m == 0:
                            pe.wait_ge(x2_done, 4 * (g - 2) + k + 1)
                        rows = slice((4 * half + k) * P, (4 * half + k + 1) * P)
                        for c in range(2):
                            last = three(ps[:, 4 * j + k, :], m_hi[:, 2 * m + c, rows], m_lo[:, 2 * m + c, rows],
                                         wh[:, c, :], wl[:, c, :], m == 0 and c == 0, m == KD // 2 - 1 and c == 1)
                    last.then_inc(products, 1)
                    if g == 2:
                        turn_x2(m, 4 + 2 * (m % 2))
            pe.wait_ge(xh2_done, NT // 2)
            for k in range(2):
                ready(block(N_UP + k))
                pe.wait_ge(x2_done, 4 * 3 + 2 * k + 1)
                by_half(block(N_UP + k), 0, 4 + 2 * k, h2_hi, h2_lo)
                pe.wait_ge(x2_done, 4 * 3)
                for t in (4 + 2 * k, 5 + 2 * k):
                    turn_x2(t, 2 * (t % 2))
            pe.wait_ge(xh2_done, NT)
            pe.wait_ge(xl2_done, NT)
            pe.wait_ge(x2_done, 4 * 4)
            for k in range(2):
                by_half(block(N_UP + k), 1, 5 + 2 * k, h2_hi, h2_lo).then_inc(products, 1)

            def gate_up(i, b):
                if not isinstance(i, int):
                    pe.wait_ge(act_done, 2 * i + b - 1)
                for k in range(2):
                    blk = block(N_UP + 2 * b + k, i, 4)
                    ready(blk)
                    by_column(blk, 4 * (1 - b) + 2 * k, h2_hi, h2_lo).then_inc(products, 1)

            gate_up(0, 1)
            with pe.Fori(1, NF // 2) as i:
                gate_up(i, 0)
                gate_up(i, 1)

            def down(blk, c0, j, first, last_block):
                ready(blk)
                wh, wl = views(blk, 2)
                for c in range(2):
                    pe.wait_ge(ach_done, c0 + c + 1)
                    pe.wait_ge(acl_done, c0 + c + 1)
                    for k, t in enumerate(DOWN_TILES):
                        if first and c == 0:
                            if j:
                                pe.wait_ge(y_done, k + 1)
                            elif k % 4 == 0:
                                pe.wait_ge(act_done, NF - 1 + k // 4)
                        rows = slice(t * P, (t + 1) * P)
                        last = three(ps[:, t, :], ac_hi[:, c, rows], ac_lo[:, c, rows], wh[:, c, :], wl[:, c, :],
                                     first and c == 0, last_block and c == 1)
                        if last_block and c == 1 and k < NT - 1:
                            last.then_inc(summed, 1)
                    last.then_inc(products if c else ac_used, 1)

            for j in range(2):
                base = j * DR
                down(block(N_DN + base), 2 * base, j, True, False)
                with pe.Fori(0, (DR - 1) // 2 - 1) as i:
                    for b in range(2):
                        down(block(N_DN + base + 1 + b, i, 2), 2 * base + 2 + 2 * b + 4 * i, j, False, False)
                down(block(N_DN + base + DR - 2), 2 * (base + DR - 2), j, False, False)
                down(block(N_DN + base + DR - 1), 2 * (base + DR - 1), j, False, True)

        @engines.vector
        def _(dve):
            def minus(dst, a, b):
                return nc.vector.tensor_tensor(dst, a, b, ALU.subtract)

            for g, w in enumerate(POOL_WINDOWS):
                for k in range(PAD):
                    nc.vector.memset(edge[:, g * PAD + k:g * PAD + k + 1],
                                     float(w) / min(k + 1, w)).then_inc(edge_ready, 1)
            def indexer_keys(half):
                cols = slice(half * HALF, (half + 1) * HALF)
                dve.wait_ge(kih_done, 2 * half + 2)
                dve.wait_ge(wit_done, half + 1)
                for o in range(2):
                    minus(ki_lo[o * HD:(o + 1) * HD, cols], ps[0:HD, 2 + half, :],
                          ki_hi[0:HD, cols].bitcast(F32)).then_inc(kil_done, 1)

            def indexer_queries(u):
                b, half = QI_ORDER[u]
                cols = slice(half * HALF, (half + 1) * HALF)
                dve.wait_ge(qih_done, 2 * u + 1)
                minus(qi[HD:P, 2 * b, cols], ps[0:HD, u % 2, :], qi[0:HD, 2 * b, cols].bitcast(F32)).then_inc(qil_done, 1)
                dve.wait_ge(qih_done, 2 * u + 2)
                minus(qi[0:HD, 2 * b + 1, cols], ps[HD:P, u % 2, :],
                      qi[HD:P, 2 * b + 1, cols].bitcast(F32)).then_inc(qil_done, 1)

            dve.wait_ge(gain_in, 16)
            for t in range(NT + 1):
                if t < NT:
                    dve.wait_ge(rs_done, t + 1)
                    dve.wait_ge(x_landed[t % 4], 16 * (t // 4 + 1))
                    if t >= 2:
                        dve.wait_ge(tr_done, t - 1)
                    nc.vector.scalar_tensor_tensor(xn[:, t % 2, :], x_in[:, t % 4, :], rs[:, t:t + 1], gain[:],
                                                   ALU.mult, ALU.mult).then_inc(xn_done, 1)
                if t == 2:
                    dve.wait_ge(kw_in, 16)
                    dve.wait_ge(kwh_done, 1)
                    minus(kw_lo[:], kw_raw[:], kw_hi[:].bitcast(F32)).then_inc(kwl_done, 1)
                if t >= 1:
                    s = t - 1
                    dve.wait_ge(xh_done, s + 1)
                    tile = slice(s * P, (s + 1) * P)
                    minus(h_lo[:, :, tile], pair(4 + 2 * (s % 2)).rearrange("p (c n) -> p c n", c=KD),
                          h_hi[:, :, tile].bitcast(F32)).then_inc(xl_done, 1)
                if t == 6:
                    indexer_keys(0)
                    indexer_queries(0)
            indexer_queries(1)
            indexer_keys(1)
            indexer_queries(2)
            indexer_queries(3)
            dve.wait_ge(wi_turned, 1)
            nc.vector.tensor_scalar(w_idx[:], ps[:, 6, 0:NT * IH], 1.0, None, ALU.mult).then_inc(widx_done, 1)
            dve.wait_ge(consts_in, 16 * 5)
            nc.vector.tensor_scalar(gq[:], gq[:], HD ** -0.5, None, ALU.mult).then_inc(gq_ready, 1)
            for u in range(4, N_QI):
                indexer_queries(u)
            dve.wait_ge(pw_in, 16)
            dve.wait_ge(pwh_done, 1)
            minus(pw_lo[:], pw_raw[:], pw_hi[:].bitcast(F32)).then_inc(pwl_done, 1)
            dve.wait_ge(widx_done, 1)

            def score_sum(i):
                t, h = IDX[i]
                dve.wait_ge(relu_done, i + 1)
                w = w_idx[:, t * IH + h:t * IH + h + 1]
                s = score_tile(t)
                r = relu[:, i % 3, :(t + 1) * P]
                if h == 0:
                    nc.vector.tensor_scalar(s, r, w, None, ALU.mult).then_inc(acc_done, 1)
                else:
                    dve.wait_ge(acc_done, i)
                    nc.vector.scalar_tensor_tensor(s, r, w, s, ALU.mult, ALU.add).then_inc(acc_done, 1)

            def count_reached(i, k, value, compare, into):
                if i >= 2:
                    dve.wait_ge(counted, i - 1)
                nc.vector.tensor_scalar(reached[:, i % 2, :(T0 + k + 1) * P], score_tile(T0 + k), value, 0.0,
                                        compare, ALU.add, accum_out=into[:, k:k + 1]).then_inc(counted, 1)

            def search_sign():
                dve.wait_ge(masked, NS)
                for k in range(NS):
                    count_reached(k, k, 0.0, ALU.is_ge, counts)
                dve.wait_ge(counted, NS)
                dve.wait_ge(bits_ready, TOP_BIT + 1)
                nc.vector.tensor_scalar(flips[:], counts[:], float(KEEP), -1.0, ALU.is_lt,
                                        ALU.mult).then_inc(flips_done, 1)
                dve.wait_ge(flips_done, 1)
                nc.vector.tensor_tensor(threshold[:], flips[:], bit_value[:, TOP_BIT:].broadcast_to([P, NS]),
                                        ALU.bitwise_xor).then_inc(threshold_done, 1)

            def search_bit(b, part):
                done = TOP_BIT - b + 1
                dve.wait_ge(threshold_done, done)
                for k in (range(NS - 2), range(NS - 2, NS))[part]:
                    count_reached(NS * done + k, k, threshold[:, k:k + 1].bitcast(F32), ALU.is_ge, counts)
                if part == 0:
                    return
                dve.wait_ge(counted, NS * (done + 1))
                nc.vector.tensor_scalar(flips[:], counts[:], float(KEEP), float(1 << b), ALU.is_lt,
                                        ALU.mult).then_inc(flips_done, 1)
                dve.wait_ge(flips_done, done + 1)
                if b:
                    nc.vector.scalar_tensor_tensor(threshold[:], flips[:], bit_value[:, b - 1:b], threshold[:],
                                                   ALU.bitwise_xor, ALU.bitwise_xor).then_inc(threshold_done, 1)
                else:
                    nc.vector.tensor_tensor(threshold[:], flips[:], threshold[:],
                                            ALU.bitwise_xor).then_inc(threshold_done, 1)

            def select(t, part):
                k = t - T0
                s = score_tile(t)
                r = rank[:, :(t + 1) * P]
                v = threshold[:, k:k + 1].bitcast(F32)
                step = 7 * k
                if part == 1:
                    dve.wait_ge(select_step, step + 3)
                    nc.vector.tensor_scalar(r, r, above[:, k:k + 1], None, ALU.is_le).then_inc(select_step, 1)
                    dve.wait_ge(select_step, step + 4)
                    nc.vector.scalar_tensor_tensor(r, s, v, r, ALU.is_equal, ALU.mult).then_inc(select_step, 1)
                    dve.wait_ge(select_step, step + 5)
                    nc.vector.scalar_tensor_tensor(s, s, v, r, ALU.is_le, ALU.subtract).then_inc(select_step, 1)
                    dve.wait_ge(select_step, step + 6)
                    nc.vector.scalar_tensor_tensor(s, s, PENALTY, key_minus_row[:, :(t + 1) * P], ALU.mult,
                                                   ALU.add).then_inc(select_step, 1)
                    return
                dve.wait_ge(threshold_done, TOP_BIT + 2)
                if k:
                    dve.wait_ge(select_step, step)
                count_reached(NS * (TOP_BIT + 2) + k, k, v, ALU.is_gt, above)
                dve.wait_ge(counted, NS * (TOP_BIT + 2) + k + 1)
                nc.vector.tensor_scalar(above[:, k:k + 1], above[:, k:k + 1], -1.0, float(KEEP), ALU.mult,
                                        ALU.add).then_inc(select_step, 1)
                nc.vector.tensor_scalar(r, s, v, None, ALU.is_equal).then_inc(select_step, 1)
                dve.wait_ge(select_step, step + 2)
                nc.vector.tensor_tensor_scan(r, r, r, 0.0, ALU.add, ALU.max).then_inc(select_step, 1)

            def distances(t):
                nc.vector.tensor_scalar(dist_tile(t), key_minus_row[:, :(t + 1) * P], 1.0, None,
                                        ALU.mult).then_inc(dist_done, 1)

            def logits(i):
                t, h = ATT[i]
                W = (t + 1) * P
                row = probs[:, i % 2, :W]
                if i == 0:
                    dve.wait_ge(pm_done, 2 * G)
                    dve.wait_ge(ptl_done, 2 * G)
                if h == 0 and t < T0:
                    dve.wait_ge(pen_done, t + 1)
                elif h == 0:
                    dve.wait_ge(select_step, 7 * (t - T0 + 1))
                if i >= 2:
                    dve.wait_ge(tp_done, i - 1)
                nc.vector.tensor_scalar(row, dist_tile(t), float(-t * P), SLOPES[h], ALU.add, ALU.mult).then_inc(bias_done, 1)
                dve.wait_ge(bias_done, i + 1)
                dve.wait_ge(qk_done, i + 1)
                nc.vector.tensor_tensor_reduce(row, pair(2)[:, :W], row, 1.0, MASKED, ALU.add, ALU.max,
                                               row_max[:, i % 2:i % 2 + 1]).then_inc(lg_done, 1)
                dve.wait_ge(lg_done, i + 1)
                if i >= 2:
                    dve.wait_ge(ex_done, i - 1)
                nc.vector.tensor_scalar(neg_max[:, i % 2:i % 2 + 1], row_max[:, i % 2:i % 2 + 1], -1.0, None,
                                        ALU.mult).then_inc(nm_done, 1)

            for n, q, side in slots:
                for what, *arg in side:
                    if what == "idx":
                        score_sum(arg[0])
                    elif what == "sign":
                        search_sign()
                    elif what == "bit":
                        search_bit(*arg)
                    elif what == "select":
                        select(*arg)
                    elif what == "knorm":
                        dve.wait_ge(ksq_done, 1)
                        nc.vector.tensor_reduce(kss[:], k_sq[:], AX.X, ALU.add).then_inc(kss_done, 1)
                        dve.wait_ge(krs_done, 1)
                        for o in range(2):
                            nc.vector.tensor_tensor(kn[:, :, o, :], kv_nat[:, :, 0:HD],
                                                    krs[:].unsqueeze(2).broadcast_to([P, NT, HD]),
                                                    ALU.mult).then_inc(kn_done, 1)
                    elif what == "kturn":
                        half = arg[0]
                        cols = slice(half * HALF, (half + 1) * HALF)
                        dve.wait_ge(kh_done, half + 1)
                        nc.vector.scalar_tensor_tensor(k_lo[:, cols], ps[:, 7, :], gk[:, 0:1], k_hi[:, cols].bitcast(F32),
                                                       ALU.mult, ALU.subtract).then_inc(kl_done, 1)
                    elif what == "qnorm":
                        t = arg[0]
                        dve.wait_ge(qsq_done, t + 1)
                        if t:
                            dve.wait_ge(qrs_done, t)
                        nc.vector.tensor_reduce(qss[:], q_sq[:].rearrange("p (h d) -> p h d", h=NH), AX.X,
                                                ALU.add).then_inc(qss_done, 1)
                    elif what == "qscale":
                        t = arg[0]
                        dve.wait_ge(qrs_done, t + 1)
                        if t:
                            dve.wait_ge(qt_done, t)
                        nc.vector.tensor_tensor(q_s[:].rearrange("p (h d) -> p h d", h=NH),
                                                q_nat[:, t, :].rearrange("p (h d) -> p h d", h=NH),
                                                qrs[:].unsqueeze(2).broadcast_to([P, NH, HD]),
                                                ALU.mult).then_inc(qs_done, 1)
                    elif what == "qturn":
                        t = arg[0]
                        for o in range(2):
                            dve.wait_ge(qh_done, 2 * t + o + 1)
                            rows, other = slice(o * HD, (o + 1) * HD), slice((1 - o) * HD, (2 - o) * HD)
                            nc.vector.scalar_tensor_tensor(q_st[other, t % 2, o::2, :],
                                                           ps[rows, 7, :].rearrange("p (c n) -> p c n", c=NH // 2),
                                                           gq[rows, :], q_st[rows, t % 2, o::2, :].bitcast(F32),
                                                           ALU.mult, ALU.subtract).then_inc(ql_done, 1)
                    elif what == "dist":
                        distances(arg[0])
                    elif what == "att" and arg[0] < len(ATT):
                        logits(arg[0])
                    elif what == "attend":
                        t = arg[0]
                        dve.wait_ge(ex_done, NH * (t + 1))
                        nc.vector.reciprocal(row_inv[:], row_sum[:, (t % 2) * NH:(t % 2 + 1) * NH]).then_inc(ri_done, 1)
                        dve.wait_ge(ri_done, t + 1)
                        dve.wait_ge(pv_done, NH * (t + 1))
                        nc.vector.tensor_tensor(q_nat[:, t, :].rearrange("p (h d) -> p h d", h=NH),
                                                ps[:, 6, :].rearrange("p (h d) -> p h d", h=NH),
                                                row_inv[:].unsqueeze(2).broadcast_to([P, NH, HD]),
                                                ALU.mult).then_inc(an_done, 1)
                    elif what == "aturn":
                        t = arg[0]
                        dve.wait_ge(ah_done, t + 1)
                        tile = slice(t * P, (t + 1) * P)
                        minus(a_lo[:, :, tile], ps[:, 7, :].rearrange("p (c n) -> p c n", c=KA),
                              a_hi[:, :, tile].bitcast(F32)).then_inc(al_done, 1)
            for j in range(KD):
                multiplied(dve, "ba", j // 2, j % 2)
                dve.wait_ge(merge_in[j], 32)
                if j >= 2:
                    dve.wait_ge(ml_done, j - 1)
                nc.vector.tensor_tensor(m_f[:, j % 2, :], pair(2 * (j % 4)), g_attn[:, j, :], ALU.mult).then_inc(mg_done, 1)
                dve.wait_ge(mg_done, j + 1)
                nc.vector.tensor_tensor(m_f[:, j % 2, :], m_f[:, j % 2, :], m_pool[:, j, :], ALU.add).then_inc(mf_done, 1)
            dve.wait_ge(x_loaded[0], 16)

            def x_plus(g):
                half, j = QUARTERS[g]
                multiplied(dve, "wo", KD // 2 * (g + 1) - 1)
                dve.wait_ge(x_loaded[half], 16)
                for k in range(4):
                    cols = slice(j * HALF, (j + 1) * HALF)
                    nc.vector.tensor_tensor(x2[:, 4 * half + k, cols], ps[:, 4 * j + k, :], x2[:, 4 * half + k, cols],
                                            ALU.add).then_inc(x2_done, 1)

            def norm_half(half):
                dve.wait_ge(x2_done, 4 * 2 * (half + 1))
                for t in range(4 * half, 4 * half + 5):
                    if t < 4 * half + 4:
                        dve.wait_ge(rs2_done, t + 1)
                        if t >= 2:
                            dve.wait_ge(tr2_done, t - 1)
                        nc.vector.scalar_tensor_tensor(xn2[:, t % 2, :], x2[:, t, :], rs[:, t:t + 1], gain[:],
                                                       ALU.mult, ALU.mult).then_inc(xn2_done, 1)
                    if t > 4 * half:
                        s = t - 1
                        dve.wait_ge(xh2_done, s + 1)
                        tile = slice(s * P, (s + 1) * P)
                        minus(h2_lo[:, :, tile], turned_x2(s).rearrange("p (c n) -> p c n", c=KD),
                              h2_hi[:, :, tile].bitcast(F32)).then_inc(xl2_done, 1)

            x_plus(0)
            x_plus(1)
            dve.wait_ge(gain2_in, 16)
            norm_half(0)
            x_plus(2)
            x_plus(3)
            norm_half(1)
            dve.wait_ge(x2_stored, 16 * NT)
            dve.wait_ge(tr2_done, NT)

            def gate_up(i):
                for b in range(2):
                    f = 2 * i + b
                    dve.wait_ge(silu_done, f + 1)
                    dve.wait_ge(products, PRODUCTS[N_UP] + 4 * i + 2 * b + 2)
                    dst = act_t[:, f, :] if isinstance(f, int) else act_t[:, bass.ds(f, 1), :].rearrange("p o n -> p (o n)")
                    nc.vector.tensor_tensor(dst, pair(4 * (1 - b) + 2), silu[:, b, :], ALU.mult).then_inc(act_done, 1)

            def act_lo(m, f, s, first=False):
                dve.wait_ge(ach_done, 2 * m + s + 1)
                if not first:
                    slot_free(dve, m, s)
                src = act_t[:, f, :] if isinstance(f, int) else act_t[:, bass.ds(f, 1), :].rearrange("p o n -> p (o n)")
                minus(ac_lo[:, s, :], src, ac_hi[:, s, :].bitcast(F32)).then_inc(acl_done, 1)

            gate_up(0)
            dve.wait_ge(act_done, 2)
            act_lo(0, 0, 0, True)
            act_lo(0, 1, 1, True)
            with dve.Fori(1, NF // 2) as i:
                gate_up(i)
            dve.wait_ge(act_done, NF)
            for j in range(2):
                with dve.Fori(0, (NF - 2) // 2) as i:
                    for b in range(2):
                        act_lo(j * DR + 1 + i, 2 + 2 * i + b, b)
                if j == 0:
                    act_lo(DR, 0, 0)
                    dve.wait_ge(x2_loaded, 16)
                for k, t in enumerate(DOWN_TILES):
                    if k < NT - 1:
                        dve.wait_ge(summed, (NT - 1) * j + k + 1)
                    else:
                        dve.wait_ge(products, PRODUCTS[N_DN] + DR * (j + 1))
                    if j:
                        dve.wait_ge(y_stored, 16 * NT)
                    nc.vector.tensor_tensor(y[:, t, :], ps[:, t, :], x2b[:, t, j * HALF:(j + 1) * HALF],
                                            ALU.add).then_inc(y_done, 1)
                if j == 0:
                    act_lo(DR, 1, 1)


_INS = ["x", "norm_mix", "w_in", "q_norm", "k_norm", "w_pool_group", "pool_scale", "w_branch_attn",
        "w_branch_pool", "w_out", "norm_ffn", "w_ffn_gate", "w_ffn_up", "w_ffn_down"]
_OUTS = [((1, 1024, 1024), "float32")]


def kernel(**inputs):
    import numpy as _np
    import concourse.bacc as _bacc
    from concourse import mybir as _mybir
    from concourse.bass_utils import run_bass_kernel_spmd as _run

    nc = _bacc.Bacc("TRN2", target_bir_lowering=False, num_devices=1)
    arrays, args = {}, []
    for name in _INS:
        a = _np.ascontiguousarray(inputs[name])
        arrays[f"in_{name}_dram"] = a
        args.append(nc.dram_tensor(f"in_{name}_dram", a.shape, _mybir.dt.from_np(a.dtype), kind="ExternalInput").ap())
    for i, (shape, dtype) in enumerate(_OUTS):
        dt = _mybir.dt.from_np(_np.dtype(dtype))
        args.append(nc.dram_tensor(f"out_{i}_dram", shape, dt, kind="ExternalOutput").ap())
    hybrid_block(nc, *args)
    r = _run(nc, [arrays], core_ids=[0])
    got = tuple(r.results[0][f"out_{i}_dram"] for i in range(len(_OUTS)))
    return got[0]
```
